# Optimizing a Trainium2 kernel written in Bass

```python
import jax, jax.numpy as jnp
from jax import lax
import numpy as np

D_MODEL = 1024
BATCH = 1
SEQ = 128
DEPTH = 2
DEC_BATCH = 1
DEC_SEQ = 128
PAST_LEN = 128

GRID_W = 64
N_MIXERS = 2
N_HGRN_LAYERS = (DEPTH + N_MIXERS - 1) // N_MIXERS
N_NA_LAYERS = DEPTH // N_MIXERS
HG_HEADS = 8
HG_DK = 128
HG_DV = D_MODEL // HG_HEADS
HG_KDIM = HG_HEADS * HG_DK
HG_VDIM = HG_HEADS * HG_DV
CHUNK = 64
NA_HEADS = 16
NA_HD = D_MODEL // NA_HEADS
WIN_R = 8
WIN_C = 16
N_COL_BLOCKS = GRID_W // WIN_C
KEY_COLS = 2 * WIN_C
N_EXPERTS = 64
TOP_K = 6
N_GROUPS = 8
TOPK_GROUPS = 4
D_EXPERT = 256
D_SHARED = 256
ROUTED_SCALE = 2.5
EPS = 1e-6

kernel_name = "hybrid_hgrn2_natten_moe_diffusion_step"

def _rmsnorm(x, w):
    x32 = x.astype(jnp.float32)
    y = x32 * lax.rsqrt(jnp.mean(x32 * x32, axis=-1, keepdims=True) + EPS)
    return (y * w.astype(jnp.float32)).astype(x.dtype)

def _modulation(cvec, ada_w, ada_b):
    m = jax.nn.silu(cvec) @ ada_w + ada_b
    return jnp.split(m[:, None, :], 6, axis=-1)

def _gla_scan(q, k, v, g, s0):
    B, T, H, K = q.shape
    V = v.shape[-1]
    n = T // CHUNK

    def to_chunks(a):
        return a.reshape(B, n, CHUNK, H, a.shape[-1]).transpose(1, 0, 3, 2, 4)

    tril = jnp.tril(jnp.ones((CHUNK, CHUNK), dtype=bool))[None, None, :, :, None]

    def step(S, inp):
        qc, kc, vc, gc = inp
        b = jnp.cumsum(gc, axis=2)
        o_inter = jnp.einsum('bhck,bhkv->bhcv', qc * jnp.exp(b), S)
        diff = b[:, :, :, None, :] - b[:, :, None, :, :]
        dec = jnp.exp(jnp.where(tril, diff, -jnp.inf))
        A = jnp.einsum('bhtk,bhsk,bhtsk->bhts', qc, kc, dec)
        o = o_inter + jnp.einsum('bhts,bhsv->bhtv', A, vc)
        b_last = b[:, :, -1:, :]
        S = jnp.exp(b_last[:, :, 0, :])[..., None] * S + jnp.einsum('bhsk,bhsv->bhkv', kc * jnp.exp(b_last - b), vc)
        return S, o

    S, o = lax.scan(step, s0, (to_chunks(q), to_chunks(k), to_chunks(v), to_chunks(g)))
    return o.transpose(1, 0, 3, 2, 4).reshape(B, T, H, V), S

def _hgrn_mixer(h, w_in, w_out, gn_w, lb, s0_f, s0_b):
    B, T, _ = h.shape
    proj = (h @ w_in).astype(jnp.float32)
    q, f_fw, f_bw, i_in, gate = jnp.split(
        proj, [HG_KDIM, 2 * HG_KDIM, 3 * HG_KDIM, 3 * HG_KDIM + HG_VDIM], axis=-1)
    q = q.reshape(B, T, HG_HEADS, HG_DK)
    v = i_in.reshape(B, T, HG_HEADS, HG_DV)
    lbh = lb.reshape(HG_HEADS, HG_DK).astype(jnp.float32)

    def key_and_log_decay(f_raw):
        f = lbh + (1.0 - lbh) * jax.nn.sigmoid(f_raw.reshape(B, T, HG_HEADS, HG_DK))
        return 1.0 - f, jnp.log(f)

    k_f, g_f = key_and_log_decay(f_fw)
    k_b, g_b = key_and_log_decay(f_bw)
    o_f, s_f = _gla_scan(q, k_f, v, g_f, s0_f.astype(jnp.float32))
    o_b, s_b = _gla_scan(q[:, ::-1], k_b[:, ::-1], v[:, ::-1], g_b[:, ::-1], s0_b.astype(jnp.float32))
    o = o_f + o_b[:, ::-1]
    o = o * lax.rsqrt(jnp.mean(o * o, axis=-1, keepdims=True) + EPS) * gn_w.astype(jnp.float32)
    o = o.reshape(B, T, HG_VDIM) * jax.nn.silu(gate)
    return o.astype(h.dtype) @ w_out, s_f.astype(h.dtype), s_b.astype(h.dtype)

def _na_context(h, w_qkv, w_o):
    B, S, _ = h.shape
    q, k, v = jnp.split(h @ w_qkv, 3, axis=-1)
    q = q.reshape(B, S, NA_HEADS, NA_HD) * (NA_HD ** -0.5)
    k = k.reshape(B, S, NA_HEADS, NA_HD)
    v = v.reshape(B, S, NA_HEADS, NA_HD)
    s = jnp.einsum('bqhd,bkhd->bhqk', q, k).astype(jnp.float32)
    p = jax.nn.softmax(s, axis=-1).astype(v.dtype)
    o = jnp.einsum('bhqk,bkhd->bqhd', p, v).reshape(B, S, D_MODEL)
    return o @ w_o, k, v

def _na_latent(h, w_qkv, w_o, rpb, k_ctx, v_ctx):
    B, T, _ = h.shape
    rows = T // GRID_W
    kr = min(WIN_R, rows)
    n_loc = kr * KEY_COLS
    q, k, v = jnp.split(h @ w_qkv, 3, axis=-1)
    q = q.reshape(B, rows, N_COL_BLOCKS, WIN_C, NA_HEADS, NA_HD) * (NA_HD ** -0.5)
    k = k.reshape(B, T, NA_HEADS, NA_HD)
    v = v.reshape(B, T, NA_HEADS, NA_HD)
    r = np.arange(rows)
    key_rows = np.clip(r - kr // 2, 0, rows - kr)[:, None] + np.arange(kr)
    jb = np.arange(N_COL_BLOCKS)
    key_cols = np.clip(jb * WIN_C - WIN_C // 2, 0, GRID_W - KEY_COLS)[:, None] + np.arange(KEY_COLS)
    q_cols = jb[:, None] * WIN_C + np.arange(WIN_C)
    win_start = np.clip(q_cols - WIN_C // 2, 0, GRID_W - WIN_C)
    col_ok = (key_cols[:, None, :] >= win_start[:, :, None]) & (key_cols[:, None, :] < win_start[:, :, None] + WIN_C)
    mask = np.broadcast_to(col_ok[:, :, None, :], (N_COL_BLOCKS, WIN_C, kr, KEY_COLS)).reshape(N_COL_BLOCKS, WIN_C, n_loc)
    idx = (key_rows[:, None, :, None] * GRID_W + key_cols[None, :, None, :]).reshape(rows, N_COL_BLOCKS, n_loc)
    dr = key_rows - r[:, None] + WIN_R - 1
    dc = np.clip(key_cols[:, None, :] - q_cols[:, :, None] + WIN_C - 1, 0, 2 * WIN_C - 2)
    bias = rpb[:, dr[:, None, None, :, None], dc[None, :, :, None, :]].reshape(
        NA_HEADS, rows, N_COL_BLOCKS, WIN_C, n_loc).astype(jnp.float32)
    kg = jnp.take(k, idx, axis=1)
    vg = jnp.take(v, idx, axis=1)
    s_loc = jnp.einsum('brjuhd,brjlhd->bhrjul', q, kg).astype(jnp.float32) + bias
    s_loc = jnp.where(mask, s_loc, -jnp.inf)
    s_ctx = jnp.einsum('brjuhd,bphd->bhrjup', q, k_ctx).astype(jnp.float32)
    p = jax.nn.softmax(jnp.concatenate([s_loc, s_ctx], axis=-1), axis=-1).astype(v.dtype)
    o = (jnp.einsum('bhrjul,brjlhd->brjuhd', p[..., :n_loc], vg)
         + jnp.einsum('bhrjup,bphd->brjuhd', p[..., n_loc:], v_ctx))
    return o.reshape(B, T, D_MODEL) @ w_o

def _moe(h, w_router, router_bias, w_gate, w_up, w_down, ws_gate, ws_up, ws_down):
    B, T, D = h.shape
    x = h.reshape(B * T, D)
    scores = jax.nn.sigmoid(x.astype(jnp.float32) @ w_router.astype(jnp.float32))
    sel = scores + router_bias.astype(jnp.float32)
    grp = sel.reshape(-1, N_GROUPS, N_EXPERTS // N_GROUPS)
    grp_score = lax.top_k(grp, 2)[0].sum(-1)
    _, gidx = lax.top_k(grp_score, TOPK_GROUPS)
    gmask = jax.nn.one_hot(gidx, N_GROUPS).sum(1) > 0
    emask = jnp.repeat(gmask, N_EXPERTS // N_GROUPS, axis=1)
    _, eidx = lax.top_k(jnp.where(emask, sel, -jnp.inf), TOP_K)
    wsel = jnp.take_along_axis(scores, eidx, axis=1)
    wsel = wsel / jnp.sum(wsel, axis=-1, keepdims=True) * ROUTED_SCALE
    combine = jnp.einsum('nk,nke->ne', wsel, jax.nn.one_hot(eidx, N_EXPERTS, dtype=jnp.float32)).astype(h.dtype)
    hid = jax.nn.silu(jnp.einsum('nd,edf->nef', x, w_gate)) * jnp.einsum('nd,edf->nef', x, w_up)
    routed = jnp.einsum('nef,efd->nd', hid * combine[:, :, None], w_down)
    shared = (jax.nn.silu(x @ ws_gate) * (x @ ws_up)) @ ws_down
    return (routed + shared).reshape(B, T, D)

def setup_inputs(seed: int = 0) -> dict:
    key = jax.random.key(seed)
    ks = iter(jax.random.split(key, 40))

    def nrm(shape, scale):
        return jax.random.normal(next(ks), shape, jnp.float32) * scale

    def gain(shape):
        return 1.0 + nrm(shape, 0.02)

    return {
        "x_prompt": nrm((BATCH, SEQ, D_MODEL), 1.0),
        "x_sample": nrm((DEC_BATCH, DEC_SEQ, D_MODEL), 1.0),
        "state_hgrn_fwd": nrm((DEC_BATCH, N_HGRN_LAYERS, HG_HEADS, HG_DK, HG_DV), 0.5),
        "state_hgrn_bwd": nrm((DEC_BATCH, N_HGRN_LAYERS, HG_HEADS, HG_DK, HG_DV), 0.5),
        "cache_na_k": nrm((DEC_BATCH, N_NA_LAYERS, PAST_LEN, NA_HEADS, NA_HD), 1.0),
        "cache_na_v": nrm((DEC_BATCH, N_NA_LAYERS, PAST_LEN, NA_HEADS, NA_HD), 1.0),
        "c": nrm((DEC_BATCH, D_MODEL), 1.0),
        "c_ctx": nrm((D_MODEL,), 1.0),
        "norm1_w": gain((DEPTH, D_MODEL)),
        "norm2_w": gain((DEPTH, D_MODEL)),
        "ada_w": nrm((DEPTH, D_MODEL, 6 * D_MODEL), 0.5 * D_MODEL ** -0.5),
        "ada_b": nrm((DEPTH, 6 * D_MODEL), 0.02),
        "hgrn_w_in": nrm((N_HGRN_LAYERS, D_MODEL, 3 * HG_KDIM + 2 * HG_VDIM), D_MODEL ** -0.5),
        "hgrn_lb_logits": nrm((DEPTH + 1, HG_KDIM), 0.1),
        "hgrn_gn_w": gain((N_HGRN_LAYERS, HG_DV)),
        "hgrn_w_out": nrm((N_HGRN_LAYERS, HG_VDIM, D_MODEL), HG_VDIM ** -0.5),
        "na_w_qkv": nrm((N_NA_LAYERS, D_MODEL, 3 * D_MODEL), D_MODEL ** -0.5),
        "na_rpb": nrm((N_NA_LAYERS, NA_HEADS, 2 * WIN_R - 1, 2 * WIN_C - 1), 0.1),
        "na_w_o": nrm((N_NA_LAYERS, D_MODEL, D_MODEL), D_MODEL ** -0.5),
        "moe_w_router": nrm((DEPTH, D_MODEL, N_EXPERTS), D_MODEL ** -0.5),
        "moe_router_bias": nrm((DEPTH, N_EXPERTS), 0.01),
        "moe_w_gate": nrm((DEPTH, N_EXPERTS, D_MODEL, D_EXPERT), D_MODEL ** -0.5),
        "moe_w_up": nrm((DEPTH, N_EXPERTS, D_MODEL, D_EXPERT), D_MODEL ** -0.5),
        "moe_w_down": nrm((DEPTH, N_EXPERTS, D_EXPERT, D_MODEL), D_EXPERT ** -0.5),
        "shared_w_gate": nrm((DEPTH, D_MODEL, D_SHARED), D_MODEL ** -0.5),
        "shared_w_up": nrm((DEPTH, D_MODEL, D_SHARED), D_MODEL ** -0.5),
        "shared_w_down": nrm((DEPTH, D_SHARED, D_MODEL), D_SHARED ** -0.5),
        "final_norm_w": gain((D_MODEL,)),
    }

def reference(x_prompt, x_sample, state_hgrn_fwd, state_hgrn_bwd, cache_na_k, cache_na_v, c, c_ctx,
              norm1_w, norm2_w, ada_w, ada_b, hgrn_w_in, hgrn_lb_logits, hgrn_gn_w, hgrn_w_out,
              na_w_qkv, na_rpb, na_w_o, moe_w_router, moe_router_bias, moe_w_gate, moe_w_up, moe_w_down,
              shared_w_gate, shared_w_up, shared_w_down, final_norm_w):
    xp, xs = x_prompt, x_sample
    lb_table = jnp.cumsum(jax.nn.softmax(hgrn_lb_logits.astype(jnp.float32), axis=0), axis=0)
    sf_list, sb_list, k_list, v_list = [], [], [], []
    for l in range(DEPTH):
        sh1p, sc1p, g1p, sh2p, sc2p, g2p = _modulation(c_ctx[None, :], ada_w[l], ada_b[l])
        sh1s, sc1s, g1s, sh2s, sc2s, g2s = _modulation(c, ada_w[l], ada_b[l])
        hp = _rmsnorm(xp, norm1_w[l]) * (1 + sc1p) + sh1p
        hs = _rmsnorm(xs, norm1_w[l]) * (1 + sc1s) + sh1s
        if l % N_MIXERS == 0:
            a = l // N_MIXERS
            zero = jnp.zeros((xp.shape[0], HG_HEADS, HG_DK, HG_DV), jnp.float32)
            op, s_f, s_b = _hgrn_mixer(hp, hgrn_w_in[a], hgrn_w_out[a], hgrn_gn_w[a], lb_table[l], zero, zero)
            os_, _, _ = _hgrn_mixer(hs, hgrn_w_in[a], hgrn_w_out[a], hgrn_gn_w[a], lb_table[l],
                                    state_hgrn_fwd[:, a], state_hgrn_bwd[:, a])
            sf_list.append(s_f)
            sb_list.append(s_b)
        else:
            n = l // N_MIXERS
            op, k_c, v_c = _na_context(hp, na_w_qkv[n], na_w_o[n])
            os_ = _na_latent(hs, na_w_qkv[n], na_w_o[n], na_rpb[n], cache_na_k[:, n], cache_na_v[:, n])
            k_list.append(k_c)
            v_list.append(v_c)
        xp = xp + g1p * op
        xs = xs + g1s * os_
        hp = _rmsnorm(xp, norm2_w[l]) * (1 + sc2p) + sh2p
        hs = _rmsnorm(xs, norm2_w[l]) * (1 + sc2s) + sh2s
        moe_args = (moe_w_router[l], moe_router_bias[l], moe_w_gate[l], moe_w_up[l], moe_w_down[l],
                    shared_w_gate[l], shared_w_up[l], shared_w_down[l])
        xp = xp + g2p * _moe(hp, *moe_args)
        xs = xs + g2s * _moe(hs, *moe_args)
    y_prompt = _rmsnorm(xp, final_norm_w)
    y_sample = _rmsnorm(xs, final_norm_w)
    new_state_hgrn_fwd = jnp.stack(sf_list, axis=1)
    new_state_hgrn_bwd = jnp.stack(sb_list, axis=1)
    new_cache_na_k = jnp.stack(k_list, axis=1)
    new_cache_na_v = jnp.stack(v_list, axis=1)
    return (y_prompt, y_sample, new_state_hgrn_fwd, new_state_hgrn_bwd, new_cache_na_k, new_cache_na_v)


_drawn_inputs = setup_inputs


def setup_inputs(seed=0):
    import zlib

    import numpy as np

    out = dict(_drawn_inputs(seed))
    spreads = {}
    factors = {'na_rpb': 6.128, 'final_norm_w': 3.103}
    for name, (base, spread) in spreads.items():
        noise = np.random.default_rng([zlib.crc32(name.encode()), seed]).standard_normal(out[name].shape)
        drawn = base * np.exp(spread * noise) if base else spread * noise
        out[name] = __import__('jax').numpy.asarray(drawn.astype(out[name].dtype))
    for name, factor in factors.items():
        out[name] = (out[name] * factor).astype(out[name].dtype)
    return out
```

```python
from contextlib import ExitStack

import numpy as np

import concourse.bass as bass
from concourse import mybir
from concourse.alu_op_type import AluOpType as ALU

ACT = mybir.ActivationFunctionType
AX = mybir.AxisListType
F32 = mybir.dt.float32
I32 = mybir.dt.int32

P = 128
D = 1024
K = D // P
T = 128
NT = 2 * T
EPS = 1e-6
HEADS, DK, DV = 8, 128, 128
GROUP = 4
A_HEADS, HD = 16, 64
GRID_W, WIN_R, WIN_C = 64, 8, 16
E, TOP_K, GROUPS, TOP_GROUPS = 64, 6, 8, 4
F = 256
SLOTS = 64
PAIRS = E // 2
ROUTED_SCALE = 2.5
LOW = -1e30
BLOCK = 512
BLOCK_W = K * BLOCK

C_ID, C_MASKF, C_MASKB, C_BEFORE, C_IOTA, C_SEL, C_WIN, C_WNEG, C_FLIP, C_END = np.cumsum(
    [0, 128, 128, 32, 128, 4 * SLOTS, 2, 128, 128, 128]).tolist()


def shape_constants():
    c = np.zeros((P, C_END), np.float32)
    i, j = np.arange(P)[:, None], np.arange(P)[None, :]
    c[:, C_ID:C_ID + P] = i == j
    c[:, C_MASKF:C_MASKF + P] = (i // 32 != j // 32) | (i <= j)
    c[:, C_MASKB:C_MASKB + 32] = i % 32 >= np.arange(32)[None, :]
    c[:, C_BEFORE:C_BEFORE + P] = i < j
    c[:, C_IOTA:C_IOTA + 4 * SLOTS] = np.arange(4 * SLOTS)[None, :]
    for g in range(4):
        for s in range(2):
            c[32 * g + s, C_SEL + s] = 1.0
    start = np.clip(np.arange(GRID_W) - WIN_C // 2, 0, GRID_W - WIN_C)
    col = np.arange(P) % GRID_W
    inside = (col[None, :] >= start[col][:, None]) & (col[None, :] < start[col][:, None] + WIN_C)
    c[:, C_WIN:C_WIN + P] = inside
    c[:, C_WNEG:C_WNEG + P] = np.where(inside, 0.0, LOW)
    c[:, C_FLIP:C_FLIP + P] = (i // GRID_W == j // GRID_W) & (i % GRID_W + j % GRID_W == GRID_W - 1)
    return c


def build(nc, io):
    ctx = ExitStack()
    with ctx:
        def sem(name):
            return ctx.enter_context(nc.semaphore(name))

        WORDS = 53100
        arena = ctx.enter_context(nc.sbuf_tensor("arena", [P, WORDS], F32))
        top = [0]

        def cut(n, shape=None, at=None):
            a = top[0] if at is None else at
            if at is None:
                top[0] += n
                assert top[0] <= WORDS, top[0]
            v = arena[:, a:a + n]
            if shape:
                names = "abcd"[:len(shape)]
                v = v.rearrange(f"p ({' '.join(names)}) -> p {' '.join(names)}", **dict(zip(names, shape)))
            return v

        xT = cut(K * NT, (K, NT))
        hT = cut(K * NT, (K, NT))
        consts = cut(C_END)
        ones = cut(P)
        mod = cut(2 * 48 * 2, (2, 6, K, 2))
        gain = cut(4 * K * 2, (4, K, 2))
        norm_w = cut(5 * K, (5, K))
        ada_b = cut(2 * 48, (2, 6, K))
        lb = cut(3 * HEADS, (3, HEADS))
        lb0 = cut(HEADS)
        lb_t = cut(HEADS)
        one_minus_lb = cut(HEADS)
        gn_w = cut(1)
        eps = cut(1)
        cond = cut(2 * K, (2, K))
        cond_act = cut(K * 32, (K, 32))
        router_w = cut(2 * K * E, (2, K, E))
        router_b = cut(2 * E, (2, E))
        rank = cut(2 * (E + 2), (2, E + 2))
        comb = cut(2 * (E + 2), (2, E + 2))
        extra = cut(1)
        rstd = cut(NT)
        PAIR_W = 6 * K * F
        ring_at = top[0]
        ring = cut(2 * PAIR_W, (2, 6, K * F))
        late_at = top[0]
        late = cut(HEADS * D, (HEADS, D))
        ws_gu = cut(K * 2 * F, (K, 2 * F), at=late_at)
        ws_dn = cut(2 * D, (2, D), at=late_at + K * 2 * F)
        scratch_at = top[0]
        SCRATCH_W = WORDS - scratch_at

        class Scratch:
            def __init__(self, at, size):
                self.at, self.end = at, at + size

            def __call__(self, n, shape=None):
                self.at += n
                assert self.at <= self.end, (self.at, self.end)
                return cut(n, shape, at=self.at - n)

        stage = [cut(BLOCK_W, (K, BLOCK), at=ring_at + n * BLOCK_W) for n in range(3)]

        sc = Scratch(scratch_at, SCRATCH_W)
        h_tok = sc(2 * D, (2, K, P))
        xg = sc(2 * K * P, (2, K, P))
        onehot = sc(2 * 2 * P, (2, 2, P))
        onehot_w = sc(2 * 2 * P, (2, 2, P))
        hidT_c = sc(2 * 4 * P, (2, 4, P))
        hid = sc(2 * 2 * P, (2, 2 * P))
        silu = sc(2 * F, (2, F))
        y = sc(2 * D, (2, K, P))
        route = sc(12 * 2 * E, (12, 2, E))
        sq = cut(K * NT, (K, NT), at=scratch_at)
        sh_silu = y[:, 0, 0:4, :].rearrange("p (a b) c -> p a (b c)", a=2)
        sh_hid = y[:, 0, 4:8, :].rearrange("p (a b) c -> p a (b c)", a=2)
        sh_hidT = y[:, 1, 0:4, :].rearrange("p (a b) c -> p a (b c)", a=2)

        sc = Scratch(ring_at + PAIR_W, PAIR_W)
        q = sc(HEADS * NT, (HEADS, NT))
        kk = [sc(HEADS * NT, (HEADS, NT)) for _ in range(2)]
        bb = [sc(HEADS * NT, (HEADS, NT)) for _ in range(2)]
        gate = sc(HEADS * NT, (HEADS, NT))
        oT = q
        sc = Scratch(scratch_at, SCRATCH_W)
        v = sc(2 * D, (2, D))
        s0 = sc(2 * D, (2, HEADS, DV))
        UNITS = GROUP * 2
        Q = [sc(UNITS * T, (UNITS, T)) for _ in range(2)]
        Kd = [sc(UNITS * T, (UNITS, T)) for _ in range(2)]
        dif = [sc(UNITS * T, (UNITS, T)) for _ in range(2)]
        AT = dif[1]
        fb_sb = sc(UNITS * 32, (UNITS, 32))
        scan_keep = sc(UNITS * T)
        mrow = sc(D, (D,))
        x_tok = cut(2 * D, (2, D), at=scratch_at)
        lbrow = cut(3 * P, (3, P), at=scratch_at + 2 * D)

        sc = Scratch(ring_at + PAIR_W, PAIR_W)
        qT = sc(K * NT, (K, NT))
        kT = sc(K * NT, (K, NT))
        va = sc(2 * D, (2, D))
        ckT = sc(K * T, (K, T))
        cv = sc(D, (D,))
        ck = sc(D, (D,))
        bias = sc(A_HEADS * P, (A_HEADS, P))
        sc = Scratch(scratch_at, SCRATCH_W)
        sc(K * NT)
        S_lat = sc(4 * 2 * P, (4, 2 * P))
        S_pr = sc(4 * P, (4, P))
        PT = sc(12 * P, (12, P))
        oTa = sc(K * NT, (K, NT))
        kout = sc(D, (K, P))
        neg_max = sc(8)
        row_sum = sc(8)
        y_tok = cut(2 * D, (2, P, K), at=scratch_at + K * NT)

        ident = consts[:, C_ID:C_ID + P]
        mask_f = consts[:, C_MASKF:C_MASKF + P]
        mask_b = consts[:, C_MASKB:C_MASKB + 32]
        before = consts[:, C_BEFORE:C_BEFORE + P]
        sel = consts[:, C_SEL:C_SEL + 2]
        window = consts[:, C_WIN:C_WIN + P]
        window_neg = consts[:, C_WNEG:C_WNEG + P]
        flip = consts[:, C_FLIP:C_FLIP + P]

        psum = ctx.enter_context(nc.psum_tensor("psum", [P, 8, 512], F32))

        s_const, s_x, s_small, s_s0 = sem("consts_in"), sem("x_in"), sem("small_in"), sem("states_in")
        stage_in = [sem(f"stage_in{n}") for n in range(3)]
        stage_used = sem("stage_used")
        late_in, late_used = sem("late_in"), sem("late_used")
        cache_in, bias_in = sem("cache_in"), sem("bias_in")
        ready = sem("start_values_ready")
        x_ps, x_sb = sem("xT_in_psum"), sem("xT_in_sbuf")
        lb_ps, lb_shift, lb_exp = sem("lb_in_psum"), sem("lb_shifted"), sem("lb_exp")
        cond_done = sem("cond_act_done")
        ada_ps, ada_row, sel_ps, mod_done = sem("ada_in_psum"), sem("ada_rows"), sem("ada_cols_in_psum"), sem("mod_done")
        sq_done, ssum, root, h_done = sem("squares"), sem("square_sums"), sem("root"), sem("h_done")
        proj, gate_sig, v_sb = sem("proj_in_psum"), sem("gate_sigmoid"), sem("v_rows")
        unit_free = [sem("proj_unit0_read"), sem("proj_unit1_read")]
        f_done, ln_done = sem("decay_done"), sem("log_decay_done")
        dif_done, exp_done, qk_done, qk_used = sem("dif_done"), sem("exp_done"), sem("qk_done"), sem("qk_used")
        at_done, pv_done, o_copied, o_sq, o_ssum, o_rstd, o_done = (
            sem(n) for n in ("scores_masked", "pv_done", "o_copied", "o_squares", "o_square_sums", "o_rstd", "o_done"))
        kd_ps, kd_sb, st_ps, st_sb, st_out = (
            sem(n) for n in ("kdecT_in_psum", "kdecT", "state_in_psum", "state", "state_stored"))
        out_ps, resid = sem("mixer_out_in_psum"), sem("residual_added")
        dve_c, act_c = sem("dve_chain"), sem("act_chain")
        tr_ps, tr_sb = sem("key_rows_in_psum"), sem("key_rows")
        bias_ps, bias_done = sem("bias_in_psum"), sem("bias_windowed")
        sc_ps, sc_sb, p_exp, p_norm, pt_ps, pt_sb, oa_ps, oa_sb = (
            sem(n) for n in ("scores_in_psum", "scores_read", "probs", "probs_normed", "probsT_in_psum", "probsT",
                             "attn_in_psum", "attn_done"))
        cache_out = sem("cache_stored")
        yt_ps, yt_sb, y_out = sem("yT_in_psum"), sem("y_rows"), sem("y_stored")

        class Moe:

            def __init__(self, l):
                def s(name):
                    return sem(f"{name}_{l}")

                self.logits, self.scores = s("logits"), s("scores")
                self.htok_ps, self.htok = s("htok_ps"), s("htok")
                self.mask, self.rank_ps, self.table = s("mask"), s("rank_ps"), s("table")
                self.sh_in, self.sh_ps, self.sh_silu, self.sh_hid = s("sh_in"), s("sh_ps"), s("sh_silu"), s("sh_hid")
                self.sh_used = s("sh_used")
                self.gu_in = [s("gu_in0"), s("gu_in1")]
                self.dn_in = [s("dn_in0"), s("dn_in1")]
                self.gu, self.dn_used = s("gu"), s("dn_used")
                self.onehot = s("onehot")
                self.xg_ps = [s("xg_ps0"), s("xg_ps1")]
                self.xg = [s("xg_act"), s("xg_dve")]
                self.silu, self.hid, self.t_ps, self.t_sb = s("silu"), s("hid"), s("t_ps"), s("t_sb")
                self.y_ps = [s("y_ps0"), s("y_ps1")]
                self.y = [s("y_act"), s("y_dve")]
                self.comb, self.c_zero, self.done = s("comb"), s("c_zero"), s("moe_done")

        moe = [Moe(0), Moe(1)]

        block = ctx.enter_context(nc.Block())

        KINDS = ["f_fw", "f_bw", "gate", "q", "v"]
        COL = {"q": 0, "f_fw": D, "f_bw": 2 * D, "v": 3 * D, "gate": 4 * D}
        parts = [(l, j) for l in range(2) for j in range(6)]
        stages = [("ada", l, j, half) for l, j in parts[:2] for half in range(2)]
        for b in range(10):
            l, j = parts[2 + b]
            stages += [("ada", l, j, 0), ("in", b // 5, KINDS[b % 5]), ("ada", l, j, 1)]
        stages0 = len(stages)
        stages += [("qkv", n) for n in range(6)]

        def stage_source(what):
            if what[0] == "ada":
                _, l, j, half = what
                src = io["ada_w"][l, :, j * D + half * BLOCK:j * D + (half + 1) * BLOCK]
            elif what[0] == "in":
                c = COL[what[2]] + what[1] * BLOCK
                src = io["hgrn_w_in"][0, :, c:c + BLOCK]
            else:
                src = io["na_w_qkv"][0, :, what[1] * BLOCK:(what[1] + 1) * BLOCK]
            return src.rearrange("(p k) n -> p k n", p=P)

        SMALL = 12 * 16

        def bank(n, count=1):
            return psum[:, n:n + count, :].rearrange("p b n -> p (b n)")

        def heads(a, g):
            return a[:, GROUP * g:GROUP * (g + 1)].rearrange("p h (s t) -> p (h s) t", s=2)

        @block.sync
        def _(sp):
            sp.dma_start(x_tok[:, 0, :], io["x_prompt"][0]).then_inc(s_x, 16)
            sp.dma_start(x_tok[:, 1, :], io["x_sample"][0]).then_inc(s_x, 16)
            sp.dma_start(consts, io["table"]).then_inc(s_const, 16)

            def load_stage(n):
                if n >= 3:
                    sp.wait_ge(stage_used, n - 2)
                sp.dma_start(stage[n % 3], stage_source(stages[n])).then_inc(stage_in[n % 3], 16)

            def load_gate_up(m, j, expert):
                for e in range(2):
                    for w, name in enumerate(("moe_w_gate", "moe_w_up")):
                        src = io[name][m][bass.ds(expert + e, 1)].rearrange("e (p k) f -> p (e k f)", p=P)
                        sp.dma_start(ring[:, j, 2 * e + w, :], src).then_inc(moe[m].gu_in[j], 16)

            def load_down(m, j, expert):
                for e in range(2):
                    src = io["moe_w_down"][m][bass.ds(expert + e, 1)].rearrange("e (c p) d -> p (e c) d", p=P)
                    dst = ring[:, j, 4 + e, :].rearrange("p (c d) -> p c d", c=2)
                    sp.dma_start(dst, src).then_inc(moe[m].dn_in[j], 16)

            def load_shared(m):
                for w, name in enumerate(("shared_w_gate", "shared_w_up")):
                    sp.dma_start(ws_gu[:, :, w * F:(w + 1) * F],
                                 io[name][m].rearrange("(p k) f -> p k f", p=P)).then_inc(moe[m].sh_in, 16)
                sp.dma_start(ws_dn, io["shared_w_down"][m].rearrange("(c p) d -> p c d", p=P))\
                  .then_inc(moe[m].sh_in, 16)

            def stream_experts(m):
                with sp.Fori(1, PAIRS // 2) as h:
                    for j in range(2):
                        sp.wait_ge(moe[m].gu, h * 2 + (j - 1))
                        load_gate_up(m, j, h * 4 + 2 * j)
                        sp.wait_ge(moe[m].dn_used, h * 2 + (j - 1))
                        load_down(m, j, h * 4 + 2 * j)
                sp.wait_ge(moe[m].table, 1)
                more = sp.value_load(extra[0:1, 0:1].bitcast(I32), min_val=0, max_val=3)
                with sp.If(more > 0):
                    with sp.Fori(0, more) as r:
                        with sp.Fori(0, PAIRS // 2) as h:
                            for j in range(2):
                                sp.wait_ge(moe[m].gu, r * PAIRS + h * 2 + (PAIRS + j - 1))
                                load_gate_up(m, j, h * 4 + 2 * j)
                                sp.wait_ge(moe[m].dn_used, r * PAIRS + h * 2 + (PAIRS + j - 1))
                                load_down(m, j, h * 4 + 2 * j)

            for n in range(4):
                load_stage(n)
            sp.wait_ge(lb_ps, 1)
            for d, name in enumerate(("state_hgrn_fwd", "state_hgrn_bwd")):
                sp.dma_start(s0[:, d], io[name][0, 0].rearrange("h k v -> k h v")).then_inc(s_s0, 16)
            for n in range(4, stages0):
                load_stage(n)
            sp.dma_start(late, io["hgrn_w_out"][0].rearrange("(h p) d -> p h d", p=P)).then_inc(late_in, 16)
            sp.wait_ge(stage_used, stages0)
            load_gate_up(0, 0, 0)
            load_down(0, 0, 0)
            sp.wait_ge(late_used, 1)
            load_shared(0)
            load_gate_up(0, 1, 2)
            load_down(0, 1, 2)
            stream_experts(0)

            sp.wait_ge(moe[0].done, 1)
            for n in range(stages0, stages0 + 3):
                sp.dma_start(stage[n % 3], stage_source(stages[n])).then_inc(stage_in[n % 3], 16)
            sp.dma_start(ck, io["cache_na_k"][0, 0].rearrange("s h d -> s (h d)")).then_inc(cache_in, 16)
            sp.dma_start(cv, io["cache_na_v"][0, 0].rearrange("s h d -> s (h d)")).then_inc(cache_in, 16)
            rpb = io["na_rpb"]
            for r in range(2):
                for r2 in range(2):
                    at = rpb.offset + (r2 - r + WIN_R - 1) * (2 * WIN_C - 1) + WIN_C - 1 - (GRID_W - 1)
                    src = bass.AP(tensor=rpb.tensor, offset=at,
                                  ap=[[1, GRID_W], [(2 * WIN_R - 1) * (2 * WIN_C - 1), A_HEADS], [1, GRID_W]])
                    sp.dma_start(bias[GRID_W * r:GRID_W * (r + 1), :, GRID_W * r2:GRID_W * (r2 + 1)], src)\
                      .then_inc(bias_in, 16)
            for n in range(stages0 + 3, stages0 + 6):
                load_stage(n)
            sp.dma_start(late, io["na_w_o"][0].rearrange("(c p) d -> p c d", p=P)).then_inc(late_in, 16)
            sp.wait_ge(stage_used, stages0 + 6)
            load_gate_up(1, 0, 0)
            load_down(1, 0, 0)
            sp.wait_ge(late_used, 2)
            sp.wait_ge(cache_out, 32)
            load_shared(1)
            load_gate_up(1, 1, 2)
            load_down(1, 1, 2)
            stream_experts(1)
            sp.wait_ge(st_out, 16 * 4)
            sp.wait_ge(cache_out, 32)
            sp.wait_ge(y_out, 32)

        @block.gpsimd
        def _(pool):
            pool.memset(ones, 1.0).then_inc(ready, 1)
            pool.memset(eps, EPS).then_inc(ready, 1)
            pool.memset(cond_act, 0.0).then_inc(ready, 1)
            pool.memset(scan_keep, 1.0).then_inc(ready, 1)
            pool.wait_ge(ready, 4)
            pool.memset(scan_keep.rearrange("p (u t) -> p u t", t=T)[:, :, 0:1], 0.0).then_inc(ready, 1)
            small = [
                (cond[:, 0, :], io["c_ctx"].rearrange("(p k) -> p k", p=P)),
                (cond[:, 1, :], io["c"][0].rearrange("(p k) -> p k", p=P)),
                (norm_w[:, 0:4:2, :], io["norm1_w"].rearrange("l (p k) -> p l k", p=P)),
                (norm_w[:, 1:4:2, :], io["norm2_w"].rearrange("l (p k) -> p l k", p=P)),
                (norm_w[:, 4, :], io["final_norm_w"].rearrange("(p k) -> p k", p=P)),
                (ada_b.rearrange("p l j k -> p (l j) k"), io["ada_b"].rearrange("l (j p k) -> p (l j) k", p=P, j=6)),
                (lbrow[0:HEADS], io["hgrn_lb_logits"].rearrange("i (h d) -> h i d", h=HEADS)),
                (gn_w, io["hgrn_gn_w"].rearrange("a d -> d a")),
                (router_w[:, 0], io["moe_w_router"][0].rearrange("(p k) e -> p k e", p=P)),
                (router_w[:, 1], io["moe_w_router"][1].rearrange("(p k) e -> p k e", p=P)),
                (router_b[:, 0], io["moe_router_bias"][0:1].broadcast_to((P, E))),
                (router_b[:, 1], io["moe_router_bias"][1:2].broadcast_to((P, E))),
            ]
            assert len(small) * 16 == SMALL
            for dst, src in small:
                pool.dma_start(dst, src).then_inc(s_small, 16)

        @block.scalar
        def _(act):
            def copy(out, in_, **kw):
                return act.activation(out, in_, ACT.Copy, **kw)

            def squares():
                act.activation(sq[:, 0:4], xT[:, 0:4], ACT.Square).then_inc(sq_done, 1)

            def norm_root(n):
                act.wait_ge(ssum, n + 1)
                act.activation(rstd, psum[:, 4, 0:NT], ACT.Sqrt, scale=1.0 / D, bias=eps).then_inc(root, 1)

            def ada_rows(n):
                act.wait_ge(ada_ps, n + 1)
                if n % 2 == 0 and n >= 2:
                    act.wait_ge(sel_ps, n // 2)
                copy(mrow[:, (n % 2) * BLOCK:(n % 2 + 1) * BLOCK], psum[:, 7, :]).then_inc(ada_row, 1)

            act.wait_ge(s_small, SMALL)
            act.wait_ge(ready, 5)
            act.activation(cond_act[:, :, 0:2], cond.rearrange("p s k -> p k s"), ACT.Silu).then_inc(cond_done, 1)
            for n in (0, 2):
                act.wait_ge(x_ps, n + 1)
                copy(xT[:, 2 * n:2 * n + 4, 0:T], psum[:, n, :].rearrange("p (k t) -> p k t", t=T)).then_inc(x_sb, 1)
            act.wait_ge(x_sb, 4)
            squares()
            act.wait_ge(lb_shift, 1)
            act.activation(lb, lb, ACT.Exp).then_inc(lb_exp, 1)
            for n in range(4):
                ada_rows(n)
            norm_root(0)

            def project(b):
                g, kind = b // 5, KINDS[b % 5]
                dst = {"f_fw": kk[0], "f_bw": kk[1], "gate": gate, "q": q, "v": None}[kind]
                if dst is None:
                    return
                act.wait_ge(proj, b + 1)
                dst = dst[:, GROUP * g:GROUP * (g + 1)].rearrange("p h t -> p (h t)")
                ins = act.activation(dst, bank(2 * (b % 2), 2), ACT.Copy if kind == "q" else ACT.Sigmoid)
                ins.then_inc(gate_sig if kind == "gate" else unit_free[b % 2], 1)

            def decay_exps(g, n):
                for d in range(2):
                    c = 8 * g + 2 * n + d
                    act.wait_ge(dif_done, c + 1)
                    if c >= 2:
                        act.wait_ge(qk_used, c - 1)
                    if n < 2:
                        H = 64 >> n
                        vq, vk, vd = (a.rearrange("p u (b t) -> p (u b) t", t=2 * H) for a in (Q[d], Kd[d], dif[d]))
                        early, behind = slice(0, H), slice(H, 2 * H)
                        qs, ks = (behind, early) if d == 0 else (early, behind)
                        act.activation(vq[:, :, qs], vd[:, :, qs], ACT.Exp)
                        ins = act.activation(vk[:, :, ks], vd[:, :, ks], ACT.Exp, scale=-1.0)
                    elif n == 2:
                        act.activation(Q[d], dif[d], ACT.Exp)
                        ins = act.activation(Kd[d], dif[d], ACT.Exp, scale=-1.0)
                    else:
                        act.activation(Q[d][:, 0:GROUP], bb[d][:, GROUP * g:GROUP * (g + 1), T:NT], ACT.Exp)
                        ins = act.activation(Kd[d][:, 0:GROUP], dif[d][:, 0:GROUP], ACT.Exp, scale=-1.0)
                    ins.then_inc(exp_done, 1)

            def keys_turned(g, d):
                act.wait_ge(kd_ps, 2 * g + d + 1)
                copy(Kd[d][:, GROUP:UNITS].rearrange("p u t -> p (u t)"), psum[:, 6, :]).then_inc(kd_sb, 1)

            def state_out(g, d):
                act.wait_ge(st_ps, 2 * g + d + 1)
                copy(Q[d][:, GROUP:UNITS].rearrange("p u t -> p (u t)"), psum[:, 6, :]).then_inc(st_sb, 1)
                act.wait_ge(st_sb, 2 * g + d + 1)
                dst = io["out_state_fwd" if d == 0 else "out_state_bwd"][0, 0, GROUP * g:GROUP * (g + 1)]
                act.dma_start(dst.rearrange("h k v -> k h v"), Q[d][:, GROUP:UNITS]).then_inc(st_out, 16)

            def recur(g, item):
                if item == 0:
                    for d in range(2):
                        act.wait_ge(f_done, 2 * g + d + 1)
                        if g:
                            act.wait_ge(o_done if d == 0 else pv_done, g)
                        act.activation(dif[d].rearrange("p u t -> p (u t)"),
                                       bb[d][:, GROUP * g:GROUP * (g + 1)].rearrange("p h t -> p (h t)"),
                                       ACT.Ln).then_inc(ln_done, 1)
                    if g:
                        act.wait_ge(st_out, 32 * g)
                if item <= 3:
                    decay_exps(g, item)
                elif item == 4:
                    act.wait_ge(o_copied, g + 1)
                    act.activation(dif[0], heads(oT, g), ACT.Square).then_inc(o_sq, 1)
                    keys_turned(g, 0)
                elif item == 5:
                    act.wait_ge(o_ssum, g + 1)
                    act.activation(dif[0].rearrange("p u t -> p (u t)"), bank(4, 2), ACT.Ln, scale=1.0 / DV,
                                   bias=eps).then_inc(act_c, 1)
                    act.wait_ge(act_c, g + 1)
                    act.activation(dif[0], dif[0], ACT.Exp, scale=-0.5).then_inc(o_rstd, 1)
                    state_out(g, 0)
                elif item == 6:
                    keys_turned(g, 1)
                elif item == 7:
                    state_out(g, 1)

            for b in range(10):
                ada_rows(4 + 2 * b)
                if b >= 5:
                    recur(0, b - 5)
                project(b)
                ada_rows(5 + 2 * b)
            for item in (5, 6, 7):
                recur(0, item)
            for item in range(8):
                recur(1, item)

            def experts_front(m):
                M = moe[m]
                act.wait_ge(resid, 2 * m + 1)
                squares()
                norm_root(2 * m + 1)
                act.wait_ge(M.logits, 1)
                act.activation(route[:, 0], psum[:, 5, 0:2 * E].rearrange("p (a e) -> p a e", a=2), ACT.Sigmoid)\
                   .then_inc(M.scores, 1)
                for n in range(4):
                    act.wait_ge(M.htok_ps, n + 1)
                    copy(h_tok[:, n // 2, 4 * (n % 2):4 * (n % 2) + 4],
                         psum[:, 6 + n % 2, :].rearrange("p (k t) -> p k t", t=P)).then_inc(M.htok, 1)
                for a in range(2):
                    act.wait_ge(M.sh_ps, a + 1)
                    act.activation(sh_silu[:, a], psum[:, 6 + a, 0:F], ACT.Silu).then_inc(M.sh_silu, 1)
                act.wait_ge(M.t_ps, 1)
                copy(sh_hidT.rearrange("p c t -> p (c t)"), psum[:, 4, :]).then_inc(M.t_sb, 1)
                act.sem_inc(M.y[0], 1)

            def gathered(M, g, j):
                act.wait_ge(M.xg_ps[0], g + 1)
                copy(xg[:, j, 0:4], psum[:, 6, :].rearrange("p (k t) -> p k t", t=P)).then_inc(M.xg[0], 1)

            def experts_pass(M, r):
                gathered(M, r * (PAIRS + 1), 0)
                with act.Fori(0, PAIRS // 2) as h:
                    for j in range(2):
                        n, g = r * PAIRS + h * 2 + j, r * (PAIRS + 1) + h * 2 + j
                        act.wait_ge(M.gu, n + 1)
                        act.activation(silu[:, j], psum[:, 4, 0:F], ACT.Silu).then_inc(M.silu, 1)
                        gathered(M, g + 1, 1 - j)
                        act.wait_ge(M.t_ps, n + 2)
                        copy(hidT_c[:, j].rearrange("p c t -> p (c t)"), psum[:, 5, :]).then_inc(M.t_sb, 1)
                        act.wait_ge(M.y_ps[0], n + 1)
                        copy(y[:, j, :, 0:P // 2].rearrange("s k p -> s p k"),
                             psum[:, 6, :].rearrange("s (p k) -> s p k", k=K)).then_inc(M.y[0], 1)

            def experts(m):
                experts_pass(moe[m], 0)
                act.wait_ge(moe[m].table, 1)
                more = act.value_load(extra[0:1, 0:1].bitcast(I32), min_val=0, max_val=3)
                with act.If(more > 0):
                    with act.Fori(0, more) as r:
                        experts_pass(moe[m], r + 1)

            act.wait_ge(st_out, 64)
            experts_front(0)
            experts(0)

            act.wait_ge(resid, 2)
            squares()
            norm_root(2)
            for n in (0, 1):
                act.wait_ge(proj, 10 + n + 1)
                copy(qT[:, 4 * n:4 * n + 4].rearrange("p k t -> p (k t)"), bank(2 * (n % 2), 2), scale=HD ** -0.5)\
                    .then_inc(unit_free[n % 2], 1)
            for n in range(2):
                act.wait_ge(tr_ps, n + 1)
                copy(ckT[:, 4 * n:4 * n + 4], psum[:, 4 + n, :].rearrange("p (k t) -> p k t", t=P)).then_inc(tr_sb, 1)
            for n in (4, 5):
                act.wait_ge(proj, 10 + n + 1)
                copy(va[:, :, (n - 4) * BLOCK:(n - 3) * BLOCK], psum[:, 2 * (n % 2):2 * (n % 2) + 2, :])\
                    .then_inc(unit_free[n % 2], 1)
            for n in range(2):
                act.wait_ge(tr_ps, n + 3)
                copy(kout[:, 4 * n:4 * n + 4], psum[:, 4 + n, :].rearrange("p (k t) -> p k t", t=P)).then_inc(tr_sb, 1)
            act.wait_ge(tr_sb, 4)
            act.dma_start(io["out_cache_k"][0, 0].rearrange("s h d -> s (h d)"), kout.rearrange("p k t -> p (k t)"))\
               .then_inc(cache_out, 16)
            act.wait_ge(unit_free[0], 8)
            act.wait_ge(unit_free[1], 8)
            act.dma_start(io["out_cache_v"][0, 0].rearrange("s h d -> s (h d)"), va[:, 0]).then_inc(cache_out, 16)
            for g in range(4):
                act.wait_ge(sc_sb, g + 1)
                for n in range(4):
                    act.activation(S_lat[:, n], S_lat[:, n], ACT.Exp, bias=neg_max[:, n:n + 1],
                                   accum_out=row_sum[:, n:n + 1])
                for n in range(4):
                    ins = act.activation(S_pr[:, n], psum[:, 6 + n // 2, (n % 2) * P:(n % 2 + 1) * P], ACT.Exp,
                                         bias=neg_max[:, 4 + n:5 + n], accum_out=row_sum[:, 4 + n:5 + n])
                ins.then_inc(p_exp, 1)
                act.wait_ge(pt_ps, g + 1)
                copy(PT[:, 0:8].rearrange("p n t -> p (n t)"), bank(0, 2)).then_inc(pt_sb, 1)
                act.wait_ge(oa_ps, g + 1)
                copy(oTa[:, 2 * g:2 * g + 2].rearrange("p k t -> p (k t)"), psum[:, 3, :]).then_inc(oa_sb, 1)

            act.wait_ge(cache_out, 32)
            experts_front(1)
            experts(1)

            act.wait_ge(resid, 4)
            squares()
            norm_root(4)
            for n in (0, 2):
                act.wait_ge(yt_ps, n + 1)
                copy(y_tok[:, n // 2, :, 0:4].rearrange("s p k -> s k p"),
                     psum[:, n, :].rearrange("s (k p) -> s k p", p=P)).then_inc(yt_sb, 1)
            act.wait_ge(yt_sb, 4)
            for a, name in enumerate(("out_prompt", "out_sample")):
                act.dma_start(io[name][0], y_tok[:, a].rearrange("s p k -> s (p k)")).then_inc(y_out, 16)

        @block.vector
        def _(dve):
            n_c = [0]

            def mark(ins):
                n_c[0] += 1
                ins.then_inc(dve_c, 1)

            def done():
                dve.wait_ge(dve_c, n_c[0])

            def link(ins):
                mark(ins)
                done()

            def squares(n):
                if n:
                    dve.wait_ge(resid, n)
                dve.tensor_tensor(sq[:, 4:8], xT[:, 4:8], xT[:, 4:8], ALU.mult).then_inc(sq_done, 1)

            def norm(n, shift):
                dve.wait_ge(root, n + 1)
                link(dve.reciprocal(rstd, rstd))
                link(dve.tensor_tensor(hT, xT, rstd.unsqueeze(1).broadcast_to((P, K, NT)), ALU.mult))
                for k in range(K):
                    for s in range(2):
                        part = hT[:, k, s * T:(s + 1) * T]
                        if shift is None:
                            ins = dve.tensor_scalar(part, part, norm_w[:, 4, k:k + 1], None, ALU.mult)
                        else:
                            ins = dve.tensor_scalar(part, part, gain[:, n, k, s:s + 1], shift[:, k, s:s + 1],
                                                    ALU.mult, ALU.add)
                ins.then_inc(h_done, 1)

            def modulation(n):
                l, j = parts[n]
                dve.wait_ge(sel_ps, n + 1)
                dve.tensor_tensor(mod[:, l, j], psum[:, 7, 0:2 * K].rearrange("p (k s) -> p k s", s=2),
                                  ada_b[:, l, j].unsqueeze(2).broadcast_to((P, K, 2)), ALU.add).then_inc(mod_done, 1)
                if j in (1, 4):
                    m = 2 * l + j // 4
                    dve.wait_ge(mod_done, n + 1)
                    link(dve.scalar_tensor_tensor(out=gain[:, m], in0=mod[:, l, j], scalar=1.0,
                                                  in1=norm_w[:, m].unsqueeze(2).broadcast_to((P, K, 2)),
                                                  op0=ALU.add, op1=ALU.mult))

            def residual(g, src):
                for k in range(K):
                    src(k)
                    for s in range(2):
                        at = slice(s * T, (s + 1) * T)
                        ins = dve.scalar_tensor_tensor(
                            out=xT[:, k, at], in0=psum[:, k // 2, (k % 2) * NT + s * T:(k % 2) * NT + (s + 1) * T],
                            scalar=g[:, k, s:s + 1], in1=xT[:, k, at], op0=ALU.mult, op1=ALU.add)
                ins.then_inc(resid, 1)

            dve.memset(rank, -1.0)
            dve.memset(comb, 0.0)
            for n in (1, 3):
                dve.wait_ge(x_ps, n + 1)
                dve.tensor_copy(xT[:, 2 * (n - 1):2 * (n - 1) + 4, T:NT],
                                psum[:, n, :].rearrange("p (k t) -> p k t", t=T)).then_inc(x_sb, 1)
            dve.wait_ge(x_sb, 4)
            squares(0)
            dve.wait_ge(s_small, SMALL)
            dve.wait_ge(lb_ps, 1)
            link(dve.tensor_copy(lb, psum[:, 5, 0:3 * HEADS].rearrange("p (i h) -> p i h", i=3)))
            link(dve.tensor_tensor(lb_t, lb[:, 0], lb[:, 1], ALU.max))
            link(dve.tensor_tensor(lb_t, lb_t, lb[:, 2], ALU.max))
            dve.tensor_tensor(lb, lb, lb_t.unsqueeze(1).broadcast_to((P, 3, HEADS)), ALU.subtract).then_inc(lb_shift, 1)
            dve.wait_ge(lb_exp, 1)
            link(dve.tensor_tensor(lb_t, lb[:, 0], lb[:, 1], ALU.add))
            link(dve.tensor_tensor(lb_t, lb_t, lb[:, 2], ALU.add))
            link(dve.reciprocal(lb_t, lb_t))
            link(dve.tensor_tensor(lb0, lb[:, 0], lb_t, ALU.mult))
            link(dve.tensor_scalar(one_minus_lb, lb0, -1.0, 1.0, ALU.mult, ALU.add))
            modulation(0)
            modulation(1)
            norm(0, mod[:, 0, 0])

            def project(b):
                g, kind = b // 5, KINDS[b % 5]
                if kind == "gate":
                    dve.wait_ge(gate_sig, g + 1)
                    part = gate[:, GROUP * g:GROUP * (g + 1)].rearrange("p h t -> p (h t)")
                    dve.tensor_tensor(part, part, bank(2 * (b % 2), 2), ALU.mult).then_inc(unit_free[b % 2], 1)
                elif kind == "v":
                    dve.wait_ge(proj, b + 1)
                    dve.tensor_copy(v[:, :, g * BLOCK:(g + 1) * BLOCK], psum[:, 2 * (b % 2):2 * (b % 2) + 2, :])\
                       .then_inc(unit_free[b % 2], 1)

            def decay(g):
                for d in range(2):
                    dve.wait_ge(unit_free[(5 * g + d) % 2], (5 * g + d) // 2 + 1)
                    for h in range(GROUP * g, GROUP * (g + 1)):
                        mark(dve.tensor_scalar(bb[d][:, h], kk[d][:, h], one_minus_lb[:, h:h + 1], lb0[:, h:h + 1],
                                               ALU.mult, ALU.add))
                    done()
                    part = slice(GROUP * g, GROUP * (g + 1))
                    dve.tensor_scalar(kk[d][:, part], bb[d][:, part], -1.0, 1.0, ALU.mult, ALU.add)\
                       .then_inc(f_done, 1)
                for d in range(2):
                    dve.wait_ge(ln_done, 2 * g + d + 1)
                    out = bb[d][:, GROUP * g:GROUP * (g + 1)].rearrange("p h t -> p (h t)")
                    logs = dif[d].rearrange("p u t -> p (u t)")
                    if d:
                        out, logs = out[:, ::-1], logs[:, ::-1]
                    mark(dve.tensor_tensor_scan(out, scan_keep, logs, 0.0, ALU.mult, ALU.add))
                done()

            def decays(g, n):
                for d in range(2):
                    c = 8 * g + 2 * n + d
                    if n:
                        dve.wait_ge(exp_done, c - 1)
                    B = heads(bb[d], g)
                    if n < 3:
                        size = (128, 64, 32)[n]
                        at = size // 2 - (d == 0)
                        view = B.rearrange("p u (b t) -> p (u b) t", t=size)
                        shape = (P, UNITS * (T // size), size)
                        ins = dve.tensor_tensor(dif[d].rearrange("p u (b t) -> p (u b) t", t=size), view,
                                                view[:, :, at:at + 1].broadcast_to(shape), ALU.subtract)
                    else:
                        view = bb[d][:, GROUP * g:GROUP * (g + 1), 0:T]
                        at = T - 1 if d == 0 else 0
                        ins = dve.tensor_tensor(dif[d][:, 0:GROUP], view,
                                                view[:, :, at:at + 1].broadcast_to((P, GROUP, T)), ALU.subtract)
                    ins.then_inc(dif_done, 1)
                for d in range(2):
                    dve.wait_ge(exp_done, 8 * g + 2 * n + d + 1)
                    if n < 2:
                        H = 64 >> n
                        vq, vk, vqq, vkk = (a.rearrange("p u (b t) -> p (u b) t", t=2 * H)
                                            for a in (Q[d], Kd[d], heads(q, g), heads(kk[d], g)))
                        early, behind = slice(0, H), slice(H, 2 * H)
                        qs, ks = (behind, early) if d == 0 else (early, behind)
                        dve.tensor_tensor(vq[:, :, qs], vq[:, :, qs], vqq[:, :, qs], ALU.mult)
                        ins = dve.tensor_tensor(vk[:, :, ks], vk[:, :, ks], vkk[:, :, ks], ALU.mult)
                    elif n == 2:
                        dve.tensor_tensor(Q[d], Q[d], heads(q, g), ALU.mult)
                        ins = dve.tensor_tensor(Kd[d], Kd[d], heads(kk[d], g), ALU.mult)
                    else:
                        part = slice(GROUP * g, GROUP * (g + 1))
                        dve.tensor_tensor(Q[d][:, 0:GROUP], Q[d][:, 0:GROUP], q[:, part, T:NT], ALU.mult)
                        ins = dve.tensor_tensor(Kd[d][:, 0:GROUP], Kd[d][:, 0:GROUP], kk[d][:, part, 0:T], ALU.mult)
                    ins.then_inc(qk_done, 1)

            def recur(g, item):
                if item == 0:
                    decay(g)
                if item <= 3:
                    decays(g, item)
                if item == 3:
                    dve.wait_ge(qk_used, 8 * g + 6)
                    mark(dve.tensor_tensor(AT, psum[:, 4:6, :].rearrange("p b (u t) -> p (b u) t", t=T),
                                           mask_f.unsqueeze(1).broadcast_to((P, UNITS, T)), ALU.mult))
                    mark(dve.tensor_tensor(fb_sb, psum[:, 6, 0:UNITS * 32].rearrange("p (u t) -> p u t", t=32),
                                           mask_b.unsqueeze(1).broadcast_to((P, UNITS, 32)), ALU.mult))
                    done()
                    for i in range(4):
                        at = slice(32 * i, 32 * i + 32)
                        ins = dve.tensor_tensor(AT[at, :, at], AT[at, :, at], fb_sb[at], ALU.add)
                    ins.then_inc(at_done, 1)
                elif item == 4:
                    dve.wait_ge(pv_done, g + 1)
                    dve.tensor_copy(heads(oT, g), psum[:, 4:6, :].rearrange("p b (u t) -> p (b u) t", t=T))\
                       .then_inc(o_copied, 1)
                elif item == 5:
                    dve.wait_ge(o_rstd, g + 1)
                    part = oT[:, GROUP * g:GROUP * (g + 1)].rearrange("p h t -> p (h t)")
                    link(dve.scalar_tensor_tensor(out=part, in0=part, scalar=gn_w[:, 0:1],
                                                  in1=dif[0].rearrange("p u t -> p (u t)"), op0=ALU.mult, op1=ALU.mult))
                    dve.tensor_tensor(part, part, gate[:, GROUP * g:GROUP * (g + 1)].rearrange("p h t -> p (h t)"),
                                      ALU.mult).then_inc(o_done, 1)

            for b in range(10):
                if b:
                    modulation(b + 1)
                if b >= 5:
                    recur(0, b - 5)
                project(b)
            modulation(11)
            recur(0, 5)
            for item in range(6):
                recur(1, item)

            def mixer_bank(m):
                def wait(k):
                    if k % 2 == 0:
                        dve.wait_ge(out_ps, 4 * m + k // 2 + 1)
                return wait

            residual(mod[:, 0, 2], mixer_bank(0))

            def top(values, pads, keep, out):
                for a in range(2):
                    best = best8[:, a]
                    link(dve.max(best, values[:, a, 0:values.shape[2] - pads]))
                    link(dve.memset(best[:, keep:8], 2 * LOW))
                    mark(dve.match_replace(out[:, a], best, values[:, a], 3 * LOW))
                done()

            scores, selv, t2, t3, mask = (route[:, n] for n in range(5))
            small16 = route[:, 5].rearrange("p a e -> p (a e)")
            m1, cnt, m2, c2 = (small16[:, 16 * n:16 * (n + 1)] for n in range(4))
            best8 = small16[:, 64:80].rearrange("p (a e) -> p a e", a=2)
            gs = route[:, 6].rearrange("p a e -> p (a e)")[:, 0:24].rearrange("p (a e) -> p a e", a=2)
            gs_o = route[:, 6].rearrange("p a e -> p (a e)")[:, 32:56].rearrange("p (a e) -> p a e", a=2)
            gmask = small16[:, 80:96].rearrange("p (a g) -> p a g", a=2)
            wsum = small16[:, 96:98]
            t1 = small16[:, 98:99]
            wide = route[:, 7:11].rearrange("p n a e -> p (n a e)")
            cand = wide[:, 0:2 * (E + 2)].rearrange("p (a e) -> p a e", a=2)
            cand_o = wide[:, 2 * (E + 2):4 * (E + 2)].rearrange("p (a e) -> p a e", a=2)

            def experts_front(m):
                M = moe[m]
                dve.memset(y[:, 1, 4:8], 0.0).then_inc(M.y[1], 1)
                squares(2 * m + 1)
                norm(2 * m + 1, mod[:, m, 3])
                link(dve.memset(gs, 2 * LOW))
                link(dve.memset(cand, 2 * LOW))
                dve.wait_ge(M.scores, 1)
                link(dve.tensor_tensor(selv, scores, router_b[:, m].unsqueeze(1).broadcast_to((P, 2, E)), ALU.add))

                def groups(a):
                    return a.rearrange("p a (g e) -> p (a g) e", g=GROUPS)

                link(dve.tensor_reduce(m1, groups(selv), AX.X, ALU.max))
                link(dve.tensor_tensor(groups(t2), groups(selv), m1.unsqueeze(2).broadcast_to((P, 16, 8)), ALU.is_equal))
                mark(dve.tensor_reduce(cnt, groups(t2), AX.X, ALU.add))
                link(dve.scalar_tensor_tensor(out=t3, in0=t2, scalar=LOW, in1=selv, op0=ALU.mult, op1=ALU.add))
                mark(dve.tensor_reduce(m2, groups(t3), AX.X, ALU.max))
                link(dve.tensor_scalar(c2, cnt, 1.5, LOW, ALU.is_lt, ALU.mult))
                link(dve.tensor_tensor(c2, c2, m1, ALU.add))
                link(dve.tensor_tensor(m2, m2, c2, ALU.max))
                link(dve.tensor_tensor(gs[:, :, 0:GROUPS], m1.rearrange("p (a g) -> p a g", a=2),
                                       m2.rearrange("p (a g) -> p a g", a=2), ALU.add))
                top(gs, 4, TOP_GROUPS, gs_o)
                link(dve.tensor_tensor(gmask, gs_o[:, :, 0:GROUPS], gs[:, :, 0:GROUPS], ALU.not_equal))
                link(dve.tensor_scalar(gmask, gmask, -1.0, -LOW, ALU.add, ALU.mult))
                for a in range(2):
                    mark(dve.tensor_tensor(cand[:, a, 0:E].rearrange("p (g e) -> p g e", g=GROUPS),
                                           selv[:, a].rearrange("p (g e) -> p g e", g=GROUPS),
                                           gmask[:, a].unsqueeze(2).broadcast_to((P, GROUPS, E // GROUPS)), ALU.add))
                done()
                top(cand, 2, TOP_K, cand_o)
                dve.tensor_tensor(mask, cand_o[:, :, 0:E], cand[:, :, 0:E], ALU.not_equal).then_inc(M.mask, 1)
                dve.wait_ge(M.mask, 1)
                link(dve.tensor_tensor(t2, scores, mask, ALU.mult))
                link(dve.tensor_reduce(wsum, t2, AX.X, ALU.add))
                link(dve.reciprocal(wsum, wsum))
                for a in range(2):
                    mark(dve.tensor_scalar(comb[:, a, 0:E], t2[:, a], wsum[:, a:a + 1], ROUTED_SCALE,
                                           ALU.mult, ALU.mult))
                dve.wait_ge(M.rank_ps, 1)
                link(dve.scalar_tensor_tensor(out=t3, in0=psum[:, 5, 0:2 * E].rearrange("p (a e) -> p a e", a=2),
                                              scalar=1.0, in1=mask, op0=ALU.add, op1=ALU.mult))
                mark(dve.tensor_scalar(rank[:, :, 0:E], t3, -1.0, None, ALU.add))
                link(dve.tensor_reduce(t1, psum[:, 5, 2 * E:3 * E], AX.X, ALU.max))
                link(dve.tensor_scalar(wsum[:, 0:1], t1, float(SLOTS), None, ALU.is_gt))
                link(dve.scalar_tensor_tensor(out=wsum[:, 1:2], in0=t1, scalar=2.0 * SLOTS, in1=wsum[:, 0:1],
                                              op0=ALU.is_gt, op1=ALU.add))
                dve.scalar_tensor_tensor(out=extra.bitcast(I32), in0=t1, scalar=3.0 * SLOTS, in1=wsum[:, 1:2],
                                         op0=ALU.is_gt, op1=ALU.add).then_inc(M.table, 1)
                for a in range(2):
                    dve.wait_ge(M.sh_silu, a + 1)
                    dve.tensor_tensor(sh_hid[:, a], sh_silu[:, a], psum[:, 6 + a, F:2 * F], ALU.mult)\
                       .then_inc(M.hid if a else M.sh_hid, 1)

            def one_hots(M, r, expert, j):
                base = C_IOTA + r * SLOTS
                shape = (P, 2, 2, SLOTS)
                slots = (consts[:, base:base + SLOTS] if isinstance(base, int) else consts[:, bass.ds(base, SLOTS)])
                ranks = rank[:, :, bass.ds(expert, 2)] if not isinstance(expert, int) else rank[:, :, expert:expert + 2]
                weights = comb[:, :, bass.ds(expert, 2)] if not isinstance(expert, int) else comb[:, :, expert:expert + 2]
                out = onehot[:, j].rearrange("p a (e s) -> p a e s", e=2)
                dve.tensor_tensor(out, slots.unsqueeze(1).unsqueeze(1).broadcast_to(shape),
                                  ranks.unsqueeze(3).broadcast_to(shape), ALU.is_equal).then_inc(M.onehot, 1)
                return out, weights.unsqueeze(3).broadcast_to(shape)

            def gathered(M, g, j):
                dve.wait_ge(M.xg_ps[1], g + 1)
                dve.tensor_copy(xg[:, j, 4:8], psum[:, 7, :].rearrange("p (k t) -> p k t", t=P)).then_inc(M.xg[1], 1)

            def experts_pass(M, r):
                first = r * (PAIRS + 1)
                if not isinstance(r, int):
                    dve.wait_ge(M.comb, first)
                dve.memset(hidT_c[:, 1, 2:4], 0.0).then_inc(M.c_zero, 1)

                def hots(expert, g, j):
                    out, weights = one_hots(M, r, expert, j)
                    dve.wait_ge(M.onehot, 2 * g + 1)
                    dve.tensor_tensor(onehot_w[:, j].rearrange("p a (e s) -> p a e s", e=2), out, weights, ALU.mult)\
                       .then_inc(M.onehot, 1)

                hots(0, first, 0)
                gathered(M, first, 0)
                with dve.Fori(0, PAIRS // 2) as h:
                    for j in range(2):
                        n, g = r * PAIRS + h * 2 + j, r * (PAIRS + 1) + h * 2 + j
                        dve.wait_ge(M.t_ps, n + 1)
                        hots(h * 4 + 2 * (j + 1), g + 1, 1 - j)
                        dve.wait_ge(M.silu, n + 1)
                        dve.tensor_tensor(hid[:, j], silu[:, j], psum[:, 4, F:2 * F], ALU.mult).then_inc(M.hid, 1)
                        gathered(M, g + 1, 1 - j)
                        dve.wait_ge(M.y_ps[1], n + 1)
                        dve.tensor_copy(y[:, j, :, P // 2:P].rearrange("s k p -> s p k"),
                                        psum[:, 7, :].rearrange("s (p k) -> s p k", k=K)).then_inc(M.y[1], 1)

            def experts(m):
                M = moe[m]
                dve.wait_ge(M.table, 1)
                experts_pass(M, 0)
                more = dve.value_load(extra[0:1, 0:1].bitcast(I32), min_val=0, max_val=3)
                with dve.If(more > 0):
                    with dve.Fori(0, more) as r:
                        experts_pass(M, r + 1)
                dve.wait_ge(M.done, 1)
                residual(mod[:, m, 5], lambda k: None)

            dve.wait_ge(st_out, 64)
            experts_front(0)
            experts(0)

            squares(2)
            norm(2, mod[:, 1, 0])
            for n in range(4):
                dve.wait_ge(bias_ps, n + 1)
                dve.tensor_tensor(bias[:, 4 * n:4 * n + 4], psum[:, 6 + n % 2, :].rearrange("p (h s) -> p h s", s=P),
                                  window.unsqueeze(1).broadcast_to((P, 4, P)), ALU.mult).then_inc(bias_done, 1)
            dve.wait_ge(bias_done, 4)
            link(dve.tensor_tensor(bias, bias, window_neg.unsqueeze(1).broadcast_to((P, A_HEADS, P)), ALU.add))
            for n in (2, 3):
                dve.wait_ge(proj, 10 + n + 1)
                dve.tensor_copy(kT[:, 4 * (n - 2):4 * (n - 2) + 4].rearrange("p k t -> p (k t)"), bank(2 * (n % 2), 2))\
                   .then_inc(unit_free[n % 2], 1)
            for g in range(4):
                dve.wait_ge(sc_ps, g + 1)
                for par in range(2):
                    lat = psum[:, 4 + par, :].rearrange("p (i n) -> p i n", i=2)
                    mark(dve.tensor_tensor(S_lat[:, 2 * par:2 * par + 2, 0:P], lat[:, :, 0:P],
                                           bias[:, 4 * g + par:4 * g + 4:2, :], ALU.add))
                    mark(dve.tensor_copy(S_lat[:, 2 * par:2 * par + 2, P:2 * P], lat[:, :, P:2 * P]))
                    mark(dve.tensor_reduce(neg_max[:, 4 + 2 * par:6 + 2 * par],
                                           psum[:, 6 + par, 0:2 * P].rearrange("p (i n) -> p i n", i=2), AX.X, ALU.max,
                                           negate=True))
                done()
                dve.tensor_reduce(neg_max[:, 0:4], S_lat, AX.X, ALU.max, negate=True).then_inc(sc_sb, 1)
                dve.wait_ge(p_exp, g + 1)
                link(dve.reciprocal(row_sum, row_sum))
                dve.tensor_tensor(S_lat, S_lat, row_sum[:, 0:4].unsqueeze(2).broadcast_to((P, 4, 2 * P)), ALU.mult)
                dve.tensor_tensor(S_pr, S_pr, row_sum[:, 4:8].unsqueeze(2).broadcast_to((P, 4, P)), ALU.mult)\
                   .then_inc(p_norm, 1)
                dve.wait_ge(pt_ps, g + 1)
                dve.tensor_copy(PT[:, 8:12].rearrange("p n t -> p (n t)"), psum[:, 2, :]).then_inc(pt_sb, 1)
            residual(mod[:, 1, 2], mixer_bank(1))

            dve.wait_ge(cache_out, 32)
            experts_front(1)
            experts(1)
            squares(4)
            norm(4, None)
            for n in (1, 3):
                dve.wait_ge(yt_ps, n + 1)
                dve.tensor_copy(y_tok[:, n // 2, :, 4:8].rearrange("s p k -> s k p"),
                                psum[:, n, :].rearrange("s (k p) -> s k p", p=P)).then_inc(yt_sb, 1)

        @block.tensor
        def _(pe):
            def mm(out, lhsT, rhs, start, stop, **kw):
                return pe.matmul(out, lhsT, rhs, start=start, stop=stop, skip_group_check=True, **kw)

            pe.wait_ge(s_const, 16)
            pe.wait_ge(s_x, 32)
            for n in range(4):
                for i in range(4):
                    k = 4 * (n // 2) + i
                    ins = pe.transpose(psum[:, n, i * T:(i + 1) * T], x_tok[:, n % 2, k::K], ident)
                ins.then_inc(x_ps, 1)
            pe.wait_ge(s_small, SMALL)
            for i in range(3):
                ins = pe.transpose(psum[:, 5, i * HEADS:(i + 1) * HEADS], lbrow[0:HEADS, i], ident[0:HEADS, 0:HEADS])
            ins.then_inc(lb_ps, 1)
            pe.wait_ge(ready, 5)

            def norm_sums(n):
                pe.wait_ge(sq_done, 2 * (n + 1))
                for k in range(K):
                    ins = mm(psum[:, 4, 0:NT], ones, sq[:, k], k == 0, k == K - 1)
                ins.then_inc(ssum, 1)

            norm_sums(0)
            pe.wait_ge(cond_done, 1)
            at_stage = [0]

            def staged():
                n = at_stage[0]
                at_stage[0] += 1
                pe.wait_ge(stage_in[n % 3], 16 * (n // 3 + 1))
                return stage[n % 3]

            def ada(n):
                w = staged()
                if n % 2:
                    pe.wait_ge(ada_row, n)
                elif n:
                    pe.wait_ge(mod_done, n // 2)
                for i in range(K // 4):
                    for c in range(4):
                        ins = mm(psum[32 * c:32 * c + 32, 7, :], cond_act[:, 4 * i + c, :], w[:, 4 * i + c, :],
                                 i == 0, i == K // 4 - 1)
                ins.then_inc(ada_ps, 1)
                pe.wait_ge(ada_ps, n + 1)
                pe.sem_inc(stage_used, 1)

            def ada_columns(n):
                pe.wait_ge(ada_row, 2 * n + 2)
                for k in range(K):
                    ins = mm(psum[:, 7, 2 * k:2 * k + 2], mrow[:, k::K], sel, True, True)
                ins.then_inc(sel_ps, 1)

            for n in range(2):
                ada(2 * n)
                ada(2 * n + 1)
                ada_columns(n)
            pe.wait_ge(h_done, 1)

            def project(b, by_rows):
                w = staged()
                u = 2 * (b % 2)
                if b >= 2:
                    pe.wait_ge(unit_free[b % 2], b // 2)
                if by_rows:
                    for a in range(2):
                        for k in range(K):
                            ins = mm(psum[:, u + a, :], hT[:, k, a * T:(a + 1) * T], w[:, k], k == 0, k == K - 1)
                else:
                    for n in range(4):
                        for k in range(K):
                            ins = mm(psum[:, u + n // 2, (n % 2) * NT:(n % 2 + 1) * NT], w[:, k, n * P:(n + 1) * P],
                                     hT[:, k], k == 0, k == K - 1)
                ins.then_inc(proj, 1)
                pe.wait_ge(proj, b + 1)
                pe.sem_inc(stage_used, 1)

            def scores(g, n):
                if n == 0 and g:
                    pe.wait_ge(o_rstd, g)
                if n == 2 and g:
                    pe.wait_ge(st_sb, 2 * g)
                for d in range(2):
                    pe.wait_ge(qk_done, 8 * g + 2 * n + d + 1)
                    for u in range(UNITS):
                        size = (128, 64, 32)[n]
                        for i in range(T // size):
                            early = slice(size * i, size * i + size // 2)
                            behind = slice(size * i + size // 2, size * (i + 1))
                            ss, ts = (early, behind) if d == 0 else (behind, early)
                            if n == 2:
                                ss = ts = slice(size * i, size * (i + 1))
                            if n == 2 and d:
                                out = psum[ss, 6, 32 * u:32 * u + 32]
                            else:
                                c = (u % 4) * T
                                out = psum[ss, 4 + u // 4, c + ts.start:c + ts.stop]
                            ins = mm(out, Kd[d][:, u, ss], Q[d][:, u, ts], True, True)
                    ins.then_inc(qk_used, 1)

            def values(g):
                pe.wait_ge(at_done, g + 1)
                pe.wait_ge(qk_done, 8 * g + 8)
                pe.wait_ge(unit_free[(5 * g + 4) % 2], (5 * g + 4) // 2 + 1)
                pe.wait_ge(s_s0, 32)
                for u in range(UNITS):
                    h, s = GROUP * g + u // 2, u % 2
                    out = psum[:, 4 + u // 4, (u % 4) * T:(u % 4 + 1) * T]
                    ins = mm(out, v[:, s, h * DV:(h + 1) * DV], AT[:, u], True, s == 0)
                    if s:
                        for d in range(2):
                            ins = mm(out, s0[:, d, h], Q[d][:, u // 2], False, d == 1)
                ins.then_inc(pv_done, 1)

            def turn_keys(g, d):
                if d:
                    pe.wait_ge(st_sb, 2 * g + 1)
                for i in range(GROUP):
                    ins = pe.transpose(psum[:, 6, i * T:(i + 1) * T], Kd[d][:, i], ident)
                ins.then_inc(kd_ps, 1)
                if d:
                    pe.wait_ge(kd_ps, 2 * g + 2)
                    pe.sem_inc(qk_used, 2)

            def state(g, d):
                pe.wait_ge(kd_sb, 2 * g + d + 1)
                for i in range(GROUP):
                    h = GROUP * g + i
                    ins = mm(psum[:, 6, i * DV:(i + 1) * DV], Kd[d][:, GROUP + i], v[:, 0, h * DV:(h + 1) * DV],
                             True, True)
                ins.then_inc(st_ps, 1)

            def recur(g, item):
                if item <= 2:
                    scores(g, item)
                elif item == 3:
                    values(g)
                    turn_keys(g, 0)
                elif item == 4:
                    pe.wait_ge(o_sq, g + 1)
                    for i in range(2):
                        ins = mm(psum[:, 4 + i, :], ones, dif[0][:, 4 * i:4 * i + 4], True, True)
                    ins.then_inc(o_ssum, 1)
                    state(g, 0)
                elif item == 5:
                    turn_keys(g, 1)
                elif item == 6:
                    state(g, 1)

            for b in range(10):
                if b:
                    ada_columns(b + 1)
                ada(4 + 2 * b)
                project(b, KINDS[b % 5] == "v")
                if b >= 5:
                    recur(0, b - 5)
                ada(5 + 2 * b)
            ada_columns(11)
            for item in (5, 6):
                recur(0, item)
            for item in range(7):
                recur(1, item)

            def project_out(m, src, read):
                pe.wait_ge(late_in, 16 * (m + 1))
                for a, n in read:
                    pe.wait_ge(a, n)
                for k in range(K):
                    for h in range(K):
                        ins = mm(psum[:, k // 2, (k % 2) * NT:(k % 2 + 1) * NT], late[:, h, k::K], src[:, h],
                                 h == 0, h == K - 1)
                    if k % 2:
                        ins.then_inc(out_ps, 1)
                pe.wait_ge(out_ps, 4 * (m + 1))
                pe.sem_inc(late_used, 1)

            project_out(0, oT, [(o_done, 2), (unit_free[0], 5), (unit_free[1], 5)])

            def experts_front(m):
                M = moe[m]
                norm_sums(2 * m + 1)
                pe.wait_ge(h_done, 2 * m + 2)
                for a in range(2):
                    for k in range(K):
                        ins = mm(psum[:, 5, a * E:(a + 1) * E], hT[:, k, a * T:(a + 1) * T], router_w[:, m, k],
                                 k == 0, k == K - 1)
                ins.then_inc(M.logits, 1)
                for n in range(4):
                    if n >= 2:
                        pe.wait_ge(M.htok, n - 1)
                    for i in range(4):
                        ins = pe.transpose(psum[:, 6 + n % 2, i * P:(i + 1) * P],
                                           hT[:, 4 * (n % 2) + i, (n // 2) * T:(n // 2 + 1) * T], ident)
                    ins.then_inc(M.htok_ps, 1)
                pe.wait_ge(M.sh_in, 48)
                for a in range(2):
                    pe.wait_ge(M.htok, 3 + a)
                    for k in range(K):
                        ins = mm(psum[:, 6 + a, :], hT[:, k, a * T:(a + 1) * T], ws_gu[:, k], k == 0, k == K - 1)
                    ins.then_inc(M.sh_ps, 1)
                pe.wait_ge(M.mask, 1)
                mask = route[:, 4]
                mm(psum[:, 5, 0:E], before, mask[:, 0], True, True)
                mm(psum[:, 5, E:2 * E], ones, mask[:, 0], True, False)
                mm(psum[:, 5, E:2 * E], before, mask[:, 1], False, True)
                mm(psum[:, 5, 2 * E:3 * E], ones, mask[:, 0], True, False)
                mm(psum[:, 5, 2 * E:3 * E], ones, mask[:, 1], False, True).then_inc(M.rank_ps, 1)
                pe.wait_ge(M.sh_hid, 1)
                pe.wait_ge(M.hid, 1)
                for c in range(2):
                    for a in range(2):
                        ins = pe.transpose(psum[:, 4, c * NT + a * T:c * NT + (a + 1) * T],
                                           sh_hid[:, a, c * P:(c + 1) * P], ident)
                ins.then_inc(M.t_ps, 1)
                pe.wait_ge(M.t_sb, 1)
                for k in range(K):
                    for c in range(2):
                        ins = mm(psum[:, k // 2, (k % 2) * NT:(k % 2 + 1) * NT], ws_dn[:, c, k::K], sh_hidT[:, c],
                                 k % 2 == 0 and c == 0, False)
                ins.then_inc(M.sh_used, 1)

            def gather(M, g, n, j):
                pe.wait_ge(M.onehot, g * 2 + 2)
                for half in range(2):
                    pe.wait_ge(M.y[half], n + 1)
                    for i in range(4):
                        for a in range(2):
                            ins = mm(psum[:, 6 + half, i * P:(i + 1) * P], h_tok[:, a, 4 * half + i], onehot[:, j, a],
                                     a == 0, a == 1)
                    ins.then_inc(M.xg_ps[half], 1)

            def combine(M, j):
                for k in range(K):
                    ins = mm(psum[:, k // 2, (k % 2) * NT:(k % 2 + 1) * NT], y[:, j, k],
                             hidT_c[:, j, 2:4].rearrange("p a t -> p (a t)"), False, False)
                ins.then_inc(M.comb, 1)

            def experts_pass(M, r):
                if not isinstance(r, int):
                    for half in range(2):
                        pe.wait_ge(M.xg[half], r * (PAIRS + 1))
                gather(M, r * (PAIRS + 1), r * PAIRS, 0)
                with pe.Fori(0, PAIRS // 2) as h:
                    for j in range(2):
                        n, g = r * PAIRS + h * 2 + j, r * (PAIRS + 1) + h * 2 + j
                        pe.wait_ge(M.gu_in[j], (r * (PAIRS // 2) + h) * 64 + 64)
                        pe.wait_ge(M.xg[0], g + 1)
                        pe.wait_ge(M.xg[1], g + 1)
                        pe.wait_ge(M.hid, n + 1)
                        for k in range(K):
                            for w in range(2):
                                for e in range(2):
                                    at = slice(SLOTS * e, SLOTS * (e + 1))
                                    ins = mm(psum[at, 4, w * F:(w + 1) * F], xg[:, j, k, at],
                                             ring[:, j, 2 * e + w, k * F:(k + 1) * F], k == 0 and w == 0, k == K - 1)
                        ins.then_inc(M.gu, 1)
                        gather(M, g + 1, n, 1 - j)
                        pe.wait_ge(M.hid, n + 2)
                        pe.wait_ge(M.t_sb, n + 1)
                        for c in range(2):
                            pe.transpose(psum[:, 5, c * P:(c + 1) * P], hid[:, j, c * P:(c + 1) * P], ident)
                        for a in range(2):
                            ins = pe.transpose(psum[:, 5, (2 + a) * P:(3 + a) * P], onehot_w[:, j, a], ident)
                        ins.then_inc(M.t_ps, 1)
                        pe.wait_ge(M.c_zero, r + 1)
                        combine(M, 1 - j)
                        pe.wait_ge(M.dn_in[j], (r * (PAIRS // 2) + h) * 32 + 32)
                        pe.wait_ge(M.t_sb, n + 2)
                        for half in range(2):
                            pe.wait_ge(M.xg[half], g + 2)
                            for c in range(2):
                                for e in range(2):
                                    at = slice(SLOTS * e, SLOTS * (e + 1))
                                    ins = mm(psum[at, 6 + half, :], hidT_c[:, j, c, at],
                                             ring[:, j, 4 + e, c * D + half * BLOCK:c * D + (half + 1) * BLOCK],
                                             c == 0, c == 1)
                            ins.then_inc(M.y_ps[half], 1)
                        pe.wait_ge(M.y_ps[1], n + 1)
                        pe.sem_inc(M.dn_used, 1)
                for half in range(2):
                    pe.wait_ge(M.y[half], r * PAIRS + PAIRS + 1)
                combine(M, 1)

            def experts(m):
                M = moe[m]
                experts_pass(M, 0)
                pe.wait_ge(M.table, 1)
                more = pe.value_load(extra[0:1, 0:1].bitcast(I32), min_val=0, max_val=3)
                with pe.If(more > 0):
                    with pe.Fori(0, more) as r:
                        experts_pass(M, r + 1)
                pe.wait_ge(M.comb, more * (PAIRS + 1) + (PAIRS + 1))
                pe.sem_inc(M.done, 1)

            experts_front(0)
            experts(0)

            norm_sums(2)
            pe.wait_ge(h_done, 3)
            for b in range(10, 12):
                project(b, False)
            pe.wait_ge(cache_in, 32)
            for n in range(2):
                for i in range(4):
                    ins = pe.transpose(psum[:, 4 + n, i * P:(i + 1) * P], ck[:, (4 * n + i) * P:(4 * n + i + 1) * P], ident)
                ins.then_inc(tr_ps, 1)
            pe.wait_ge(bias_in, 64)
            for n in range(4):
                if n >= 2:
                    pe.wait_ge(bias_done, n - 1)
                mm(psum[:, 6 + n % 2, :], flip, bias[:, 4 * n:4 * n + 4].rearrange("p h s -> p (h s)"), True, True)\
                    .then_inc(bias_ps, 1)
            for b in range(12, 14):
                project(b, False)
            for b in range(14, 16):
                project(b, True)
            for n in range(2):
                pe.wait_ge(tr_sb, n + 1)
                pe.wait_ge(unit_free[n], 7)
                for i in range(4):
                    ins = pe.transpose(psum[:, 4 + n, i * P:(i + 1) * P], kT[:, 4 * n + i, 0:T], ident)
                ins.then_inc(tr_ps, 1)
            for u in range(2):
                pe.wait_ge(unit_free[u], 8)
            pe.wait_ge(tr_sb, 4)

            def attend(g):
                if g:
                    pe.wait_ge(p_exp, g)
                for i in range(2):
                    for par in range(2):
                        rows, c = slice(HD * par, HD * (par + 1)), 2 * g + i
                        at = psum[:, 4 + par, i * 2 * P:(i + 1) * 2 * P]
                        mm(at[:, 0:P], qT[rows, c, T:NT], kT[rows, c, T:NT], True, True)
                        mm(at[:, P:2 * P], qT[rows, c, T:NT], ckT[rows, c], True, True)
                for i in range(2):
                    for par in range(2):
                        rows, c = slice(HD * par, HD * (par + 1)), 2 * g + i
                        ins = mm(psum[:, 6 + par, i * P:(i + 1) * P], qT[rows, c, 0:T], kT[rows, c, 0:T], True, True)
                ins.then_inc(sc_ps, 1)

            attend(0)
            for g in range(4):
                pe.wait_ge(p_norm, g + 1)
                for n in range(4):
                    for i in range(2):
                        m = 2 * n + i
                        pe.transpose(psum[:, m // 4, (m % 4) * P:(m % 4 + 1) * P], S_lat[:, n, i * P:(i + 1) * P], ident)
                for n in range(4):
                    ins = pe.transpose(psum[:, 2, n * P:(n + 1) * P], S_pr[:, n], ident)
                ins.then_inc(pt_ps, 1)
                if g < 3:
                    attend(g + 1)
                pe.wait_ge(pt_sb, 2 * (g + 1))
                if g:
                    pe.wait_ge(oa_sb, g)
                for n in range(4):
                    par, i = n // 2, n % 2
                    cols = slice((4 * g + 2 * i + par) * HD, (4 * g + 2 * i + par + 1) * HD)
                    rows = slice(HD * par, HD * (par + 1))
                    mm(psum[rows, 3, (2 * i + 1) * P:(2 * i + 2) * P], va[:, 1, cols], PT[:, 2 * n], True, False)
                    mm(psum[rows, 3, (2 * i + 1) * P:(2 * i + 2) * P], cv[:, cols], PT[:, 2 * n + 1], False, True)
                    ins = mm(psum[rows, 3, 2 * i * P:(2 * i + 1) * P], va[:, 0, cols], PT[:, 8 + n], True, True)
                ins.then_inc(oa_ps, 1)
            project_out(1, oTa, [(oa_sb, 4)])
            experts_front(1)
            experts(1)
            norm_sums(4)
            pe.wait_ge(h_done, 5)
            for n in range(4):
                for i in range(4):
                    k = 4 * (n % 2) + i
                    ins = pe.transpose(psum[:, n, i * P:(i + 1) * P], hT[:, k, (n // 2) * T:(n // 2 + 1) * T], ident)
                ins.then_inc(yt_ps, 1)


INPUTS = ["x_prompt", "x_sample", "state_hgrn_fwd", "state_hgrn_bwd", "cache_na_k", "cache_na_v", "c", "c_ctx",
          "norm1_w", "norm2_w", "ada_w", "ada_b", "hgrn_w_in", "hgrn_lb_logits", "hgrn_gn_w", "hgrn_w_out",
          "na_w_qkv", "na_rpb", "na_w_o", "moe_w_router", "moe_router_bias", "moe_w_gate", "moe_w_up", "moe_w_down",
          "shared_w_gate", "shared_w_up", "shared_w_down", "final_norm_w"]
OUTPUTS = [("out_prompt", (1, T, D)), ("out_sample", (1, T, D)),
           ("out_state_fwd", (1, 1, HEADS, DK, DV)), ("out_state_bwd", (1, 1, HEADS, DK, DV)),
           ("out_cache_k", (1, 1, T, A_HEADS, HD)), ("out_cache_v", (1, 1, T, A_HEADS, HD))]


def kernel(**inputs):
    import concourse.bacc as bacc
    from concourse.bass_utils import run_bass_kernel_spmd

    nc = bacc.Bacc("TRN2", target_bir_lowering=False, num_devices=1)
    arrays = {f"in_{n}": np.ascontiguousarray(inputs[n]) for n in INPUTS}
    arrays["in_table"] = shape_constants()
    io = {n[3:]: nc.dram_tensor(n, a.shape, mybir.dt.from_np(a.dtype), kind="ExternalInput").ap()
          for n, a in arrays.items()}
    for n, shape in OUTPUTS:
        io[n] = nc.dram_tensor(n, shape, F32, kind="ExternalOutput").ap()
    build(nc, io)
    r = run_bass_kernel_spmd(nc, [arrays], core_ids=[0])
    return tuple(r.results[0][n] for n, _ in OUTPUTS)
```

```python
from contextlib import ExitStack

import numpy as np

import concourse.bass as bass
from concourse import mybir
from concourse.alu_op_type import AluOpType as ALU

ACT = mybir.ActivationFunctionType
AX = mybir.AxisListType
F32 = mybir.dt.float32
BF16 = mybir.dt.bfloat16
I32 = mybir.dt.int32

P = 128
D = 1024
K = D // P
T = 128
NT = 2 * T
EPS = 1e-6
HEADS, DK, DV = 8, 128, 128
GROUP = 4
A_HEADS, HD = 16, 64
GRID_W, WIN_R, WIN_C = 64, 8, 16
E, TOP_K, GROUPS, TOP_GROUPS = 64, 6, 8, 4
F = 256
SLOTS = 64
PAIRS = E // 2
ROUTED_SCALE = 2.5
LOW = -1e30
BLOCK = 512
BLOCK_W = K * BLOCK

C_ID, C_MASKF, C_MASKB, C_BEFORE, C_IOTA, C_SEL, C_WIN, C_WNEG, C_FLIP, C_END = np.cumsum(
    [0, 128, 128, 32, 128, 4 * SLOTS, 2, 128, 128, 128]).tolist()


def shape_constants():
    c = np.zeros((P, C_END), np.float32)
    i, j = np.arange(P)[:, None], np.arange(P)[None, :]
    c[:, C_ID:C_ID + P] = i == j
    c[:, C_MASKF:C_MASKF + P] = (i // 32 != j // 32) | (i <= j)
    c[:, C_MASKB:C_MASKB + 32] = i % 32 >= np.arange(32)[None, :]
    c[:, C_BEFORE:C_BEFORE + P] = i < j
    c[:, C_IOTA:C_IOTA + 4 * SLOTS] = np.arange(4 * SLOTS)[None, :]
    for g in range(4):
        for s in range(2):
            c[32 * g + s, C_SEL + s] = 1.0
    start = np.clip(np.arange(GRID_W) - WIN_C // 2, 0, GRID_W - WIN_C)
    col = np.arange(P) % GRID_W
    inside = (col[None, :] >= start[col][:, None]) & (col[None, :] < start[col][:, None] + WIN_C)
    c[:, C_WIN:C_WIN + P] = inside
    c[:, C_WNEG:C_WNEG + P] = np.where(inside, 0.0, LOW)
    c[:, C_FLIP:C_FLIP + P] = (i // GRID_W == j // GRID_W) & (i % GRID_W + j % GRID_W == GRID_W - 1)
    return c


def build(nc, io):
    ctx = ExitStack()
    with ctx:
        def sem(name):
            return ctx.enter_context(nc.semaphore(name))

        WORDS = 53200
        arena = ctx.enter_context(nc.sbuf_tensor("arena", [P, WORDS], F32))
        top = [0]

        def cut(n, shape=None, at=None, dtype=None):
            a = top[0] if at is None else at
            if at is None:
                top[0] += n
                assert top[0] <= WORDS, top[0]
            v = arena[:, a:a + n]
            if dtype is not None:
                v = v.bitcast(dtype)
            if shape:
                names = "abcd"[:len(shape)]
                v = v.rearrange(f"p ({' '.join(names)}) -> p {' '.join(names)}", **dict(zip(names, shape)))
            return v

        xT = cut(K * NT, (K, NT))
        hT = cut(K * NT, (K, NT))
        consts = cut(C_END)
        ones = cut(P)
        mod = cut(2 * 48 * 2, (2, 6, K, 2))
        gain = cut(4 * K * 2, (4, K, 2))
        norm_w = cut(5 * K, (5, K))
        ada_b = cut(2 * 48, (2, 6, K))
        lb = cut(3 * HEADS, (3, HEADS))
        lb0 = cut(HEADS)
        lb_t = cut(HEADS)
        one_minus_lb = cut(HEADS)
        gn_w = cut(1)
        eps = cut(1)
        cond = cut(2 * K, (2, K))
        cond_act = cut(K * 32, (K, 32))
        router_w = cut(2 * K * E, (2, K, E))
        router_b = cut(2 * E, (2, E))
        rank = cut(2 * (E + 2), (2, E + 2))
        comb = cut(3 * (E + 2), (2, E + 2, 3), dtype=BF16)
        ident_b = cut(P // 2, dtype=BF16)
        extra = cut(1)
        rstd = cut(NT)
        PAIR_W = 6 * K * F
        ring_at = top[0]
        ring = cut(2 * PAIR_W, (2, 6, K * F))
        late_at = top[0]
        late = cut(HEADS * D, (HEADS, D))
        ws_gu = cut(K * 2 * F, (K, 2 * F), at=late_at)
        ws_dn = cut(2 * D, (2, D), at=late_at + K * 2 * F)
        scratch_at = top[0]
        SCRATCH_W = WORDS - scratch_at

        class Scratch:
            def __init__(self, at, size):
                self.at, self.end = at, at + size

            def __call__(self, n, shape=None, dtype=None):
                self.at += n
                assert self.at <= self.end, (self.at, self.end)
                return cut(n, shape, at=self.at - n, dtype=dtype)

        stage = [cut(BLOCK_W, (K, BLOCK), at=at + n * BLOCK_W)
                 for at, count in ((ring_at, 3), (late_at, 2)) for n in range(count)]

        sc = Scratch(scratch_at, SCRATCH_W)
        h_tok = sc(3 * D, (3, 2, K, P), BF16)
        xg = sc(2 * K * P, (2, K, P))
        onehot = sc(2 * P, (2, 2, P), BF16)
        onehot_t = sc(2 * P, (2, 2, P), BF16)
        hidT = sc(2 * 2 * P, (2, 2, P))
        hid = sc(2 * 2 * P, (2, 2 * P))
        silu = sc(2 * F, (2, F))
        y = sc(3 * D, (2, 3, K, P), BF16)
        route = sc(12 * 2 * E, (12, 2, E))
        slot_w = sc(2)
        slot_parts = sc(2 * 3, (2, 3))
        h_rest = xg
        y_rest = route.rearrange("p n a e -> p (n a e)")[:, 0:D].rearrange("p (k t) -> p k t", k=K)
        sq = cut(K * NT, (K, NT), at=scratch_at)
        sh_room = y[:, 0].rearrange("p i k t -> p (i k t)").bitcast(F32).rearrange("p (n a f) -> p n a f", n=3, a=2)
        sh_silu, sh_hid, sh_hidT = (sh_room[:, n] for n in range(3))

        sc = Scratch(ring_at + PAIR_W, PAIR_W)
        q = sc(HEADS * NT, (HEADS, NT))
        kk = [sc(HEADS * NT, (HEADS, NT)) for _ in range(2)]
        bb = [sc(HEADS * NT, (HEADS, NT)) for _ in range(2)]
        gate = sc(HEADS * NT, (HEADS, NT))
        oT = q
        sc = Scratch(scratch_at, SCRATCH_W)
        v = sc(2 * D, (2, D))
        s0 = sc(2 * D, (2, HEADS, DV))
        UNITS = GROUP * 2
        Q = [sc(UNITS * T, (UNITS, T)) for _ in range(2)]
        Kd = [sc(UNITS * T, (UNITS, T)) for _ in range(2)]
        dif = [sc(UNITS * T, (UNITS, T)) for _ in range(2)]
        AT = dif[1]
        fb_sb = sc(UNITS * 32, (UNITS, 32))
        scan_keep = sc(UNITS * T)
        mrow = sc(D, (D,))
        x_tok = cut(2 * D, (2, D), at=scratch_at)
        lbrow = cut(3 * P, (3, P), at=scratch_at + 2 * D)

        sc = Scratch(ring_at + PAIR_W, PAIR_W)
        qT = sc(K * NT, (K, NT))
        kT = sc(K * NT, (K, NT))
        va = sc(2 * D, (2, D))
        ckT = sc(K * T, (K, T))
        cv = sc(D, (D,))
        ck = sc(D, (D,))
        bias = sc(A_HEADS * P, (A_HEADS, P))
        sc = Scratch(scratch_at, SCRATCH_W)
        sc(K * NT)
        S_lat = sc(2 * 4 * 2 * P, (2, 4, 2 * P))
        S_pr = sc(2 * 4 * P, (2, 4, P))
        PT = sc(12 * P, (12, P))
        oTa = sc(K * NT, (K, NT))
        kout = sc(D, (K, P))
        neg_max = sc(2 * 8, (2, 8))
        row_sum = sc(2 * 8, (2, 8))
        y_tok = cut(2 * D, (2, P, K), at=scratch_at + K * NT)

        ident = consts[:, C_ID:C_ID + P]
        mask_f = consts[:, C_MASKF:C_MASKF + P]
        mask_b = consts[:, C_MASKB:C_MASKB + 32]
        before = consts[:, C_BEFORE:C_BEFORE + P]
        sel = consts[:, C_SEL:C_SEL + 2]
        window = consts[:, C_WIN:C_WIN + P]
        window_neg = consts[:, C_WNEG:C_WNEG + P]
        flip = consts[:, C_FLIP:C_FLIP + P]

        psum = ctx.enter_context(nc.psum_tensor("psum", [P, 8, 512], F32))

        s_const, s_x, s_small, s_s0 = sem("consts_in"), sem("x_in"), sem("small_in"), sem("states_in")
        stage_in = [sem(f"stage_in{n}") for n in range(5)]
        late_in, late_half = sem("late_in"), sem("late_half_used")
        cache_in, bias_in = sem("cache_in"), sem("bias_in")
        ready = sem("start_values_ready")
        x_ps, x_sb = sem("xT_in_psum"), sem("xT_in_sbuf")
        lb_ps, lb_shift, lb_exp = sem("lb_in_psum"), sem("lb_shifted"), sem("lb_exp")
        cond_done = sem("cond_act_done")
        ada_ps, ada_row, sel_ps, mod_done = sem("ada_in_psum"), sem("ada_rows"), sem("ada_cols_in_psum"), sem("mod_done")
        sq_done, ssum, root, h_done = sem("squares"), sem("square_sums"), sem("root"), sem("h_done")
        x_normed, gains = sem("x_normed"), sem("gains_ready")
        proj, gate_sig, v_sb = sem("proj_in_psum"), sem("gate_sigmoid"), sem("v_rows")
        unit_free = [sem("proj_unit0_read"), sem("proj_unit1_read")]
        f_done, ln_done = sem("decay_done"), sem("log_decay_done")
        dif_done, exp_done, qk_done, qk_used = sem("dif_done"), sem("exp_done"), sem("qk_done"), sem("qk_used")
        at_done, pv_done, o_copied, o_sq, o_ssum, o_rstd, o_done = (
            sem(n) for n in ("scores_masked", "pv_done", "o_copied", "o_squares", "o_square_sums", "o_rstd", "o_done"))
        kd_ps, kd_sb, st_ps, st_sb, st_out = (
            sem(n) for n in ("kdecT_in_psum", "kdecT", "state_in_psum", "state", "state_stored"))
        out_ps, resid = sem("mixer_out_in_psum"), sem("residual_added")
        dve_c, act_c = sem("dve_chain"), sem("act_chain")
        tr_ps, tr_sb = sem("key_rows_in_psum"), sem("key_rows")
        bias_ps, bias_done = sem("bias_in_psum"), sem("bias_windowed")
        sc_ps, sc_sb, p_exp, p_norm, pt_ps, pt_sb, oa_ps, oa_sb = (
            sem(n) for n in ("scores_in_psum", "scores_read", "probs", "probs_normed", "probsT_in_psum", "probsT",
                             "attn_in_psum", "attn_done"))
        cache_out = sem("cache_stored")
        yt_ps, yt_sb, y_out = sem("yT_in_psum"), sem("y_rows"), sem("y_stored")

        class Moe:

            def __init__(self, l):
                def s(name):
                    return sem(f"{name}_{l}")

                self.logits, self.scores = s("logits"), s("scores")
                self.htok_ps, self.htok, self.h_high = s("htok_ps"), s("htok"), s("h_high")
                self.h_rest, self.h_mid, self.h_low = s("h_rest"), s("h_mid"), s("h_low")
                self.mask, self.rank_ps, self.table = s("mask"), s("rank_ps"), s("table")
                self.sh_in, self.sh_ps, self.sh_silu, self.sh_hid = s("sh_in"), s("sh_ps"), s("sh_silu"), s("sh_hid")
                self.sh_used = s("sh_used")
                self.gu_in = [s("gu_in0"), s("gu_in1")]
                self.dn_in = [s("dn_in0"), s("dn_in1")]
                self.gu = s("gu")
                self.onehot, self.hot_ps, self.hot_t = s("onehot"), s("hot_ps"), s("hot_t")
                self.xg_ps = [s("xg_ps0"), s("xg_ps1")]
                self.xg = [s("xg_act"), s("xg_dve")]
                self.silu, self.hid, self.t_ps, self.t_sb = s("silu"), s("hid"), s("t_ps"), s("t_sb")
                self.y_ps = [s("y_ps0"), s("y_ps1")]
                self.y_high, self.y_rest, self.y_mid, self.y_low = s("y_high"), s("y_rest"), s("y_mid"), s("y_low")
                self.comb, self.c_zero, self.done = s("comb"), s("c_zero"), s("moe_done")

        moe = [Moe(0), Moe(1)]

        block = ctx.enter_context(nc.Block())

        KINDS = ["f_fw", "f_bw", "q", "gate", "v"]
        ROUNDS = [(0, [], 1), (1, [], 1), (2, [], 1), (3, [(0, 0)], 1), (4, [(0, 1)], 1), (5, [(0, 2)], 1),
                  (6, [(0, 3)], 2), (7, [(0, 4)], 2), (8, [(0, 5), (0, 6)], 2), (9, [(0, 7), (1, 0)], 2),
                  (None, [(1, 1)], 1), (None, [(1, 2)], 1), (None, [(1, 3)], 1), (None, [(1, 4)], 1),
                  (None, [(1, 5)], 1), (None, [(1, 6)], 1), (None, [(1, 7)], 0)]
        COL = {"q": 0, "f_fw": D, "f_bw": 2 * D, "v": 3 * D, "gate": 4 * D}
        parts = [(l, j) for l in range(2) for j in range(6)]
        stages = [("ada", l, j, half) for l, j in parts[:2] for half in range(2)]
        halves = [("ada", l, j, half) for l, j in parts[2:] for half in range(2)]
        for b, _, count in ROUNDS:
            stages += [("in", b // 5, KINDS[b % 5])] if b is not None else []
            stages += [halves.pop(0) for _ in range(count)]
        assert not halves

        def ada_rounds():
            first = 4
            for b, items, count in ROUNDS:
                yield b, items, (first // 2 - 1 if first % 2 == 0 and first > 4 else None), range(first, first + count)
                first += count

        stages0 = len(stages)
        stages += [("qkv", n) for n in range(6)]

        def stage_source(what):
            if what[0] == "ada":
                _, l, j, half = what
                src = io["ada_w"][l, :, j * D + half * BLOCK:j * D + (half + 1) * BLOCK]
            elif what[0] == "in":
                c = COL[what[2]] + what[1] * BLOCK
                src = io["hgrn_w_in"][0, :, c:c + BLOCK]
            else:
                src = io["na_w_qkv"][0, :, what[1] * BLOCK:(what[1] + 1) * BLOCK]
            return src.rearrange("(p k) n -> p k n", p=P)

        rooms = [(n - stages0 + 3) % 5 for n in range(stages0)] + [3, 4, 0, 1, 2, 0]
        room_count = [rooms[:n + 1].count(rooms[n]) for n in range(len(rooms))]

        def block_used(n):
            ada_n = sum(w[0] == "ada" for w in stages[:n + 1])
            return (ada_ps, ada_n) if stages[n][0] == "ada" else (proj, n + 1 - ada_n)

        SMALL = 12 * 16

        def bank(n, count=1):
            return psum[:, n:n + count, :].rearrange("p b n -> p (b n)")

        def heads(a, g):
            return a[:, GROUP * g:GROUP * (g + 1)].rearrange("p h (s t) -> p (h s) t", s=2)

        small = [
            (cond[:, 0, :], io["c_ctx"].rearrange("(p k) -> p k", p=P)),
            (cond[:, 1, :], io["c"][0].rearrange("(p k) -> p k", p=P)),
            (norm_w[:, 0:4:2, :], io["norm1_w"].rearrange("l (p k) -> p l k", p=P)),
            (norm_w[:, 1:4:2, :], io["norm2_w"].rearrange("l (p k) -> p l k", p=P)),
            (norm_w[:, 4, :], io["final_norm_w"].rearrange("(p k) -> p k", p=P)),
            (ada_b.rearrange("p l j k -> p (l j) k"), io["ada_b"].rearrange("l (j p k) -> p (l j) k", p=P, j=6)),
            (lbrow[0:HEADS], io["hgrn_lb_logits"].rearrange("i (h d) -> h i d", h=HEADS)),
            (gn_w, io["hgrn_gn_w"].rearrange("a d -> d a")),
            (router_w[:, 0], io["moe_w_router"][0].rearrange("(p k) e -> p k e", p=P)),
            (router_w[:, 1], io["moe_w_router"][1].rearrange("(p k) e -> p k e", p=P)),
            (router_b[:, 0], io["moe_router_bias"][0:1].broadcast_to((P, E))),
            (router_b[:, 1], io["moe_router_bias"][1:2].broadcast_to((P, E))),
        ]
        assert len(small) * 16 == SMALL

        @block.sync
        def _(sp):
            sp.dma_start(x_tok[:, 0, :], io["x_prompt"][0]).then_inc(s_x, 16)
            sp.dma_start(x_tok[:, 1, :], io["x_sample"][0]).then_inc(s_x, 16)
            for dst, src in small[0::2]:
                sp.dma_start(dst, src).then_inc(s_small, 16)

            def load_stage(n):
                sp.dma_start(stage[rooms[n]], stage_source(stages[n])).then_inc(stage_in[rooms[n]], 16)

            def load_gate_up(m, j, expert):
                for e in range(2):
                    for w, name in enumerate(("moe_w_gate", "moe_w_up")):
                        src = io[name][m][bass.ds(expert + e, 1)].rearrange("e (p k) f -> p (e k f)", p=P)
                        sp.dma_start(ring[:, j, 2 * e + w, :], src).then_inc(moe[m].gu_in[j], 16)

            def load_down(m, j, expert):
                for e in range(2):
                    src = io["moe_w_down"][m][bass.ds(expert + e, 1)].rearrange("e (c p) d -> p (e c) d", p=P)
                    dst = ring[:, j, 4 + e, :].rearrange("p (c d) -> p c d", c=2)
                    sp.dma_start(dst, src).then_inc(moe[m].dn_in[j], 16)

            def load_shared_gate_up(m):
                for w, name in enumerate(("shared_w_gate", "shared_w_up")):
                    sp.dma_start(ws_gu[:, :, w * F:(w + 1) * F],
                                 io[name][m].rearrange("(p k) f -> p k f", p=P)).then_inc(moe[m].sh_in, 16)

            def load_shared_down(m):
                sp.dma_start(ws_dn, io["shared_w_down"][m].rearrange("(c p) d -> p c d", p=P))\
                  .then_inc(moe[m].sh_in, 16)

            def stream_experts(m):
                with sp.Fori(1, PAIRS // 2) as h:
                    for j in range(2):
                        sp.wait_ge(moe[m].gu, h * 2 + (j - 1))
                        load_gate_up(m, j, h * 4 + 2 * j)
                        sp.wait_ge(moe[m].y_ps[1], h * 2 + (j - 1))
                        load_down(m, j, h * 4 + 2 * j)
                sp.wait_ge(moe[m].table, 1)
                more = sp.value_load(extra[0:1, 0:1].bitcast(I32), min_val=0, max_val=3)
                with sp.If(more > 0):
                    with sp.Fori(0, more) as r:
                        with sp.Fori(0, PAIRS // 2) as h:
                            for j in range(2):
                                sp.wait_ge(moe[m].gu, r * PAIRS + h * 2 + (PAIRS + j - 1))
                                load_gate_up(m, j, h * 4 + 2 * j)
                                sp.wait_ge(moe[m].y_ps[1], r * PAIRS + h * 2 + (PAIRS + j - 1))
                                load_down(m, j, h * 4 + 2 * j)
                return more

            for n in range(5):
                load_stage(n)
            sp.wait_ge(lb_ps, 1)
            for d, name in enumerate(("state_hgrn_fwd", "state_hgrn_bwd")):
                sp.dma_start(s0[:, d], io[name][0, 0].rearrange("h k v -> k h v")).then_inc(s_s0, 16)
            for n in range(5, stages0):
                sp.wait_ge(*block_used(n - 5))
                load_stage(n)
            for n in (stages0 - 5, stages0 - 4):
                sp.wait_ge(*block_used(n))
            sp.dma_start(late, io["hgrn_w_out"][0].rearrange("(h p) d -> p h d", p=P)).then_inc(late_in, 16)
            for n in range(stages0 - 3, stages0):
                sp.wait_ge(*block_used(n))
            load_gate_up(0, 0, 0)
            load_down(0, 0, 0)
            sp.wait_ge(late_half, 1)
            load_shared_gate_up(0)
            sp.wait_ge(out_ps, 4)
            load_shared_down(0)
            load_gate_up(0, 1, 2)
            load_down(0, 1, 2)
            more = stream_experts(0)

            sp.wait_ge(moe[0].sh_used, 1)
            load_stage(stages0)
            load_stage(stages0 + 1)
            sp.wait_ge(moe[0].gu, more * PAIRS + (PAIRS - 1))
            load_stage(stages0 + 2)
            load_stage(stages0 + 3)
            sp.wait_ge(moe[0].y_ps[1], more * PAIRS + (PAIRS - 1))
            load_stage(stages0 + 4)
            sp.wait_ge(moe[0].done, 1)
            sp.dma_start(ck, io["cache_na_k"][0, 0].rearrange("s h d -> s (h d)")).then_inc(cache_in, 16)
            sp.dma_start(cv, io["cache_na_v"][0, 0].rearrange("s h d -> s (h d)")).then_inc(cache_in, 16)
            rpb = io["na_rpb"]
            for r in range(2):
                for r2 in range(2):
                    at = rpb.offset + (r2 - r + WIN_R - 1) * (2 * WIN_C - 1) + WIN_C - 1 - (GRID_W - 1)
                    src = bass.AP(tensor=rpb.tensor, offset=at,
                                  ap=[[1, GRID_W], [(2 * WIN_R - 1) * (2 * WIN_C - 1), A_HEADS], [1, GRID_W]])
                    sp.dma_start(bias[GRID_W * r:GRID_W * (r + 1), :, GRID_W * r2:GRID_W * (r2 + 1)], src)\
                      .then_inc(bias_in, 16)
            sp.wait_ge(*block_used(stages0 + 1))
            sp.dma_start(late, io["na_w_o"][0].rearrange("(c p) d -> p c d", p=P)).then_inc(late_in, 16)
            sp.wait_ge(*block_used(stages0 + 2))
            load_stage(stages0 + 5)
            sp.wait_ge(*block_used(stages0 + 5))
            load_gate_up(1, 0, 0)
            load_down(1, 0, 0)
            sp.wait_ge(late_half, 2)
            load_shared_gate_up(1)
            sp.wait_ge(out_ps, 8)
            load_shared_down(1)
            sp.wait_ge(cache_out, 32)
            load_gate_up(1, 1, 2)
            load_down(1, 1, 2)
            stream_experts(1)
            sp.wait_ge(st_out, 16 * 4)
            sp.wait_ge(cache_out, 32)
            sp.wait_ge(y_out, 32)

        @block.gpsimd
        def _(pool):
            pool.memset(ones, 1.0).then_inc(ready, 1)
            pool.memset(eps, EPS).then_inc(ready, 1)
            pool.memset(cond_act, 0.0).then_inc(ready, 1)
            pool.memset(scan_keep, 1.0).then_inc(ready, 1)
            pool.wait_ge(ready, 4)
            pool.memset(scan_keep.rearrange("p (u t) -> p u t", t=T)[:, :, 0:1], 0.0).then_inc(ready, 1)
            for M in moe:
                for part, before_it, after_it in ((0, M.htok, M.h_rest), (1, M.h_mid, M.h_low)):
                    for n in range(4):
                        pool.wait_ge(before_it, n + 1)
                        if part:
                            pool.wait_ge(M.h_rest, n + 1)
                        a, ks = n // 2, slice(4 * (n % 2), 4 * (n % 2) + 4)
                        out = h_tok[:, 2, a, ks] if part else h_rest[:, a, ks]
                        pool.tensor_tensor(out, h_rest[:, a, ks], h_tok[:, part, a, ks], ALU.subtract)\
                            .then_inc(after_it, 1)

        @block.scalar
        def _(act):
            act.dma_start(consts, io["table"]).then_inc(s_const, 16)
            for dst, src in small[1::2]:
                act.dma_start(dst, src).then_inc(s_small, 16)

            def copy(out, in_, **kw):
                return act.activation(out, in_, ACT.Copy, **kw)

            def squares():
                act.activation(sq[:, 0:4], xT[:, 0:4], ACT.Square).then_inc(sq_done, 1)

            def norm_root(n):
                act.wait_ge(ssum, n + 1)
                act.activation(rstd, psum[:, 4, 0:NT], ACT.Sqrt, scale=1.0 / D, bias=eps).then_inc(root, 1)

            def norm(n, shift):
                act.wait_ge(x_normed, 2 * n + 1)
                act.wait_ge(gains, 1 if n == 0 else 2)
                for k in range(4):
                    for s in range(2):
                        part = hT[:, k, s * T:(s + 1) * T]
                        if shift is None:
                            ins = copy(part, part, scale=norm_w[:, 4, k:k + 1])
                        else:
                            ins = act.activation(part, part, ACT.Identity, scale=gain[:, n, k, s:s + 1],
                                                 bias=shift[:, k, s:s + 1])
                ins.then_inc(h_done, 1)

            def ada_rows(n):
                act.wait_ge(ada_ps, n + 1)
                if n % 2 == 0 and n >= 2:
                    act.wait_ge(sel_ps, n // 2)
                copy(mrow[:, (n % 2) * BLOCK:(n % 2 + 1) * BLOCK], psum[:, 7, :]).then_inc(ada_row, 1)

            act.wait_ge(s_small, SMALL)
            act.wait_ge(ready, 5)
            act.activation(cond_act[:, :, 0:2], cond.rearrange("p s k -> p k s"), ACT.Silu).then_inc(cond_done, 1)
            for n in (0, 2):
                act.wait_ge(x_ps, n + 1)
                copy(xT[:, 2 * n:2 * n + 4, 0:T], psum[:, n, :].rearrange("p (k t) -> p k t", t=T)).then_inc(x_sb, 1)
            act.wait_ge(x_sb, 4)
            squares()
            act.wait_ge(lb_shift, 1)
            act.activation(lb, lb, ACT.Exp).then_inc(lb_exp, 1)
            norm_root(0)
            for n in range(4):
                ada_rows(n)
            norm(0, mod[:, 0, 0])

            def project(b):
                g, kind = b // 5, KINDS[b % 5]
                dst = {"f_fw": kk[0], "f_bw": kk[1], "gate": gate, "q": q, "v": None}[kind]
                if dst is None:
                    return
                act.wait_ge(proj, b + 1)
                dst = dst[:, GROUP * g:GROUP * (g + 1)].rearrange("p h t -> p (h t)")
                ins = act.activation(dst, bank(2 * (b % 2), 2), ACT.Copy if kind == "q" else ACT.Sigmoid)
                ins.then_inc(gate_sig if kind == "gate" else unit_free[b % 2], 1)

            def decay_exps(g, n):
                for d in range(2):
                    c = 8 * g + 2 * n + d
                    act.wait_ge(dif_done, c + 1)
                    if c >= 2:
                        act.wait_ge(qk_used, c - 1)
                    if n < 2:
                        H = 64 >> n
                        vq, vk, vd = (a.rearrange("p u (b t) -> p (u b) t", t=2 * H) for a in (Q[d], Kd[d], dif[d]))
                        early, behind = slice(0, H), slice(H, 2 * H)
                        qs, ks = (behind, early) if d == 0 else (early, behind)
                        act.activation(vq[:, :, qs], vd[:, :, qs], ACT.Exp)
                        ins = act.activation(vk[:, :, ks], vd[:, :, ks], ACT.Exp, scale=-1.0)
                    elif n == 2:
                        act.activation(Q[d], dif[d], ACT.Exp)
                        ins = act.activation(Kd[d], dif[d], ACT.Exp, scale=-1.0)
                    else:
                        act.activation(Q[d][:, 0:GROUP], bb[d][:, GROUP * g:GROUP * (g + 1), T:NT], ACT.Exp)
                        ins = act.activation(Kd[d][:, 0:GROUP], dif[d][:, 0:GROUP], ACT.Exp, scale=-1.0)
                    ins.then_inc(exp_done, 1)

            def keys_turned(g, d):
                act.wait_ge(kd_ps, 2 * g + d + 1)
                copy(Kd[d][:, GROUP:UNITS].rearrange("p u t -> p (u t)"), psum[:, 6, :]).then_inc(kd_sb, 1)

            def state_out(g, d):
                act.wait_ge(st_ps, 2 * g + d + 1)
                copy(Q[d][:, GROUP:UNITS].rearrange("p u t -> p (u t)"), psum[:, 6, :]).then_inc(st_sb, 1)
                act.wait_ge(st_sb, 2 * g + d + 1)
                dst = io["out_state_fwd" if d == 0 else "out_state_bwd"][0, 0, GROUP * g:GROUP * (g + 1)]
                act.dma_start(dst.rearrange("h k v -> k h v"), Q[d][:, GROUP:UNITS]).then_inc(st_out, 16)

            def recur(g, item):
                if item == 0:
                    for d in range(2):
                        act.wait_ge(f_done, 2 * g + d + 1)
                        if g:
                            act.wait_ge(o_done if d == 0 else pv_done, g)
                        act.activation(dif[d].rearrange("p u t -> p (u t)"),
                                       bb[d][:, GROUP * g:GROUP * (g + 1)].rearrange("p h t -> p (h t)"),
                                       ACT.Ln).then_inc(ln_done, 1)
                    if g:
                        act.wait_ge(st_out, 32 * g)
                if item <= 3:
                    decay_exps(g, item)
                elif item == 4:
                    act.wait_ge(o_copied, g + 1)
                    act.activation(dif[0], heads(oT, g), ACT.Square).then_inc(o_sq, 1)
                    keys_turned(g, 0)
                elif item == 5:
                    act.wait_ge(o_ssum, g + 1)
                    act.activation(dif[0].rearrange("p u t -> p (u t)"), bank(4, 2), ACT.Ln, scale=1.0 / DV,
                                   bias=eps).then_inc(act_c, 1)
                    act.wait_ge(act_c, g + 1)
                    act.activation(dif[0], dif[0], ACT.Exp, scale=-0.5).then_inc(o_rstd, 1)
                    state_out(g, 0)
                elif item == 6:
                    keys_turned(g, 1)
                elif item == 7:
                    state_out(g, 1)

            for b, items, _, adas in ada_rounds():
                for g, item in items:
                    recur(g, item)
                if b is not None:
                    project(b)
                for n in adas:
                    ada_rows(n)

            def experts_front(m):
                M = moe[m]
                act.wait_ge(resid, 2 * m + 1)
                squares()
                norm_root(2 * m + 1)
                norm(2 * m + 1, mod[:, m, 3])
                act.wait_ge(M.logits, 1)
                act.activation(route[:, 0], psum[:, 5, 0:2 * E].rearrange("p (a e) -> p a e", a=2), ACT.Sigmoid)\
                   .then_inc(M.scores, 1)
                for n in range(4):
                    act.wait_ge(M.htok_ps, n + 1)
                    a, ks = n // 2, slice(4 * (n % 2), 4 * (n % 2) + 4)
                    rows = psum[:, 6 + n % 2, :].rearrange("p (k t) -> p k t", t=P)
                    copy(h_rest[:, a, ks], rows)
                    copy(h_tok[:, 0, a, ks], rows).then_inc(M.htok, 1)
                for n in range(4):
                    a, ks = n // 2, slice(4 * (n % 2), 4 * (n % 2) + 4)
                    act.wait_ge(M.h_rest, n + 1)
                    copy(h_tok[:, 1, a, ks], h_rest[:, a, ks]).then_inc(M.h_mid, 1)
                for a in range(2):
                    act.wait_ge(M.sh_ps, a + 1)
                    act.activation(sh_silu[:, a], psum[:, 6 + a, 0:F], ACT.Silu).then_inc(M.sh_silu, 1)
                act.wait_ge(M.t_ps, 1)
                copy(sh_hidT, psum[:, 4, :].rearrange("p (c t) -> p c t", c=2)).then_inc(M.t_sb, 1)

            def gathered(M, g, j):
                act.wait_ge(M.xg_ps[0], g + 1)
                copy(xg[:, j, 0:4], psum[:, 6, :].rearrange("p (k t) -> p k t", t=P)).then_inc(M.xg[0], 1)

            def hots_turned(M, g, j):
                act.wait_ge(M.hot_ps, g + 1)
                copy(onehot_t[:, j].rearrange("p a t -> p (a t)"), psum[:, 5, 0:NT])
                for e in range(2):
                    at = slice(SLOTS * e, SLOTS * (e + 1))
                    ins = copy(slot_parts[at, j], psum[at, 5, NT + 3 * e:NT + 3 * (e + 1)],
                               accum_out=slot_w[at, j:j + 1])
                ins.then_inc(M.hot_t, 1)

            def experts_pass(M, r):
                gathered(M, r * (PAIRS + 1), 0)
                hots_turned(M, r * (PAIRS + 1), 0)
                with act.Fori(0, PAIRS // 2) as h:
                    for j in range(2):
                        n, g = r * PAIRS + h * 2 + j, r * (PAIRS + 1) + h * 2 + j
                        act.wait_ge(M.gu, n + 1)
                        act.activation(silu[:, j], psum[:, 4, 0:F], ACT.Silu).then_inc(M.silu, 1)
                        gathered(M, g + 1, 1 - j)
                        act.wait_ge(M.t_ps, n + 2)
                        copy(hidT[:, j].rearrange("p c t -> p (c t)"), psum[:, 5, 0:2 * P]).then_inc(M.t_sb, 1)
                        hots_turned(M, g + 1, 1 - j)
                        for half in range(2):
                            act.wait_ge(M.y_ps[half], n + 1)
                            copy(y[:, j, 0, :, half * (P // 2):(half + 1) * (P // 2)].rearrange("s k p -> s p k"),
                                 psum[:, 6 + half, :].rearrange("s (p k) -> s p k", k=K)).then_inc(M.y_high, 1)
                        act.wait_ge(M.y_rest, n * 2 + 4)
                        copy(y[:, j, 1], y_rest).then_inc(M.y_mid, 1)

            def experts(m):
                experts_pass(moe[m], 0)
                act.wait_ge(moe[m].table, 1)
                more = act.value_load(extra[0:1, 0:1].bitcast(I32), min_val=0, max_val=3)
                with act.If(more > 0):
                    with act.Fori(0, more) as r:
                        experts_pass(moe[m], r + 1)

            act.wait_ge(st_out, 64)
            experts_front(0)
            experts(0)

            act.wait_ge(resid, 2)
            squares()
            norm_root(2)
            norm(2, mod[:, 1, 0])
            for n in (0, 1):
                act.wait_ge(proj, 10 + n + 1)
                copy(qT[:, 4 * n:4 * n + 4].rearrange("p k t -> p (k t)"), bank(2 * (n % 2), 2), scale=HD ** -0.5)\
                    .then_inc(unit_free[n % 2], 1)
            for n in range(2):
                act.wait_ge(tr_ps, n + 1)
                copy(ckT[:, 4 * n:4 * n + 4], psum[:, 4 + n, :].rearrange("p (k t) -> p k t", t=P)).then_inc(tr_sb, 1)
            for n in (4, 5):
                act.wait_ge(proj, 10 + n + 1)
                copy(va[:, :, (n - 4) * BLOCK:(n - 3) * BLOCK], psum[:, 2 * (n % 2):2 * (n % 2) + 2, :])\
                    .then_inc(unit_free[n % 2], 1)
            for n in range(2):
                act.wait_ge(tr_ps, n + 3)
                copy(kout[:, 4 * n:4 * n + 4], psum[:, 4 + n, :].rearrange("p (k t) -> p k t", t=P)).then_inc(tr_sb, 1)
            act.wait_ge(tr_sb, 4)
            act.dma_start(io["out_cache_k"][0, 0].rearrange("s h d -> s (h d)"), kout.rearrange("p k t -> p (k t)"))\
               .then_inc(cache_out, 16)
            act.wait_ge(unit_free[0], 8)
            act.wait_ge(unit_free[1], 8)
            act.dma_start(io["out_cache_v"][0, 0].rearrange("s h d -> s (h d)"), va[:, 0]).then_inc(cache_out, 16)
            def heads_out(g):
                act.wait_ge(oa_ps, g + 1)
                copy(oTa[:, 2 * g:2 * g + 2].rearrange("p k t -> p (k t)"), psum[:, 3, :]).then_inc(oa_sb, 1)

            for g in range(4):
                j = g % 2
                act.wait_ge(sc_sb, g + 1)
                for n in range(4):
                    act.activation(S_lat[:, j, n], S_lat[:, j, n], ACT.Exp, bias=neg_max[:, j, n:n + 1],
                                   accum_out=row_sum[:, j, n:n + 1])
                for n in range(4):
                    ins = act.activation(S_pr[:, j, n], psum[:, 6 + n // 2, (n % 2) * P:(n % 2 + 1) * P], ACT.Exp,
                                         bias=neg_max[:, j, 4 + n:5 + n], accum_out=row_sum[:, j, 4 + n:5 + n])
                ins.then_inc(p_exp, 1)
                if g:
                    heads_out(g - 1)
            heads_out(3)

            act.wait_ge(cache_out, 32)
            experts_front(1)
            experts(1)

            act.wait_ge(resid, 4)
            squares()
            norm_root(4)
            norm(4, None)
            for n in (0, 2):
                act.wait_ge(yt_ps, n + 1)
                copy(y_tok[:, n // 2, :, 0:4].rearrange("s p k -> s k p"),
                     psum[:, n, :].rearrange("s (k p) -> s k p", p=P)).then_inc(yt_sb, 1)
            act.wait_ge(yt_sb, 4)
            for a, name in enumerate(("out_prompt", "out_sample")):
                act.dma_start(io[name][0], y_tok[:, a].rearrange("s p k -> s (p k)")).then_inc(y_out, 16)

        @block.vector
        def _(dve):
            n_c = [0]

            def mark(ins):
                n_c[0] += 1
                ins.then_inc(dve_c, 1)

            def done():
                dve.wait_ge(dve_c, n_c[0])

            def link(ins):
                mark(ins)
                done()

            def squares(n):
                if n:
                    dve.wait_ge(resid, n)
                dve.tensor_tensor(sq[:, 4:8], xT[:, 4:8], xT[:, 4:8], ALU.mult).then_inc(sq_done, 1)

            def normed(n):
                dve.wait_ge(root, n + 1)
                link(dve.reciprocal(rstd, rstd))
                for ks in (slice(0, 4), slice(4, 8)):
                    dve.tensor_tensor(hT[:, ks], xT[:, ks], rstd.unsqueeze(1).broadcast_to((P, 4, NT)), ALU.mult)\
                       .then_inc(x_normed, 1)

            def norm(n, shift):
                dve.wait_ge(x_normed, 2 * n + 2)
                for k in range(4, K):
                    for s in range(2):
                        part = hT[:, k, s * T:(s + 1) * T]
                        if shift is None:
                            ins = dve.tensor_scalar(part, part, norm_w[:, 4, k:k + 1], None, ALU.mult)
                        else:
                            ins = dve.tensor_scalar(part, part, gain[:, n, k, s:s + 1], shift[:, k, s:s + 1],
                                                    ALU.mult, ALU.add)
                ins.then_inc(h_done, 1)

            def modulation(n):
                l, j = parts[n]
                dve.wait_ge(sel_ps, n + 1)
                dve.tensor_tensor(mod[:, l, j], psum[:, 7, 0:2 * K].rearrange("p (k s) -> p k s", s=2),
                                  ada_b[:, l, j].unsqueeze(2).broadcast_to((P, K, 2)), ALU.add).then_inc(mod_done, 1)
                if j in (1, 4):
                    m = 2 * l + j // 4
                    dve.wait_ge(mod_done, n + 1)
                    link(dve.scalar_tensor_tensor(out=gain[:, m], in0=mod[:, l, j], scalar=1.0,
                                                  in1=norm_w[:, m].unsqueeze(2).broadcast_to((P, K, 2)),
                                                  op0=ALU.add, op1=ALU.mult))

            def gains_ready(m):
                dve.wait_ge(dve_c, n_c[0])
                dve.sem_inc(gains, 1)

            def residual(g, src):
                for k in range(K):
                    src(k)
                    for s in range(2):
                        at = slice(s * T, (s + 1) * T)
                        ins = dve.scalar_tensor_tensor(
                            out=xT[:, k, at], in0=psum[:, k // 2, (k % 2) * NT + s * T:(k % 2) * NT + (s + 1) * T],
                            scalar=g[:, k, s:s + 1], in1=xT[:, k, at], op0=ALU.mult, op1=ALU.add)
                ins.then_inc(resid, 1)

            dve.memset(rank, -1.0)
            dve.memset(comb, 0.0)
            dve.wait_ge(s_const, 16)
            link(dve.tensor_copy(ident_b, ident))
            for n in (1, 3):
                dve.wait_ge(x_ps, n + 1)
                dve.tensor_copy(xT[:, 2 * (n - 1):2 * (n - 1) + 4, T:NT],
                                psum[:, n, :].rearrange("p (k t) -> p k t", t=T)).then_inc(x_sb, 1)
            dve.wait_ge(x_sb, 4)
            squares(0)
            dve.wait_ge(s_small, SMALL)
            dve.wait_ge(lb_ps, 1)
            link(dve.tensor_copy(lb, psum[:, 5, 0:3 * HEADS].rearrange("p (i h) -> p i h", i=3)))
            link(dve.tensor_tensor(lb_t, lb[:, 0], lb[:, 1], ALU.max))
            link(dve.tensor_tensor(lb_t, lb_t, lb[:, 2], ALU.max))
            dve.tensor_tensor(lb, lb, lb_t.unsqueeze(1).broadcast_to((P, 3, HEADS)), ALU.subtract).then_inc(lb_shift, 1)
            dve.wait_ge(lb_exp, 1)
            link(dve.tensor_tensor(lb_t, lb[:, 0], lb[:, 1], ALU.add))
            link(dve.tensor_tensor(lb_t, lb_t, lb[:, 2], ALU.add))
            link(dve.reciprocal(lb_t, lb_t))
            link(dve.tensor_tensor(lb0, lb[:, 0], lb_t, ALU.mult))
            link(dve.tensor_scalar(one_minus_lb, lb0, -1.0, 1.0, ALU.mult, ALU.add))
            normed(0)
            modulation(0)
            modulation(1)
            gains_ready(0)
            norm(0, mod[:, 0, 0])

            def project(b):
                g, kind = b // 5, KINDS[b % 5]
                if kind == "gate":
                    dve.wait_ge(gate_sig, g + 1)
                    part = gate[:, GROUP * g:GROUP * (g + 1)].rearrange("p h t -> p (h t)")
                    dve.tensor_tensor(part, part, bank(2 * (b % 2), 2), ALU.mult).then_inc(unit_free[b % 2], 1)
                elif kind == "v":
                    dve.wait_ge(proj, b + 1)
                    dve.tensor_copy(v[:, :, g * BLOCK:(g + 1) * BLOCK], psum[:, 2 * (b % 2):2 * (b % 2) + 2, :])\
                       .then_inc(unit_free[b % 2], 1)

            def decay(g):
                for d in range(2):
                    dve.wait_ge(unit_free[(5 * g + d) % 2], (5 * g + d) // 2 + 1)
                    for h in range(GROUP * g, GROUP * (g + 1)):
                        mark(dve.tensor_scalar(bb[d][:, h], kk[d][:, h], one_minus_lb[:, h:h + 1], lb0[:, h:h + 1],
                                               ALU.mult, ALU.add))
                    done()
                    part = slice(GROUP * g, GROUP * (g + 1))
                    dve.tensor_scalar(kk[d][:, part], bb[d][:, part], -1.0, 1.0, ALU.mult, ALU.add)\
                       .then_inc(f_done, 1)
                for d in range(2):
                    dve.wait_ge(ln_done, 2 * g + d + 1)
                    out = bb[d][:, GROUP * g:GROUP * (g + 1)].rearrange("p h t -> p (h t)")
                    logs = dif[d].rearrange("p u t -> p (u t)")
                    if d:
                        out, logs = out[:, ::-1], logs[:, ::-1]
                    mark(dve.tensor_tensor_scan(out, scan_keep, logs, 0.0, ALU.mult, ALU.add))
                done()

            def decays(g, n):
                for d in range(2):
                    c = 8 * g + 2 * n + d
                    if n:
                        dve.wait_ge(exp_done, c - 1)
                    B = heads(bb[d], g)
                    if n < 3:
                        size = (128, 64, 32)[n]
                        at = size // 2 - (d == 0)
                        view = B.rearrange("p u (b t) -> p (u b) t", t=size)
                        shape = (P, UNITS * (T // size), size)
                        ins = dve.tensor_tensor(dif[d].rearrange("p u (b t) -> p (u b) t", t=size), view,
                                                view[:, :, at:at + 1].broadcast_to(shape), ALU.subtract)
                    else:
                        view = bb[d][:, GROUP * g:GROUP * (g + 1), 0:T]
                        at = T - 1 if d == 0 else 0
                        ins = dve.tensor_tensor(dif[d][:, 0:GROUP], view,
                                                view[:, :, at:at + 1].broadcast_to((P, GROUP, T)), ALU.subtract)
                    ins.then_inc(dif_done, 1)
                if n == 0:
                    dve.wait_ge(unit_free[(5 * g + 2) % 2], (5 * g + 2) // 2 + 1)
                for d in range(2):
                    dve.wait_ge(exp_done, 8 * g + 2 * n + d + 1)
                    if n < 2:
                        H = 64 >> n
                        vq, vk, vqq, vkk = (a.rearrange("p u (b t) -> p (u b) t", t=2 * H)
                                            for a in (Q[d], Kd[d], heads(q, g), heads(kk[d], g)))
                        early, behind = slice(0, H), slice(H, 2 * H)
                        qs, ks = (behind, early) if d == 0 else (early, behind)
                        dve.tensor_tensor(vq[:, :, qs], vq[:, :, qs], vqq[:, :, qs], ALU.mult)
                        ins = dve.tensor_tensor(vk[:, :, ks], vk[:, :, ks], vkk[:, :, ks], ALU.mult)
                    elif n == 2:
                        dve.tensor_tensor(Q[d], Q[d], heads(q, g), ALU.mult)
                        ins = dve.tensor_tensor(Kd[d], Kd[d], heads(kk[d], g), ALU.mult)
                    else:
                        part = slice(GROUP * g, GROUP * (g + 1))
                        dve.tensor_tensor(Q[d][:, 0:GROUP], Q[d][:, 0:GROUP], q[:, part, T:NT], ALU.mult)
                        ins = dve.tensor_tensor(Kd[d][:, 0:GROUP], Kd[d][:, 0:GROUP], kk[d][:, part, 0:T], ALU.mult)
                    ins.then_inc(qk_done, 1)

            def recur(g, item):
                if item == 0:
                    decay(g)
                if item <= 3:
                    decays(g, item)
                if item == 3:
                    dve.wait_ge(qk_used, 8 * g + 6)
                    mark(dve.tensor_tensor(AT, psum[:, 4:6, :].rearrange("p b (u t) -> p (b u) t", t=T),
                                           mask_f.unsqueeze(1).broadcast_to((P, UNITS, T)), ALU.mult))
                    mark(dve.tensor_tensor(fb_sb, psum[:, 6, 0:UNITS * 32].rearrange("p (u t) -> p u t", t=32),
                                           mask_b.unsqueeze(1).broadcast_to((P, UNITS, 32)), ALU.mult))
                    done()
                    for i in range(4):
                        at = slice(32 * i, 32 * i + 32)
                        ins = dve.tensor_tensor(AT[at, :, at], AT[at, :, at], fb_sb[at], ALU.add)
                    ins.then_inc(at_done, 1)
                elif item == 4:
                    dve.wait_ge(pv_done, g + 1)
                    dve.tensor_copy(heads(oT, g), psum[:, 4:6, :].rearrange("p b (u t) -> p (b u) t", t=T))\
                       .then_inc(o_copied, 1)
                elif item == 5:
                    dve.wait_ge(o_rstd, g + 1)
                    part = oT[:, GROUP * g:GROUP * (g + 1)].rearrange("p h t -> p (h t)")
                    link(dve.scalar_tensor_tensor(out=part, in0=part, scalar=gn_w[:, 0:1],
                                                  in1=dif[0].rearrange("p u t -> p (u t)"), op0=ALU.mult, op1=ALU.mult))
                    dve.tensor_tensor(part, part, gate[:, GROUP * g:GROUP * (g + 1)].rearrange("p h t -> p (h t)"),
                                      ALU.mult).then_inc(o_done, 1)

            finished = 2
            for b, items, part, _ in ada_rounds():
                if part == finished:
                    modulation(part)
                    finished += 1
                for g, item in items:
                    recur(g, item)
                if b is not None:
                    project(b)
            assert finished == len(parts)
            gains_ready(1)

            def mixer_bank(m):
                def wait(k):
                    if k % 2 == 0:
                        dve.wait_ge(out_ps, 4 * m + k // 2 + 1)
                return wait

            residual(mod[:, 0, 2], mixer_bank(0))

            def top(values, pads, keep, out):
                for a in range(2):
                    best = best8[:, a]
                    link(dve.max(best, values[:, a, 0:values.shape[2] - pads]))
                    link(dve.memset(best[:, keep:8], 2 * LOW))
                    mark(dve.match_replace(out[:, a], best, values[:, a], 3 * LOW))
                done()

            scores, selv, t2, t3, mask = (route[:, n] for n in range(5))
            small16 = route[:, 5].rearrange("p a e -> p (a e)")
            m1, cnt, m2, c2 = (small16[:, 16 * n:16 * (n + 1)] for n in range(4))
            best8 = small16[:, 64:80].rearrange("p (a e) -> p a e", a=2)
            gs = route[:, 6].rearrange("p a e -> p (a e)")[:, 0:24].rearrange("p (a e) -> p a e", a=2)
            gs_o = route[:, 6].rearrange("p a e -> p (a e)")[:, 32:56].rearrange("p (a e) -> p a e", a=2)
            gmask = small16[:, 80:96].rearrange("p (a g) -> p a g", a=2)
            wsum = small16[:, 96:98]
            t1 = small16[:, 98:99]
            wide = route[:, 7:11].rearrange("p n a e -> p (n a e)")
            cand = wide[:, 0:2 * (E + 2)].rearrange("p (a e) -> p a e", a=2)
            cand_o = wide[:, 2 * (E + 2):4 * (E + 2)].rearrange("p (a e) -> p a e", a=2)

            def experts_front(m):
                M = moe[m]
                dve.memset(y[:, 1], 0.0).then_inc(M.y_low, 1)
                dve.sem_inc(M.y_rest, 2)
                squares(2 * m + 1)
                normed(2 * m + 1)
                norm(2 * m + 1, mod[:, m, 3])
                link(dve.memset(gs, 2 * LOW))
                link(dve.memset(cand, 2 * LOW))
                dve.wait_ge(M.scores, 1)
                link(dve.tensor_tensor(selv, scores, router_b[:, m].unsqueeze(1).broadcast_to((P, 2, E)), ALU.add))

                def groups(a):
                    return a.rearrange("p a (g e) -> p (a g) e", g=GROUPS)

                link(dve.tensor_reduce(m1, groups(selv), AX.X, ALU.max))
                link(dve.tensor_tensor(groups(t2), groups(selv), m1.unsqueeze(2).broadcast_to((P, 16, 8)), ALU.is_equal))
                mark(dve.tensor_reduce(cnt, groups(t2), AX.X, ALU.add))
                link(dve.scalar_tensor_tensor(out=t3, in0=t2, scalar=LOW, in1=selv, op0=ALU.mult, op1=ALU.add))
                mark(dve.tensor_reduce(m2, groups(t3), AX.X, ALU.max))
                link(dve.tensor_scalar(c2, cnt, 1.5, LOW, ALU.is_lt, ALU.mult))
                link(dve.tensor_tensor(c2, c2, m1, ALU.add))
                link(dve.tensor_tensor(m2, m2, c2, ALU.max))
                link(dve.tensor_tensor(gs[:, :, 0:GROUPS], m1.rearrange("p (a g) -> p a g", a=2),
                                       m2.rearrange("p (a g) -> p a g", a=2), ALU.add))
                top(gs, 4, TOP_GROUPS, gs_o)
                link(dve.tensor_tensor(gmask, gs_o[:, :, 0:GROUPS], gs[:, :, 0:GROUPS], ALU.not_equal))
                link(dve.tensor_scalar(gmask, gmask, -1.0, -LOW, ALU.add, ALU.mult))
                for a in range(2):
                    mark(dve.tensor_tensor(cand[:, a, 0:E].rearrange("p (g e) -> p g e", g=GROUPS),
                                           selv[:, a].rearrange("p (g e) -> p g e", g=GROUPS),
                                           gmask[:, a].unsqueeze(2).broadcast_to((P, GROUPS, E // GROUPS)), ALU.add))
                done()
                top(cand, 2, TOP_K, cand_o)
                dve.tensor_tensor(mask, cand_o[:, :, 0:E], cand[:, :, 0:E], ALU.not_equal).then_inc(M.mask, 1)
                dve.wait_ge(M.mask, 1)
                link(dve.tensor_tensor(t2, scores, mask, ALU.mult))
                link(dve.tensor_reduce(wsum, t2, AX.X, ALU.add))
                link(dve.reciprocal(wsum, wsum))
                for a in range(2):
                    mark(dve.tensor_scalar(t2[:, a], t2[:, a], wsum[:, a:a + 1], ROUTED_SCALE, ALU.mult, ALU.mult))
                done()
                dve.wait_ge(M.rank_ps, 1)
                link(dve.scalar_tensor_tensor(out=t3, in0=psum[:, 5, 0:2 * E].rearrange("p (a e) -> p a e", a=2),
                                              scalar=1.0, in1=mask, op0=ALU.add, op1=ALU.mult))
                mark(dve.tensor_scalar(rank[:, :, 0:E], t3, -1.0, None, ALU.add))
                link(dve.tensor_reduce(t1, psum[:, 5, 2 * E:3 * E], AX.X, ALU.max))
                link(dve.tensor_scalar(wsum[:, 0:1], t1, float(SLOTS), None, ALU.is_gt))
                link(dve.scalar_tensor_tensor(out=wsum[:, 1:2], in0=t1, scalar=2.0 * SLOTS, in1=wsum[:, 0:1],
                                              op0=ALU.is_gt, op1=ALU.add))
                dve.scalar_tensor_tensor(out=extra.bitcast(I32), in0=t1, scalar=3.0 * SLOTS, in1=wsum[:, 1:2],
                                         op0=ALU.is_gt, op1=ALU.add).then_inc(M.table, 1)
                for i in range(3):
                    link(dve.tensor_copy(comb[:, :, 0:E, i], t2))
                    if i < 2:
                        link(dve.tensor_tensor(t2, t2, comb[:, :, 0:E, i], ALU.subtract))
                for a in range(2):
                    dve.wait_ge(M.sh_silu, a + 1)
                    dve.tensor_tensor(sh_hid[:, a], sh_silu[:, a], psum[:, 6 + a, F:2 * F], ALU.mult)\
                       .then_inc(M.hid if a else M.sh_hid, 1)

            def one_hots(r, expert, j):
                base = C_IOTA + r * SLOTS
                shape = (P, 2, 2, SLOTS)
                slots = (consts[:, base:base + SLOTS] if isinstance(base, int) else consts[:, bass.ds(base, SLOTS)])
                ranks = rank[:, :, bass.ds(expert, 2)] if not isinstance(expert, int) else rank[:, :, expert:expert + 2]
                return dve.tensor_tensor(onehot[:, j].rearrange("p a (e s) -> p a e s", e=2),
                                         slots.unsqueeze(1).unsqueeze(1).broadcast_to(shape),
                                         ranks.unsqueeze(3).broadcast_to(shape), ALU.is_equal)

            def gathered(M, g, j):
                dve.wait_ge(M.xg_ps[1], g + 1)
                dve.tensor_copy(xg[:, j, 4:8], psum[:, 7, :].rearrange("p (k t) -> p k t", t=P)).then_inc(M.xg[1], 1)

            def experts_pass(M, r):
                first = r * (PAIRS + 1)
                if not isinstance(r, int):
                    dve.wait_ge(M.comb, first)
                dve.memset(onehot_t[:, 1], 0.0).then_inc(M.c_zero, 1)
                one_hots(r, 0, 0).then_inc(M.onehot, 1)
                gathered(M, first, 0)
                with dve.Fori(0, PAIRS // 2) as h:
                    for j in range(2):
                        n, g = r * PAIRS + h * 2 + j, r * (PAIRS + 1) + h * 2 + j
                        one_hots(r, h * 4 + 2 * (j + 1), 1 - j).then_inc(M.onehot, 1)
                        dve.wait_ge(M.silu, n + 1)
                        dve.wait_ge(M.hot_t, g + 1)
                        dve.scalar_tensor_tensor(out=hid[:, j], in0=silu[:, j], scalar=slot_w[:, j:j + 1],
                                                 in1=psum[:, 4, F:2 * F], op0=ALU.mult, op1=ALU.mult)\
                           .then_inc(M.hid, 1)
                        gathered(M, g + 1, 1 - j)
                        for half in range(2):
                            dve.wait_ge(M.y_high, n * 2 + (half + 1))
                            ps = slice(half * (P // 2), (half + 1) * (P // 2))
                            dve.tensor_tensor(y_rest[:, :, ps].rearrange("s k p -> s p k"),
                                              psum[:, 6 + half, :].rearrange("s (p k) -> s p k", k=K),
                                              y[:, j, 0, :, ps].rearrange("s k p -> s p k"), ALU.subtract)\
                               .then_inc(M.y_rest, 1)
                        dve.wait_ge(M.y_rest, n * 2 + 4)
                        dve.wait_ge(M.y_mid, n + 1)
                        dve.tensor_tensor(y[:, j, 2], y_rest, y[:, j, 1], ALU.subtract).then_inc(M.y_low, 1)

            def experts(m):
                M = moe[m]
                dve.wait_ge(M.table, 1)
                experts_pass(M, 0)
                more = dve.value_load(extra[0:1, 0:1].bitcast(I32), min_val=0, max_val=3)
                with dve.If(more > 0):
                    with dve.Fori(0, more) as r:
                        experts_pass(M, r + 1)
                dve.wait_ge(M.done, 1)
                residual(mod[:, m, 5], lambda k: None)

            dve.wait_ge(st_out, 64)
            experts_front(0)
            experts(0)

            squares(2)
            normed(2)
            norm(2, mod[:, 1, 0])
            for n in range(4):
                dve.wait_ge(bias_ps, n + 1)
                dve.tensor_tensor(bias[:, 4 * n:4 * n + 4], psum[:, 6 + n % 2, :].rearrange("p (h s) -> p h s", s=P),
                                  window.unsqueeze(1).broadcast_to((P, 4, P)), ALU.mult).then_inc(bias_done, 1)
            dve.wait_ge(bias_done, 4)
            link(dve.tensor_tensor(bias, bias, window_neg.unsqueeze(1).broadcast_to((P, A_HEADS, P)), ALU.add))
            for n in (2, 3):
                dve.wait_ge(proj, 10 + n + 1)
                dve.tensor_copy(kT[:, 4 * (n - 2):4 * (n - 2) + 4].rearrange("p k t -> p (k t)"), bank(2 * (n % 2), 2))\
                   .then_inc(unit_free[n % 2], 1)
            def probs_turned(g):
                dve.wait_ge(pt_ps, g + 1)
                dve.tensor_copy(PT.rearrange("p n t -> p (n t)"), bank(0, 3)).then_inc(pt_sb, 1)

            for g in range(4):
                j = g % 2
                dve.wait_ge(sc_ps, g + 1)
                for par in range(2):
                    lat = psum[:, 4 + par, :].rearrange("p (i n) -> p i n", i=2)
                    mark(dve.tensor_tensor(S_lat[:, j, 2 * par:2 * par + 2, 0:P], lat[:, :, 0:P],
                                           bias[:, 4 * g + par:4 * g + 4:2, :], ALU.add))
                    mark(dve.tensor_copy(S_lat[:, j, 2 * par:2 * par + 2, P:2 * P], lat[:, :, P:2 * P]))
                    mark(dve.tensor_reduce(neg_max[:, j, 4 + 2 * par:6 + 2 * par],
                                           psum[:, 6 + par, 0:2 * P].rearrange("p (i n) -> p i n", i=2), AX.X, ALU.max,
                                           negate=True))
                done()
                dve.tensor_reduce(neg_max[:, j, 0:4], S_lat[:, j], AX.X, ALU.max, negate=True).then_inc(sc_sb, 1)
                if g:
                    probs_turned(g - 1)
                dve.wait_ge(p_exp, g + 1)
                link(dve.reciprocal(row_sum[:, j], row_sum[:, j]))
                dve.tensor_tensor(S_lat[:, j], S_lat[:, j],
                                  row_sum[:, j, 0:4].unsqueeze(2).broadcast_to((P, 4, 2 * P)), ALU.mult)
                dve.tensor_tensor(S_pr[:, j], S_pr[:, j],
                                  row_sum[:, j, 4:8].unsqueeze(2).broadcast_to((P, 4, P)), ALU.mult)\
                   .then_inc(p_norm, 1)
            probs_turned(3)
            residual(mod[:, 1, 2], mixer_bank(1))

            dve.wait_ge(cache_out, 32)
            experts_front(1)
            experts(1)
            squares(4)
            normed(4)
            norm(4, None)
            for n in (1, 3):
                dve.wait_ge(yt_ps, n + 1)
                dve.tensor_copy(y_tok[:, n // 2, :, 4:8].rearrange("s p k -> s k p"),
                                psum[:, n, :].rearrange("s (k p) -> s k p", p=P)).then_inc(yt_sb, 1)

        @block.tensor
        def _(pe):
            def mm(out, lhsT, rhs, start, stop, **kw):
                return pe.matmul(out, lhsT, rhs, start=start, stop=stop, skip_group_check=True, **kw)

            pe.wait_ge(s_const, 16)
            pe.wait_ge(s_x, 32)
            for n in range(4):
                for i in range(4):
                    k = 4 * (n // 2) + i
                    ins = pe.transpose(psum[:, n, i * T:(i + 1) * T], x_tok[:, n % 2, k::K], ident)
                ins.then_inc(x_ps, 1)
            pe.wait_ge(s_small, SMALL)
            for i in range(3):
                ins = pe.transpose(psum[:, 5, i * HEADS:(i + 1) * HEADS], lbrow[0:HEADS, i], ident[0:HEADS, 0:HEADS])
            ins.then_inc(lb_ps, 1)
            pe.wait_ge(ready, 5)

            def norm_sums(n):
                pe.wait_ge(sq_done, 2 * (n + 1))
                for k in range(K):
                    ins = mm(psum[:, 4, 0:NT], ones, sq[:, k], k == 0, k == K - 1)
                ins.then_inc(ssum, 1)

            norm_sums(0)
            pe.wait_ge(cond_done, 1)
            at_stage = [0]

            def staged():
                n = at_stage[0]
                at_stage[0] += 1
                pe.wait_ge(stage_in[rooms[n]], 16 * room_count[n])
                return stage[rooms[n]]

            def ada(n):
                w = staged()
                if n % 2:
                    pe.wait_ge(ada_row, n)
                elif n:
                    pe.wait_ge(mod_done, n // 2)
                for i in range(K // 4):
                    for c in range(4):
                        ins = mm(psum[32 * c:32 * c + 32, 7, :], cond_act[:, 4 * i + c, :], w[:, 4 * i + c, :],
                                 i == 0, i == K // 4 - 1)
                ins.then_inc(ada_ps, 1)

            def ada_columns(n):
                pe.wait_ge(ada_row, 2 * n + 2)
                for k in range(K):
                    ins = mm(psum[:, 7, 2 * k:2 * k + 2], mrow[:, k::K], sel, True, True)
                ins.then_inc(sel_ps, 1)

            for n in range(2):
                ada(2 * n)
                ada(2 * n + 1)
                ada_columns(n)
            pe.wait_ge(h_done, 2)

            def project(b, by_rows):
                w = staged()
                u = 2 * (b % 2)
                if b >= 2:
                    pe.wait_ge(unit_free[b % 2], b // 2)
                if by_rows:
                    for a in range(2):
                        for k in range(K):
                            ins = mm(psum[:, u + a, :], hT[:, k, a * T:(a + 1) * T], w[:, k], k == 0, k == K - 1)
                else:
                    for n in range(4):
                        for k in range(K):
                            ins = mm(psum[:, u + n // 2, (n % 2) * NT:(n % 2 + 1) * NT], w[:, k, n * P:(n + 1) * P],
                                     hT[:, k], k == 0, k == K - 1)
                ins.then_inc(proj, 1)

            def scores(g, n):
                if n == 0 and g:
                    pe.wait_ge(o_rstd, g)
                if n == 2 and g:
                    pe.wait_ge(st_sb, 2 * g)
                for d in range(2):
                    pe.wait_ge(qk_done, 8 * g + 2 * n + d + 1)
                    for u in range(UNITS):
                        size = (128, 64, 32)[n]
                        for i in range(T // size):
                            early = slice(size * i, size * i + size // 2)
                            behind = slice(size * i + size // 2, size * (i + 1))
                            ss, ts = (early, behind) if d == 0 else (behind, early)
                            if n == 2:
                                ss = ts = slice(size * i, size * (i + 1))
                            if n == 2 and d:
                                out = psum[ss, 6, 32 * u:32 * u + 32]
                            else:
                                c = (u % 4) * T
                                out = psum[ss, 4 + u // 4, c + ts.start:c + ts.stop]
                            ins = mm(out, Kd[d][:, u, ss], Q[d][:, u, ts], True, True)
                    ins.then_inc(qk_used, 1)

            def values(g):
                pe.wait_ge(at_done, g + 1)
                pe.wait_ge(qk_done, 8 * g + 8)
                pe.wait_ge(unit_free[(5 * g + 4) % 2], (5 * g + 4) // 2 + 1)
                pe.wait_ge(s_s0, 32)
                for u in range(UNITS):
                    h, s = GROUP * g + u // 2, u % 2
                    out = psum[:, 4 + u // 4, (u % 4) * T:(u % 4 + 1) * T]
                    ins = mm(out, v[:, s, h * DV:(h + 1) * DV], AT[:, u], True, s == 0)
                    if s:
                        for d in range(2):
                            ins = mm(out, s0[:, d, h], Q[d][:, u // 2], False, d == 1)
                ins.then_inc(pv_done, 1)

            def turn_keys(g, d):
                if d:
                    pe.wait_ge(st_sb, 2 * g + 1)
                for i in range(GROUP):
                    ins = pe.transpose(psum[:, 6, i * T:(i + 1) * T], Kd[d][:, i], ident)
                ins.then_inc(kd_ps, 1)
                if d:
                    pe.wait_ge(kd_ps, 2 * g + 2)
                    pe.sem_inc(qk_used, 2)

            def state(g, d):
                pe.wait_ge(kd_sb, 2 * g + d + 1)
                for i in range(GROUP):
                    h = GROUP * g + i
                    ins = mm(psum[:, 6, i * DV:(i + 1) * DV], Kd[d][:, GROUP + i], v[:, 0, h * DV:(h + 1) * DV],
                             True, True)
                ins.then_inc(st_ps, 1)

            def recur(g, item):
                if item <= 2:
                    scores(g, item)
                elif item == 3:
                    values(g)
                    turn_keys(g, 0)
                elif item == 4:
                    pe.wait_ge(o_sq, g + 1)
                    for i in range(2):
                        ins = mm(psum[:, 4 + i, :], ones, dif[0][:, 4 * i:4 * i + 4], True, True)
                    ins.then_inc(o_ssum, 1)
                    state(g, 0)
                elif item == 5:
                    turn_keys(g, 1)
                elif item == 6:
                    state(g, 1)

            finished = 2
            for b, items, part, adas in ada_rounds():
                if part == finished:
                    ada_columns(part)
                    finished += 1
                if b is not None:
                    project(b, KINDS[b % 5] == "v")
                for n in adas[:1]:
                    ada(n)
                for g, item in items:
                    recur(g, item)
                for n in adas[1:]:
                    ada(n)

            def project_out(m, src, read):
                pe.wait_ge(late_in, 16 * (m + 1))
                for a, n in read:
                    pe.wait_ge(a, n)
                for part in range(2):
                    for k in range(K):
                        for h in range(part * K // 2, (part + 1) * K // 2):
                            ins = mm(psum[:, k // 2, (k % 2) * NT:(k % 2 + 1) * NT], late[:, h, k::K], src[:, h],
                                     h == 0 and k % 2 == 0, h == K - 1)
                        if part == 1 and k % 2:
                            ins.then_inc(out_ps, 1)
                    if part == 0:
                        ins.then_inc(late_half, 1)

            project_out(0, oT, [(o_done, 2), (unit_free[0], 5), (unit_free[1], 5)])

            def experts_front(m):
                M = moe[m]
                norm_sums(2 * m + 1)
                pe.wait_ge(h_done, 4 * m + 4)
                for a in range(2):
                    for k in range(K):
                        ins = mm(psum[:, 5, a * E:(a + 1) * E], hT[:, k, a * T:(a + 1) * T], router_w[:, m, k],
                                 k == 0, k == K - 1)
                ins.then_inc(M.logits, 1)
                for n in range(4):
                    if n >= 2:
                        pe.wait_ge(M.htok, n - 1)
                    for i in range(4):
                        ins = pe.transpose(psum[:, 6 + n % 2, i * P:(i + 1) * P],
                                           hT[:, 4 * (n % 2) + i, (n // 2) * T:(n // 2 + 1) * T], ident)
                    ins.then_inc(M.htok_ps, 1)
                pe.wait_ge(M.sh_in, 48)
                for a in range(2):
                    pe.wait_ge(M.htok, 3 + a)
                    for k in range(K):
                        ins = mm(psum[:, 6 + a, :], hT[:, k, a * T:(a + 1) * T], ws_gu[:, k], k == 0, k == K - 1)
                    ins.then_inc(M.sh_ps, 1)
                pe.wait_ge(M.mask, 1)
                mask = route[:, 4]
                mm(psum[:, 5, 0:E], before, mask[:, 0], True, True)
                mm(psum[:, 5, E:2 * E], ones, mask[:, 0], True, False)
                mm(psum[:, 5, E:2 * E], before, mask[:, 1], False, True)
                mm(psum[:, 5, 2 * E:3 * E], ones, mask[:, 0], True, False)
                mm(psum[:, 5, 2 * E:3 * E], ones, mask[:, 1], False, True).then_inc(M.rank_ps, 1)
                pe.wait_ge(M.sh_hid, 1)
                pe.wait_ge(M.hid, 1)
                for c in range(2):
                    for a in range(2):
                        ins = pe.transpose(psum[:, 4, c * NT + a * T:c * NT + (a + 1) * T],
                                           sh_hid[:, a, c * P:(c + 1) * P], ident)
                ins.then_inc(M.t_ps, 1)
                pe.wait_ge(M.t_sb, 1)
                for k in range(K):
                    for c in range(2):
                        ins = mm(psum[:, k // 2, (k % 2) * NT:(k % 2 + 1) * NT], ws_dn[:, c, k::K], sh_hidT[:, c],
                                 k % 2 == 0 and c == 0, False)
                ins.then_inc(M.sh_used, 1)

            def gather(M, g, n, j):
                pe.wait_ge(M.onehot, g + 1)
                for half in range(2):
                    pe.wait_ge(M.y_rest, n * 2 + (half + 1))
                    for i in range(4):
                        for a in range(2):
                            for part in range(3):
                                ins = mm(psum[:, 6 + half, i * P:(i + 1) * P], h_tok[:, part, a, 4 * half + i],
                                         onehot[:, j, a], a == 0 and part == 0, a == 1 and part == 2)
                    ins.then_inc(M.xg_ps[half], 1)

            def turn_hots(M, expert, j):
                for a in range(2):
                    mm(psum[:, 5, a * P:(a + 1) * P], onehot[:, j, a], ident_b, True, True)
                for a in range(2):
                    weights = comb[:, a, expert:expert + 2] if isinstance(expert, int) else comb[:, a, bass.ds(expert, 2)]
                    ins = mm(psum[:, 5, NT:NT + 6], onehot[:, j, a], weights.rearrange("p e i -> p (e i)"),
                             a == 0, a == 1)
                ins.then_inc(M.hot_ps, 1)

            def combine(M, j):
                for k in range(K):
                    for part in range(3):
                        ins = mm(psum[:, k // 2, (k % 2) * NT:(k % 2 + 1) * NT], y[:, j, part, k],
                                 onehot_t[:, j].rearrange("p a t -> p (a t)"), False, False)
                ins.then_inc(M.comb, 1)

            def experts_pass(M, r):
                if not isinstance(r, int):
                    for half in range(2):
                        pe.wait_ge(M.xg[half], r * (PAIRS + 1))
                    pe.wait_ge(M.hot_t, r * (PAIRS + 1))
                gather(M, r * (PAIRS + 1), r * PAIRS, 0)
                turn_hots(M, 0, 0)
                with pe.Fori(0, PAIRS // 2) as h:
                    for j in range(2):
                        n, g = r * PAIRS + h * 2 + j, r * (PAIRS + 1) + h * 2 + j
                        pe.wait_ge(M.gu_in[j], (r * (PAIRS // 2) + h) * 64 + 64)
                        pe.wait_ge(M.xg[0], g + 1)
                        pe.wait_ge(M.xg[1], g + 1)
                        pe.wait_ge(M.hid, n + 1)
                        for k in range(K):
                            for w in range(2):
                                for e in range(2):
                                    at = slice(SLOTS * e, SLOTS * (e + 1))
                                    ins = mm(psum[at, 4, w * F:(w + 1) * F], xg[:, j, k, at],
                                             ring[:, j, 2 * e + w, k * F:(k + 1) * F], k == 0 and w == 0, k == K - 1)
                        ins.then_inc(M.gu, 1)
                        gather(M, g + 1, n, 1 - j)
                        pe.wait_ge(M.hid, n + 2)
                        pe.wait_ge(M.hot_t, g + 1)
                        for c in range(2):
                            ins = pe.transpose(psum[:, 5, c * P:(c + 1) * P], hid[:, j, c * P:(c + 1) * P], ident)
                        ins.then_inc(M.t_ps, 1)
                        pe.wait_ge(M.c_zero, r + 1)
                        pe.wait_ge(M.y_low, n + 1)
                        combine(M, 1 - j)
                        pe.wait_ge(M.t_sb, n + 2)
                        turn_hots(M, h * 4 + 2 * (j + 1), 1 - j)
                        pe.wait_ge(M.dn_in[j], (r * (PAIRS // 2) + h) * 32 + 32)
                        for half in range(2):
                            pe.wait_ge(M.xg[half], g + 2)
                            for c in range(2):
                                for e in range(2):
                                    at = slice(SLOTS * e, SLOTS * (e + 1))
                                    ins = mm(psum[at, 6 + half, :], hidT[:, j, c, at],
                                             ring[:, j, 4 + e, c * D + half * BLOCK:c * D + (half + 1) * BLOCK],
                                             c == 0, c == 1)
                            ins.then_inc(M.y_ps[half], 1)
                pe.wait_ge(M.y_low, r * PAIRS + PAIRS + 1)
                combine(M, 1)

            def experts(m):
                M = moe[m]
                pe.wait_ge(M.h_low, 4)
                experts_pass(M, 0)
                pe.wait_ge(M.table, 1)
                more = pe.value_load(extra[0:1, 0:1].bitcast(I32), min_val=0, max_val=3)
                with pe.If(more > 0):
                    with pe.Fori(0, more) as r:
                        experts_pass(M, r + 1)
                pe.wait_ge(M.comb, more * (PAIRS + 1) + (PAIRS + 1))
                pe.sem_inc(M.done, 1)

            experts_front(0)
            experts(0)

            norm_sums(2)
            pe.wait_ge(h_done, 6)
            for b in range(10, 12):
                project(b, False)
            pe.wait_ge(cache_in, 32)
            for n in range(2):
                for i in range(4):
                    ins = pe.transpose(psum[:, 4 + n, i * P:(i + 1) * P], ck[:, (4 * n + i) * P:(4 * n + i + 1) * P], ident)
                ins.then_inc(tr_ps, 1)
            pe.wait_ge(bias_in, 64)
            for n in range(4):
                if n >= 2:
                    pe.wait_ge(bias_done, n - 1)
                mm(psum[:, 6 + n % 2, :], flip, bias[:, 4 * n:4 * n + 4].rearrange("p h s -> p (h s)"), True, True)\
                    .then_inc(bias_ps, 1)
            for b in range(12, 14):
                project(b, False)
            for b in range(14, 16):
                project(b, True)
            for n in range(2):
                pe.wait_ge(tr_sb, n + 1)
                pe.wait_ge(unit_free[n], 7)
                for i in range(4):
                    ins = pe.transpose(psum[:, 4 + n, i * P:(i + 1) * P], kT[:, 4 * n + i, 0:T], ident)
                ins.then_inc(tr_ps, 1)
            for u in range(2):
                pe.wait_ge(unit_free[u], 8)
            pe.wait_ge(tr_sb, 4)

            def attend(g):
                if g:
                    pe.wait_ge(p_exp, g)
                for i in range(2):
                    for par in range(2):
                        rows, c = slice(HD * par, HD * (par + 1)), 2 * g + i
                        at = psum[:, 4 + par, i * 2 * P:(i + 1) * 2 * P]
                        mm(at[:, 0:P], qT[rows, c, T:NT], kT[rows, c, T:NT], True, True)
                        mm(at[:, P:2 * P], qT[rows, c, T:NT], ckT[rows, c], True, True)
                for i in range(2):
                    for par in range(2):
                        rows, c = slice(HD * par, HD * (par + 1)), 2 * g + i
                        ins = mm(psum[:, 6 + par, i * P:(i + 1) * P], qT[rows, c, 0:T], kT[rows, c, 0:T], True, True)
                ins.then_inc(sc_ps, 1)

            attend(0)
            for g in range(4):
                if g < 3:
                    attend(g + 1)
                pe.wait_ge(p_norm, g + 1)
                for n in range(4):
                    for i in range(2):
                        m = 2 * n + i
                        pe.transpose(psum[:, m // 4, (m % 4) * P:(m % 4 + 1) * P], S_lat[:, g % 2, n, i * P:(i + 1) * P], ident)
                for n in range(4):
                    ins = pe.transpose(psum[:, 2, n * P:(n + 1) * P], S_pr[:, g % 2, n], ident)
                ins.then_inc(pt_ps, 1)
                pe.wait_ge(pt_sb, g + 1)
                if g:
                    pe.wait_ge(oa_sb, g)
                for n in range(4):
                    par, i = n // 2, n % 2
                    cols = slice((4 * g + 2 * i + par) * HD, (4 * g + 2 * i + par + 1) * HD)
                    rows = slice(HD * par, HD * (par + 1))
                    mm(psum[rows, 3, (2 * i + 1) * P:(2 * i + 2) * P], va[:, 1, cols], PT[:, 2 * n], True, False)
                    mm(psum[rows, 3, (2 * i + 1) * P:(2 * i + 2) * P], cv[:, cols], PT[:, 2 * n + 1], False, True)
                    ins = mm(psum[rows, 3, 2 * i * P:(2 * i + 1) * P], va[:, 0, cols], PT[:, 8 + n], True, True)
                ins.then_inc(oa_ps, 1)
            project_out(1, oTa, [(oa_sb, 4)])
            experts_front(1)
            experts(1)
            norm_sums(4)
            pe.wait_ge(h_done, 10)
            for n in range(4):
                for i in range(4):
                    k = 4 * (n % 2) + i
                    ins = pe.transpose(psum[:, n, i * P:(i + 1) * P], hT[:, k, (n // 2) * T:(n // 2 + 1) * T], ident)
                ins.then_inc(yt_ps, 1)


INPUTS = ["x_prompt", "x_sample", "state_hgrn_fwd", "state_hgrn_bwd", "cache_na_k", "cache_na_v", "c", "c_ctx",
          "norm1_w", "norm2_w", "ada_w", "ada_b", "hgrn_w_in", "hgrn_lb_logits", "hgrn_gn_w", "hgrn_w_out",
          "na_w_qkv", "na_rpb", "na_w_o", "moe_w_router", "moe_router_bias", "moe_w_gate", "moe_w_up", "moe_w_down",
          "shared_w_gate", "shared_w_up", "shared_w_down", "final_norm_w"]
OUTPUTS = [("out_prompt", (1, T, D)), ("out_sample", (1, T, D)),
           ("out_state_fwd", (1, 1, HEADS, DK, DV)), ("out_state_bwd", (1, 1, HEADS, DK, DV)),
           ("out_cache_k", (1, 1, T, A_HEADS, HD)), ("out_cache_v", (1, 1, T, A_HEADS, HD))]


def kernel(**inputs):
    import concourse.bacc as bacc
    from concourse.bass_utils import run_bass_kernel_spmd

    nc = bacc.Bacc("TRN2", target_bir_lowering=False, num_devices=1)
    arrays = {f"in_{n}": np.ascontiguousarray(inputs[n]) for n in INPUTS}
    arrays["in_table"] = shape_constants()
    io = {n[3:]: nc.dram_tensor(n, a.shape, mybir.dt.from_np(a.dtype), kind="ExternalInput").ap()
          for n, a in arrays.items()}
    for n, shape in OUTPUTS:
        io[n] = nc.dram_tensor(n, shape, F32, kind="ExternalOutput").ap()
    build(nc, io)
    r = run_bass_kernel_spmd(nc, [arrays], core_ids=[0])
    return tuple(r.results[0][n] for n, _ in OUTPUTS)
```

```python
from contextlib import ExitStack

import numpy as np

import concourse.bass as bass
from concourse import mybir
from concourse.alu_op_type import AluOpType as ALU

ACT = mybir.ActivationFunctionType
AX = mybir.AxisListType
F32 = mybir.dt.float32
BF16 = mybir.dt.bfloat16
I32 = mybir.dt.int32

P = 128
D = 1024
K = D // P
T = 128
NT = 2 * T
EPS = 1e-6
HEADS, DK, DV = 8, 128, 128
GROUP = 4
A_HEADS, HD = 16, 64
GRID_W, WIN_R, WIN_C = 64, 8, 16
E, TOP_K, GROUPS, TOP_GROUPS = 64, 6, 8, 4
F = 256
SLOTS = 64
PAIRS = E // 2
ROUTED_SCALE = 2.5
LOW = -1e30
BLOCK = 512
BLOCK_W = K * BLOCK

C_ID, C_SEL, C_MASKF, C_MASKB, C_BEFORE, C_IOTA, C_WIN, C_WNEG, C_FLIP, C_END = np.cumsum(
    [0, 128, 2, 128, 32, 128, 4 * SLOTS, 128, 128, 128]).tolist()


def shape_constants():
    c = np.zeros((P, C_END), np.float32)
    i, j = np.arange(P)[:, None], np.arange(P)[None, :]
    c[:, C_ID:C_ID + P] = i == j
    c[:, C_MASKF:C_MASKF + P] = (i // 32 != j // 32) | (i <= j)
    c[:, C_MASKB:C_MASKB + 32] = i % 32 >= np.arange(32)[None, :]
    c[:, C_BEFORE:C_BEFORE + P] = i < j
    c[:, C_IOTA:C_IOTA + 4 * SLOTS] = np.arange(4 * SLOTS)[None, :]
    for g in range(4):
        for s in range(2):
            c[32 * g + s, C_SEL + s] = 1.0
    start = np.clip(np.arange(GRID_W) - WIN_C // 2, 0, GRID_W - WIN_C)
    col = np.arange(P) % GRID_W
    inside = (col[None, :] >= start[col][:, None]) & (col[None, :] < start[col][:, None] + WIN_C)
    c[:, C_WIN:C_WIN + P] = inside
    c[:, C_WNEG:C_WNEG + P] = np.where(inside, 0.0, LOW)
    c[:, C_FLIP:C_FLIP + P] = (i // GRID_W == j // GRID_W) & (i % GRID_W + j % GRID_W == GRID_W - 1)
    return c


def build(nc, io):
    ctx = ExitStack()
    with ctx:
        def sem(name):
            return ctx.enter_context(nc.semaphore(name))

        WORDS = 53200
        arena = ctx.enter_context(nc.sbuf_tensor("arena", [P, WORDS], F32))
        top = [0]

        def cut(n, shape=None, at=None, dtype=None):
            a = top[0] if at is None else at
            if at is None:
                top[0] += n
                assert top[0] <= WORDS, top[0]
            v = arena[:, a:a + n]
            if dtype is not None:
                v = v.bitcast(dtype)
            if shape:
                names = "abcd"[:len(shape)]
                v = v.rearrange(f"p ({' '.join(names)}) -> p {' '.join(names)}", **dict(zip(names, shape)))
            return v

        xT = cut(K * NT, (K, NT))
        hT = cut(K * NT, (K, NT))
        consts = cut(C_END)
        ones = cut(P)
        mod = cut(2 * 48 * 2, (2, 6, K, 2))
        gain = cut(4 * K * 2, (4, K, 2))
        norm_w = cut(5 * K, (5, K))
        ada_b = cut(2 * 48, (2, 6, K))
        lb = cut(3 * HEADS, (3, HEADS))
        lb0 = cut(HEADS)
        lb_t = cut(HEADS)
        one_minus_lb = cut(HEADS)
        gn_w = cut(1)
        eps = cut(1)
        cond = cut(2 * K, (2, K))
        cond_act = cut(K * 32, (K, 32))
        router_w = cut(2 * K * E, (2, K, E))
        router_b = cut(2 * E, (2, E))
        rank = cut(2 * E, (2, E))
        comb = cut(3 * E, (2, E, 3), dtype=BF16)
        ident_b = cut(P // 2, dtype=BF16)
        extra = cut(1)
        rstd = cut(NT)
        PAIR_W = 6 * K * F
        ring_at = top[0]
        ring = cut(2 * PAIR_W, (2, 6, K * F))
        late_at = top[0]
        late = cut(HEADS * D, (HEADS, D))
        ws_gu = cut(K * 2 * F, (K, 2 * F), at=late_at)
        ws_dn = cut(2 * D, (2, D), at=late_at + K * 2 * F)
        scratch_at = top[0]
        SCRATCH_W = WORDS - scratch_at

        class Scratch:
            def __init__(self, at, size):
                self.at, self.end = at, at + size

            def __call__(self, n, shape=None, dtype=None):
                self.at += n
                assert self.at <= self.end, (self.at, self.end)
                return cut(n, shape, at=self.at - n, dtype=dtype)

        stage = [cut(BLOCK_W, (K, BLOCK), at=at + n * BLOCK_W)
                 for at, count in ((ring_at, 3), (late_at, 2)) for n in range(count)]

        sc = Scratch(scratch_at, SCRATCH_W)
        h_tok = sc(3 * D, (3, 2, K, P), BF16)
        xg = sc(2 * K * P, (2, K, P))
        onehot = sc(2 * P, (2, 2, P), BF16)
        onehot_t = sc(2 * P, (2, 2, P), BF16)
        hidT = sc(2 * 2 * P, (2, 2, P))
        hid = sc(2 * 2 * P, (2, 2 * P))
        silu = sc(2 * F, (2, F))
        y = sc(3 * D, (2, 3, K, P), BF16)
        route = sc(12 * 2 * E, (12, 2, E))
        slot_w = sc(2)
        slot_parts = sc(2 * 3, (2, 3))
        h_rest = xg
        y_rest = route.rearrange("p n a e -> p (n a e)")[:, 0:D].rearrange("p (k t) -> p k t", k=K)
        sq = cut(K * NT, (K, NT), at=scratch_at)
        sh_room = y[:, 0].rearrange("p i k t -> p (i k t)").bitcast(F32).rearrange("p (n a f) -> p n a f", n=3, a=2)
        sh_silu, sh_hid, sh_hidT = (sh_room[:, n] for n in range(3))

        sc = Scratch(ring_at + PAIR_W, PAIR_W)
        q = sc(HEADS * NT, (HEADS, NT))
        kk = [sc(HEADS * NT, (HEADS, NT)) for _ in range(2)]
        bb = [sc(HEADS * NT, (HEADS, NT)) for _ in range(2)]
        gate = sc(HEADS * NT, (HEADS, NT))
        oT = q
        sc = Scratch(scratch_at, SCRATCH_W)
        v = sc(2 * D, (2, D))
        s0 = sc(2 * D, (2, HEADS, DV))
        UNITS = GROUP * 2
        Q = [sc(UNITS * T, (UNITS, T)) for _ in range(2)]
        Kd = [sc(UNITS * T, (UNITS, T)) for _ in range(2)]
        dif = [sc(UNITS * T, (UNITS, T)) for _ in range(2)]
        AT = dif[1]
        fb_sb = sc(UNITS * 32, (UNITS, 32))
        scan_keep = sc(UNITS * T)
        mrow = sc(D, (D,))
        x_tok = cut(2 * D, (2, D), at=scratch_at)
        lbrow = cut(3 * P, (3, P), at=scratch_at + 2 * D)

        sc = Scratch(ring_at + PAIR_W, PAIR_W)
        qT = sc(K * NT, (K, NT))
        kT = sc(K * NT, (K, NT))
        va = sc(2 * D, (2, D))
        ckT = sc(K * T, (K, T))
        cv = sc(D, (D,))
        ck = sc(D, (D,))
        bias = sc(A_HEADS * P, (A_HEADS, P))
        sc = Scratch(scratch_at, SCRATCH_W)
        sc(K * NT)
        S_lat = sc(2 * 4 * 2 * P, (2, 4, 2 * P))
        S_pr = sc(2 * 4 * P, (2, 4, P))
        PT = sc(12 * P, (12, P))
        oTa = sc(K * NT, (K, NT))
        kout = sc(D, (K, P))
        neg_max = sc(2 * 8, (2, 8))
        row_sum = sc(2 * 8, (2, 8))
        y_tok = cut(2 * D, (2, P, K), at=scratch_at + K * NT)

        ident = consts[:, C_ID:C_ID + P]
        mask_f = consts[:, C_MASKF:C_MASKF + P]
        mask_b = consts[:, C_MASKB:C_MASKB + 32]
        before = consts[:, C_BEFORE:C_BEFORE + P]
        sel = consts[:, C_SEL:C_SEL + 2]
        window = consts[:, C_WIN:C_WIN + P]
        window_neg = consts[:, C_WNEG:C_WNEG + P]
        flip = consts[:, C_FLIP:C_FLIP + P]

        psum = ctx.enter_context(nc.psum_tensor("psum", [P, 8, 512], F32))

        s_table = sem("tables_in")
        s_const, s_x, s_small, s_s0 = sem("consts_in"), sem("x_in"), sem("small_in"), sem("states_in")
        stage_in = [sem(f"stage_in{n}") for n in range(5)]
        late_in, late_half = sem("late_in"), sem("late_half_used")
        cache_in, bias_in = sem("cache_in"), sem("bias_in")
        ready = sem("start_values_ready")
        x_ps, x_sb = sem("xT_in_psum"), sem("xT_in_sbuf")
        lb_ps, lb_shift, lb_exp = sem("lb_in_psum"), sem("lb_shifted"), sem("lb_exp")
        cond_done = sem("cond_act_done")
        ada_ps, ada_row, sel_ps, mod_done = sem("ada_in_psum"), sem("ada_rows"), sem("ada_cols_in_psum"), sem("mod_done")
        sq_done, ssum, root = sem("squares"), sem("square_sums"), sem("root")
        x_normed, gains = sem("x_normed"), sem("gains_ready")
        h_done = [sem("h_first_half"), sem("h_second_half")]
        proj, gate_sig = sem("proj_in_psum"), sem("gate_sigmoid")
        unit_free = [sem("proj_unit0_read"), sem("proj_unit1_read")]
        f_done, ln_done = sem("decay_done"), sem("log_decay_done")
        dif_done, exp_done, qk_done, qk_used = sem("dif_done"), sem("exp_done"), sem("qk_done"), sem("qk_used")
        at_done, pv_done, o_copied, o_sq, o_ssum, o_rstd, o_done = (
            sem(n) for n in ("scores_masked", "pv_done", "o_copied", "o_squares", "o_square_sums", "o_rstd", "o_done"))
        kd_ps, kd_sb, st_ps, st_sb, st_out = (
            sem(n) for n in ("kdecT_in_psum", "kdecT", "state_in_psum", "state", "state_stored"))
        out_ps, resid = sem("mixer_out_in_psum"), sem("residual_added")
        dve_c, act_c = sem("dve_chain"), sem("act_chain")
        tr_ps, tr_sb = sem("key_rows_in_psum"), sem("key_rows")
        bias_ps, bias_done = sem("bias_in_psum"), sem("bias_windowed")
        sc_ps, sc_sb, p_exp, p_norm, pt_ps, pt_sb, oa_ps, oa_sb = (
            sem(n) for n in ("scores_in_psum", "scores_read", "probs", "probs_normed", "probsT_in_psum", "probsT",
                             "attn_in_psum", "attn_done"))
        sc_pr, pr_exp = sem("prompt_scores_max"), sem("prompt_probs")
        cache_out = sem("cache_stored")
        yt_ps, yt_sb, y_out = sem("yT_in_psum"), sem("y_rows"), sem("y_stored")

        class Moe:

            def __init__(self, l):
                def s(name):
                    return sem(f"{name}_{l}")

                self.logits, self.scores = s("logits"), s("scores")
                self.htok_ps, self.htok = s("htok_ps"), s("htok")
                self.h_rest, self.h_mid, self.h_low = s("h_rest"), s("h_mid"), s("h_low")
                self.mask, self.rank_ps, self.table = s("mask"), s("rank_ps"), s("table")
                self.sh_in, self.sh_ps, self.sh_silu, self.sh_hid = s("sh_in"), s("sh_ps"), s("sh_silu"), s("sh_hid")
                self.sh_used = s("sh_used")
                self.gu_in = [s("gu_in0"), s("gu_in1")]
                self.dn_in = [s("dn_in0"), s("dn_in1")]
                self.gu = s("gu")
                self.onehot, self.hot_ps, self.hot_t = s("onehot"), s("hot_ps"), s("hot_t")
                self.xg_ps = [s("xg_ps0"), s("xg_ps1")]
                self.xg = [s("xg_act"), s("xg_dve")]
                self.silu, self.hid, self.t_ps, self.t_sb = s("silu"), s("hid"), s("t_ps"), s("t_sb")
                self.y_ps = [s("y_ps0"), s("y_ps1")]
                self.y_high, self.y_rest, self.y_mid, self.y_low = s("y_high"), s("y_rest"), s("y_mid"), s("y_low")
                self.done = s("moe_done")

        moe = [Moe(0), Moe(1)]

        block = ctx.enter_context(nc.Block())

        KINDS = ["f_fw", "f_bw", "q", "v", "gate"]
        DECAY = -1
        ROUNDS = [(0, [], [], 1), (1, [], [], 1), (2, [], [(0, DECAY)], 2), (3, [], [(0, 0)], 2), (4, [(0, 1)], [(0, 2)], 2),
                  (5, [(0, 3)], [(0, 4)], 2), (6, [(0, 5)], [(0, 6)], 2), (7, [(0, 7)], [(1, DECAY)], 2),
                  (8, [(1, 0)], [(1, 1)], 2), (9, [(1, 2)], [(1, 3)], 2),
                  (None, [], [(1, 4)], 1), (None, [], [(1, 5)], 1), (None, [], [(1, 6), (1, 7)], 0)]
        COL = {"q": 0, "f_fw": D, "f_bw": 2 * D, "v": 3 * D, "gate": 4 * D}
        parts = [(l, j) for l in range(2) for j in range(6)]
        stages = [("ada", l, j, half) for l, j in parts[:2] for half in range(2)]
        halves = [("ada", l, j, half) for l, j in parts[2:] for half in range(2)]
        for b, _, _, count in ROUNDS:
            stages += [("in", b // 5, KINDS[b % 5])] if b is not None else []
            stages += [halves.pop(0) for _ in range(count)]
        assert not halves

        def ada_rounds():
            first, finished = 4, 2
            for b, middle, end, count in ROUNDS:
                part = finished if first >= 2 * finished + 2 else None
                finished += part is not None
                yield b, middle, end, part, range(first, first + count)
                first += count
            assert finished == len(parts)

        stages0 = len(stages)
        stages += [("qkv", n) for n in range(6)]

        def stage_source(what):
            if what[0] == "ada":
                _, l, j, half = what
                src = io["ada_w"][l, :, j * D + half * BLOCK:j * D + (half + 1) * BLOCK]
            elif what[0] == "in":
                c = COL[what[2]] + what[1] * BLOCK
                src = io["hgrn_w_in"][0, :, c:c + BLOCK]
            else:
                src = io["na_w_qkv"][0, :, what[1] * BLOCK:(what[1] + 1) * BLOCK]
            return src.rearrange("(p k) n -> p k n", p=P)

        rooms = [(n - stages0 + 3) % 5 for n in range(stages0)] + [3, 4, 0, 1, 2, 0]
        room_count = [rooms[:n + 1].count(rooms[n]) for n in range(len(rooms))]

        def block_used(n):
            ada_n = sum(w[0] == "ada" for w in stages[:n + 1])
            return (ada_ps, ada_n) if stages[n][0] == "ada" else (proj, n + 1 - ada_n)

        SMALL = 12 * 16

        def bank(n, count=1):
            return psum[:, n:n + count, :].rearrange("p b n -> p (b n)")

        def heads(a, g):
            return a[:, GROUP * g:GROUP * (g + 1)].rearrange("p h (s t) -> p (h s) t", s=2)

        small = [
            (cond[:, 0, :], io["c_ctx"].rearrange("(p k) -> p k", p=P)),
            (cond[:, 1, :], io["c"][0].rearrange("(p k) -> p k", p=P)),
            (norm_w[:, 0:4:2, :], io["norm1_w"].rearrange("l (p k) -> p l k", p=P)),
            (norm_w[:, 1:4:2, :], io["norm2_w"].rearrange("l (p k) -> p l k", p=P)),
            (norm_w[:, 4, :], io["final_norm_w"].rearrange("(p k) -> p k", p=P)),
            (ada_b.rearrange("p l j k -> p (l j) k"), io["ada_b"].rearrange("l (j p k) -> p (l j) k", p=P, j=6)),
            (lbrow[0:HEADS], io["hgrn_lb_logits"].rearrange("i (h d) -> h i d", h=HEADS)),
            (gn_w, io["hgrn_gn_w"].rearrange("a d -> d a")),
            (router_w[:, 0], io["moe_w_router"][0].rearrange("(p k) e -> p k e", p=P)),
            (router_w[:, 1], io["moe_w_router"][1].rearrange("(p k) e -> p k e", p=P)),
            (router_b[:, 0], io["moe_router_bias"][0:1].broadcast_to((P, E))),
            (router_b[:, 1], io["moe_router_bias"][1:2].broadcast_to((P, E))),
        ]
        assert len(small) * 16 == SMALL

        @block.sync
        def _(sp):
            sp.dma_start(x_tok[:, 0, :], io["x_prompt"][0]).then_inc(s_x, 16)
            sp.dma_start(x_tok[:, 1, :], io["x_sample"][0]).then_inc(s_x, 16)
            for dst, src in small[0::2]:
                sp.dma_start(dst, src).then_inc(s_small, 16)

            def load_stage(n):
                sp.dma_start(stage[rooms[n]], stage_source(stages[n])).then_inc(stage_in[rooms[n]], 16)

            def load_gate_up(m, j, expert):
                for w, name in enumerate(("moe_w_gate", "moe_w_up")):
                    src = io[name][m][bass.ds(expert, 2)].rearrange("e (p k) f -> p e (k f)", p=P)
                    sp.dma_start(ring[:, j, w:4:2, :], src).then_inc(moe[m].gu_in[j], 16)

            def load_down(m, j, expert):
                src = io["moe_w_down"][m][bass.ds(expert, 2)].rearrange("e (c p) d -> p (e c) d", p=P)
                dst = ring[:, j, 4:6, :].rearrange("p e (c d) -> p (e c) d", c=2)
                sp.dma_start(dst, src).then_inc(moe[m].dn_in[j], 16)

            def load_shared_gate_up(m):
                for w, name in enumerate(("shared_w_gate", "shared_w_up")):
                    sp.dma_start(ws_gu[:, :, w * F:(w + 1) * F],
                                 io[name][m].rearrange("(p k) f -> p k f", p=P)).then_inc(moe[m].sh_in, 16)

            def load_shared_down(m):
                sp.dma_start(ws_dn, io["shared_w_down"][m].rearrange("(c p) d -> p c d", p=P))\
                  .then_inc(moe[m].sh_in, 16)

            def stream_experts(m):
                with sp.Fori(1, PAIRS // 2) as h:
                    for j in range(2):
                        sp.wait_ge(moe[m].gu, h * 2 + (j - 1))
                        load_gate_up(m, j, h * 4 + 2 * j)
                        sp.wait_ge(moe[m].y_ps[1], h * 2 + (j - 1))
                        load_down(m, j, h * 4 + 2 * j)
                sp.wait_ge(moe[m].table, 1)
                more = sp.value_load(extra[0:1, 0:1].bitcast(I32), min_val=0, max_val=3)
                with sp.If(more > 0):
                    with sp.Fori(0, more) as r:
                        with sp.Fori(0, PAIRS // 2) as h:
                            for j in range(2):
                                sp.wait_ge(moe[m].gu, r * PAIRS + h * 2 + (PAIRS + j - 1))
                                load_gate_up(m, j, h * 4 + 2 * j)
                                sp.wait_ge(moe[m].y_ps[1], r * PAIRS + h * 2 + (PAIRS + j - 1))
                                load_down(m, j, h * 4 + 2 * j)
                return more

            for n in range(5):
                load_stage(n)
            sp.dma_start(consts[:, C_MASKF:], io["table"][:, C_MASKF:]).then_inc(s_table, 16)
            sp.wait_ge(lb_ps, 1)
            for d, name in enumerate(("state_hgrn_fwd", "state_hgrn_bwd")):
                sp.dma_start(s0[:, d], io[name][0, 0].rearrange("h k v -> k h v")).then_inc(s_s0, 16)
            for n in range(5, stages0):
                sp.wait_ge(*block_used(n - 5))
                load_stage(n)
            for n in (stages0 - 5, stages0 - 4):
                sp.wait_ge(*block_used(n))
            sp.dma_start(late, io["hgrn_w_out"][0].rearrange("(h p) d -> p h d", p=P)).then_inc(late_in, 16)
            for n in range(stages0 - 3, stages0):
                sp.wait_ge(*block_used(n))
            load_gate_up(0, 0, 0)
            load_down(0, 0, 0)
            sp.wait_ge(late_half, 1)
            load_shared_gate_up(0)
            sp.wait_ge(out_ps, 4)
            load_shared_down(0)
            load_gate_up(0, 1, 2)
            load_down(0, 1, 2)
            more = stream_experts(0)

            sp.wait_ge(moe[0].sh_used, 1)
            load_stage(stages0)
            load_stage(stages0 + 1)
            sp.wait_ge(moe[0].gu, more * PAIRS + (PAIRS - 1))
            load_stage(stages0 + 2)
            load_stage(stages0 + 3)
            sp.wait_ge(moe[0].y_ps[1], more * PAIRS + (PAIRS - 1))
            load_stage(stages0 + 4)
            sp.wait_ge(moe[0].done, 4)
            sp.dma_start(ck, io["cache_na_k"][0, 0].rearrange("s h d -> s (h d)")).then_inc(cache_in, 16)
            sp.dma_start(cv, io["cache_na_v"][0, 0].rearrange("s h d -> s (h d)")).then_inc(cache_in, 16)
            rpb = io["na_rpb"]
            for r in range(2):
                for r2 in range(2):
                    at = rpb.offset + (r2 - r + WIN_R - 1) * (2 * WIN_C - 1) + WIN_C - 1 - (GRID_W - 1)
                    src = bass.AP(tensor=rpb.tensor, offset=at,
                                  ap=[[1, GRID_W], [(2 * WIN_R - 1) * (2 * WIN_C - 1), A_HEADS], [1, GRID_W]])
                    sp.dma_start(bias[GRID_W * r:GRID_W * (r + 1), :, GRID_W * r2:GRID_W * (r2 + 1)], src)\
                      .then_inc(bias_in, 16)
            sp.wait_ge(*block_used(stages0 + 1))
            sp.dma_start(late, io["na_w_o"][0].rearrange("(c p) d -> p c d", p=P)).then_inc(late_in, 16)
            sp.wait_ge(*block_used(stages0 + 2))
            load_stage(stages0 + 5)
            sp.wait_ge(*block_used(stages0 + 5))
            load_gate_up(1, 0, 0)
            load_down(1, 0, 0)
            sp.wait_ge(late_half, 2)
            load_shared_gate_up(1)
            sp.wait_ge(out_ps, 8)
            load_shared_down(1)
            sp.wait_ge(cache_out, 32)
            load_gate_up(1, 1, 2)
            load_down(1, 1, 2)
            stream_experts(1)
            sp.wait_ge(st_out, 16 * 4)
            sp.wait_ge(cache_out, 32)
            sp.wait_ge(y_out, 32)

        @block.gpsimd
        def _(pool):
            pool.memset(ones, 1.0).then_inc(ready, 1)
            pool.memset(eps, EPS).then_inc(ready, 1)
            pool.memset(cond_act, 0.0).then_inc(ready, 1)
            pool.memset(scan_keep, 1.0).then_inc(ready, 1)
            pool.wait_ge(ready, 4)
            pool.memset(scan_keep.rearrange("p (u t) -> p u t", t=T)[:, :, 0:1], 0.0).then_inc(ready, 1)
            for M in moe:
                for part, before_it, after_it in ((0, M.htok, M.h_rest), (1, M.h_mid, M.h_low)):
                    for n in range(4):
                        pool.wait_ge(before_it, n + 1)
                        if part:
                            pool.wait_ge(M.h_rest, n + 1)
                        a, ks = n // 2, slice(4 * (n % 2), 4 * (n % 2) + 4)
                        out = h_tok[:, 2, a, ks] if part else h_rest[:, a, ks]
                        pool.tensor_tensor(out, h_rest[:, a, ks], h_tok[:, part, a, ks], ALU.subtract)\
                            .then_inc(after_it, 1)

        @block.scalar
        def _(act):
            act.dma_start(consts[:, 0:C_MASKF], io["table"][:, 0:C_MASKF]).then_inc(s_const, 16)
            for dst, src in small[1::2]:
                act.dma_start(dst, src).then_inc(s_small, 16)

            def copy(out, in_, **kw):
                return act.activation(out, in_, ACT.Copy, **kw)

            def squares(n):
                for i in range(4):
                    if n:
                        act.wait_ge(resid, 4 * (n - 1) + i + 1)
                    act.activation(sq[:, 2 * i:2 * i + 2], xT[:, 2 * i:2 * i + 2], ACT.Square).then_inc(sq_done, 1)

            def norm_root(n):
                act.wait_ge(ssum, n + 1)
                act.activation(rstd, psum[:, 4, 0:NT], ACT.Sqrt, scale=1.0 / D, bias=eps).then_inc(root, 1)

            def norm(n, shift):
                act.wait_ge(gains, 1 if n == 0 else 2)
                for k in range(4):
                    act.wait_ge(x_normed, 3 * n + k // 2 + 1)
                    for s in range(2):
                        part = hT[:, k, s * T:(s + 1) * T]
                        if shift is None:
                            ins = copy(part, part, scale=norm_w[:, 4, k:k + 1])
                        else:
                            ins = act.activation(part, part, ACT.Identity, scale=gain[:, n, k, s:s + 1],
                                                 bias=shift[:, k, s:s + 1])
                    ins.then_inc(h_done[0], 1)

            def ada_rows(n):
                act.wait_ge(ada_ps, n + 1)
                if n % 2 == 0 and n >= 2:
                    act.wait_ge(sel_ps, n // 2)
                copy(mrow[:, (n % 2) * BLOCK:(n % 2 + 1) * BLOCK], psum[:, 7, :]).then_inc(ada_row, 1)

            act.wait_ge(s_small, SMALL)
            act.wait_ge(ready, 5)
            act.activation(cond_act[:, :, 0:2], cond.rearrange("p s k -> p k s"), ACT.Silu).then_inc(cond_done, 1)
            for n in (0, 2):
                act.wait_ge(x_ps, n + 1)
                copy(xT[:, 2 * n:2 * n + 4, 0:T], psum[:, n, :].rearrange("p (k t) -> p k t", t=T)).then_inc(x_sb, 1)
            act.wait_ge(x_sb, 4)
            squares(0)
            act.wait_ge(lb_shift, 1)
            act.activation(lb, lb, ACT.Exp).then_inc(lb_exp, 1)
            norm_root(0)
            for n in range(4):
                ada_rows(n)
            norm(0, mod[:, 0, 0])

            def project(b):
                g, kind = b // 5, KINDS[b % 5]
                dst = {"f_fw": kk[0], "f_bw": kk[1], "gate": gate, "q": q, "v": None}[kind]
                if dst is None:
                    return
                act.wait_ge(proj, b + 1)
                dst = dst[:, GROUP * g:GROUP * (g + 1)].rearrange("p h t -> p (h t)")
                ins = act.activation(dst, bank(2 * (b % 2), 2), ACT.Copy if kind == "q" else ACT.Sigmoid)
                ins.then_inc(gate_sig if kind == "gate" else unit_free[b % 2], 1)

            def decay_exps(g, n):
                for d in range(2):
                    c = 8 * g + 2 * n + d
                    act.wait_ge(dif_done, c + 1)
                    if c >= 2:
                        act.wait_ge(qk_used, c - 1)
                    if n < 2:
                        H = 64 >> n
                        vq, vk, vd = (a.rearrange("p u (b t) -> p (u b) t", t=2 * H) for a in (Q[d], Kd[d], dif[d]))
                        early, behind = slice(0, H), slice(H, 2 * H)
                        qs, ks = (behind, early) if d == 0 else (early, behind)
                        act.activation(vq[:, :, qs], vd[:, :, qs], ACT.Exp)
                        ins = act.activation(vk[:, :, ks], vd[:, :, ks], ACT.Exp, scale=-1.0)
                    elif n == 2:
                        act.activation(Q[d], dif[d], ACT.Exp)
                        ins = act.activation(Kd[d], dif[d], ACT.Exp, scale=-1.0)
                    else:
                        act.activation(Q[d][:, 0:GROUP], bb[d][:, GROUP * g:GROUP * (g + 1), T:NT], ACT.Exp)
                        ins = act.activation(Kd[d][:, 0:GROUP], dif[d][:, 0:GROUP], ACT.Exp, scale=-1.0)
                    ins.then_inc(exp_done, 1)

            def keys_turned(g, d):
                act.wait_ge(kd_ps, 2 * g + d + 1)
                copy(Kd[d][:, GROUP:UNITS].rearrange("p u t -> p (u t)"), psum[:, 6, :]).then_inc(kd_sb, 1)

            def state_out(g, d):
                act.wait_ge(st_ps, 2 * g + d + 1)
                copy(Q[d][:, GROUP:UNITS].rearrange("p u t -> p (u t)"), psum[:, 6, :]).then_inc(st_sb, 1)
                act.wait_ge(st_sb, 2 * g + d + 1)
                dst = io["out_state_fwd" if d == 0 else "out_state_bwd"][0, 0, GROUP * g:GROUP * (g + 1)]
                act.dma_start(dst.rearrange("h k v -> k h v"), Q[d][:, GROUP:UNITS]).then_inc(st_out, 16)

            def recur(g, item):
                if item == DECAY:
                    for d in range(2):
                        act.wait_ge(f_done, 2 * g + d + 1)
                        if g:
                            act.wait_ge(o_done if d == 0 else pv_done, g)
                        act.activation(dif[d].rearrange("p u t -> p (u t)"),
                                       bb[d][:, GROUP * g:GROUP * (g + 1)].rearrange("p h t -> p (h t)"),
                                       ACT.Ln).then_inc(ln_done, 1)
                elif item <= 3:
                    if item == 0 and g:
                        act.wait_ge(st_out, 32 * g)
                    decay_exps(g, item)
                elif item == 4:
                    act.wait_ge(o_copied, g + 1)
                    act.activation(dif[0], heads(oT, g), ACT.Square).then_inc(o_sq, 1)
                    keys_turned(g, 0)
                elif item == 5:
                    act.wait_ge(o_ssum, g + 1)
                    act.activation(dif[0].rearrange("p u t -> p (u t)"), bank(4, 2), ACT.Ln, scale=1.0 / DV,
                                   bias=eps).then_inc(act_c, 1)
                    act.wait_ge(act_c, g + 1)
                    act.activation(dif[0], dif[0], ACT.Exp, scale=-0.5).then_inc(o_rstd, 1)
                    state_out(g, 0)
                elif item == 6:
                    keys_turned(g, 1)
                elif item == 7:
                    state_out(g, 1)

            for b, middle, end, _, adas in ada_rounds():
                for g, item in middle + end:
                    recur(g, item)
                if b is not None:
                    project(b)
                for n in adas:
                    ada_rows(n)

            def experts_front(m):
                M = moe[m]
                squares(2 * m + 1)
                norm_root(2 * m + 1)
                norm(2 * m + 1, mod[:, m, 3])
                act.wait_ge(M.logits, 1)
                act.activation(route[:, 0], psum[:, 5, 0:2 * E].rearrange("p (a e) -> p a e", a=2), ACT.Sigmoid)\
                   .then_inc(M.scores, 1)
                for n in range(4):
                    act.wait_ge(M.htok_ps, n + 1)
                    a, ks = n // 2, slice(4 * (n % 2), 4 * (n % 2) + 4)
                    rows = psum[:, 6 + n % 2, :].rearrange("p (k t) -> p k t", t=P)
                    copy(h_rest[:, a, ks], rows)
                    copy(h_tok[:, 0, a, ks], rows).then_inc(M.htok, 1)
                for n in range(4):
                    a, ks = n // 2, slice(4 * (n % 2), 4 * (n % 2) + 4)
                    act.wait_ge(M.h_rest, n + 1)
                    copy(h_tok[:, 1, a, ks], h_rest[:, a, ks]).then_inc(M.h_mid, 1)
                for a in range(2):
                    act.wait_ge(M.sh_ps, a + 1)
                    act.activation(sh_silu[:, a], psum[:, 6 + a, 0:F], ACT.Silu).then_inc(M.sh_silu, 1)
            def gathered(M, n, j):
                act.wait_ge(M.xg_ps[0], n + 1)
                copy(xg[:, j, 0:4], psum[:, 6, :].rearrange("p (k t) -> p k t", t=P)).then_inc(M.xg[0], 1)

            def hots_turned(M, n, j):
                act.wait_ge(M.hot_ps, n + 1)
                copy(onehot_t[:, j].rearrange("p a t -> p (a t)"), psum[:, 5, 0:NT])
                for e in range(2):
                    at = slice(SLOTS * e, SLOTS * (e + 1))
                    ins = copy(slot_parts[at, j], psum[at, 5, NT + 3 * e:NT + 3 * (e + 1)],
                               accum_out=slot_w[at, j:j + 1])
                ins.then_inc(M.hot_t, 1)

            def pair_step(M, n, j, last=False):
                act.wait_ge(M.gu, n + 1)
                act.activation(silu[:, j], psum[:, 4, 0:F], ACT.Silu).then_inc(M.silu, 1)
                if not last:
                    gathered(M, n + 1, 1 - j)
                act.wait_ge(M.t_ps, n + 2)
                copy(hidT[:, j].rearrange("p c t -> p (c t)"), psum[:, 5, 0:2 * P]).then_inc(M.t_sb, 1)
                if not last:
                    hots_turned(M, n + 1, 1 - j)
                for half in range(2):
                    act.wait_ge(M.y_ps[half], n + 1)
                    copy(y[:, j, 0, :, half * (P // 2):(half + 1) * (P // 2)].rearrange("s k p -> s p k"),
                         psum[:, 6 + half, :].rearrange("s (p k) -> s p k", k=K)).then_inc(M.y_high, 1)
                    ps = slice(half * (P // 2), (half + 1) * (P // 2))
                    act.wait_ge(M.y_rest, n * 2 + (half + 3))
                    copy(y[:, j, 1, :, ps], y_rest[:, :, ps]).then_inc(M.y_mid, 1)

            def experts_pass(M, r):
                gathered(M, r * PAIRS, 0)
                hots_turned(M, r * PAIRS, 0)
                if isinstance(r, int):
                    act.wait_ge(M.t_ps, 1)
                    copy(sh_hidT, psum[:, 4, :].rearrange("p (c t) -> p c t", c=2)).then_inc(M.t_sb, 1)
                pair_step(M, r * PAIRS, 0)
                with act.Fori(0, PAIRS // 2 - 1) as h:
                    for i in (1, 2):
                        pair_step(M, r * PAIRS + h * 2 + i, i % 2)
                pair_step(M, r * PAIRS + PAIRS - 1, 1, last=True)

            def experts(m):
                experts_pass(moe[m], 0)
                act.wait_ge(moe[m].table, 1)
                more = act.value_load(extra[0:1, 0:1].bitcast(I32), min_val=0, max_val=3)
                with act.If(more > 0):
                    with act.Fori(0, more) as r:
                        experts_pass(moe[m], r + 1)

            act.wait_ge(st_out, 64)
            experts_front(0)
            experts(0)

            squares(2)
            norm_root(2)
            norm(2, mod[:, 1, 0])
            for n in (0, 1):
                act.wait_ge(proj, 10 + n + 1)
                copy(qT[:, 4 * n:4 * n + 4].rearrange("p k t -> p (k t)"), bank(2 * (n % 2), 2), scale=HD ** -0.5)\
                    .then_inc(unit_free[n % 2], 1)
            for n in range(2):
                act.wait_ge(tr_ps, n + 1)
                copy(ckT[:, 4 * n:4 * n + 4], psum[:, 4 + n, :].rearrange("p (k t) -> p k t", t=P)).then_inc(tr_sb, 1)
            for n in range(2):
                act.wait_ge(tr_ps, n + 3)
                copy(kout[:, 4 * n:4 * n + 4], psum[:, 4 + n, :].rearrange("p (k t) -> p k t", t=P)).then_inc(tr_sb, 1)
            act.wait_ge(tr_sb, 4)
            act.dma_start(io["out_cache_k"][0, 0].rearrange("s h d -> s (h d)"), kout.rearrange("p k t -> p (k t)"))\
               .then_inc(cache_out, 16)

            def exps(g):
                j = g % 2
                act.wait_ge(sc_pr, g + 1)
                for n in range(4):
                    ins = act.activation(S_pr[:, j, n], psum[:, 6 + n // 2, (n % 2) * P:(n % 2 + 1) * P], ACT.Exp,
                                         bias=neg_max[:, j, 4 + n:5 + n], accum_out=row_sum[:, j, 4 + n:5 + n])
                ins.then_inc(pr_exp, 1)
                act.wait_ge(sc_sb, g + 1)
                for n in range(4):
                    ins = act.activation(S_lat[:, j, n], S_lat[:, j, n], ACT.Exp, bias=neg_max[:, j, n:n + 1],
                                         accum_out=row_sum[:, j, n:n + 1])
                ins.then_inc(p_exp, 1)

            def heads_out(g):
                act.wait_ge(oa_ps, g + 1)
                copy(oTa[:, 2 * g:2 * g + 2].rearrange("p k t -> p (k t)"), psum[:, 3, :]).then_inc(oa_sb, 1)

            for n in (4, 5):
                exps(n - 4)
                act.wait_ge(proj, 10 + n + 1)
                copy(va[:, :, (n - 4) * BLOCK:(n - 3) * BLOCK], psum[:, 2 * (n % 2):2 * (n % 2) + 2, :])\
                    .then_inc(unit_free[n % 2], 1)
            act.wait_ge(unit_free[0], 8)
            act.wait_ge(unit_free[1], 8)
            act.dma_start(io["out_cache_v"][0, 0].rearrange("s h d -> s (h d)"), va[:, 0]).then_inc(cache_out, 16)
            heads_out(0)
            exps(2)
            heads_out(1)
            exps(3)
            heads_out(2)
            heads_out(3)

            act.wait_ge(cache_out, 32)
            experts_front(1)
            experts(1)

            squares(4)
            norm_root(4)
            norm(4, None)
            for n in (0, 2):
                act.wait_ge(yt_ps, n + 1)
                copy(y_tok[:, n // 2, :, 0:4].rearrange("s p k -> s k p"),
                     psum[:, n, :].rearrange("s (k p) -> s k p", p=P)).then_inc(yt_sb, 1)
            act.wait_ge(yt_sb, 4)
            for a, name in enumerate(("out_prompt", "out_sample")):
                act.dma_start(io[name][0], y_tok[:, a].rearrange("s p k -> s (p k)")).then_inc(y_out, 16)

        @block.vector
        def _(dve):
            n_c = [0]

            def mark(ins):
                n_c[0] += 1
                ins.then_inc(dve_c, 1)

            def done():
                dve.wait_ge(dve_c, n_c[0])

            def link(ins):
                mark(ins)
                done()

            def normed(n):
                dve.wait_ge(root, n + 1)
                link(dve.reciprocal(rstd, rstd))
                for ks, count in ((slice(0, 2), 2), (slice(2, 4), 2), (slice(4, 8), 4)):
                    dve.tensor_tensor(hT[:, ks], xT[:, ks], rstd.unsqueeze(1).broadcast_to((P, count, NT)), ALU.mult)\
                       .then_inc(x_normed, 1)

            def norm(n, shift):
                dve.wait_ge(x_normed, 3 * n + 3)
                for k in range(4, K):
                    for s in range(2):
                        part = hT[:, k, s * T:(s + 1) * T]
                        if shift is None:
                            ins = dve.tensor_scalar(part, part, norm_w[:, 4, k:k + 1], None, ALU.mult)
                        else:
                            ins = dve.tensor_scalar(part, part, gain[:, n, k, s:s + 1], shift[:, k, s:s + 1],
                                                    ALU.mult, ALU.add)
                    ins.then_inc(h_done[1], 1)

            def modulation(n):
                l, j = parts[n]
                dve.wait_ge(sel_ps, n + 1)
                dve.tensor_tensor(mod[:, l, j], psum[:, 7, 0:2 * K].rearrange("p (k s) -> p k s", s=2),
                                  ada_b[:, l, j].unsqueeze(2).broadcast_to((P, K, 2)), ALU.add).then_inc(mod_done, 1)
                if j in (1, 4):
                    m = 2 * l + j // 4
                    dve.wait_ge(mod_done, n + 1)
                    link(dve.scalar_tensor_tensor(out=gain[:, m], in0=mod[:, l, j], scalar=1.0,
                                                  in1=norm_w[:, m].unsqueeze(2).broadcast_to((P, K, 2)),
                                                  op0=ALU.add, op1=ALU.mult))

            def gains_ready(m):
                dve.wait_ge(dve_c, n_c[0])
                dve.sem_inc(gains, 1)

            def residual(g, src):
                for k in range(K):
                    src(k)
                    for s in range(2):
                        at = slice(s * T, (s + 1) * T)
                        ins = dve.scalar_tensor_tensor(
                            out=xT[:, k, at], in0=psum[:, k // 2, (k % 2) * NT + s * T:(k % 2) * NT + (s + 1) * T],
                            scalar=g[:, k, s:s + 1], in1=xT[:, k, at], op0=ALU.mult, op1=ALU.add)
                    if k % 2:
                        ins.then_inc(resid, 1)

            dve.wait_ge(s_const, 16)
            link(dve.tensor_copy(ident_b, ident))
            for n in (1, 3):
                dve.wait_ge(x_ps, n + 1)
                dve.tensor_copy(xT[:, 2 * (n - 1):2 * (n - 1) + 4, T:NT],
                                psum[:, n, :].rearrange("p (k t) -> p k t", t=T)).then_inc(x_sb, 1)
            dve.wait_ge(s_small, SMALL)
            dve.wait_ge(lb_ps, 1)
            link(dve.tensor_copy(lb, psum[:, 5, 0:3 * HEADS].rearrange("p (i h) -> p i h", i=3)))
            link(dve.tensor_tensor(lb_t, lb[:, 0], lb[:, 1], ALU.max))
            link(dve.tensor_tensor(lb_t, lb_t, lb[:, 2], ALU.max))
            dve.tensor_tensor(lb, lb, lb_t.unsqueeze(1).broadcast_to((P, 3, HEADS)), ALU.subtract).then_inc(lb_shift, 1)
            dve.wait_ge(lb_exp, 1)
            link(dve.tensor_tensor(lb_t, lb[:, 0], lb[:, 1], ALU.add))
            link(dve.tensor_tensor(lb_t, lb_t, lb[:, 2], ALU.add))
            link(dve.reciprocal(lb_t, lb_t))
            link(dve.tensor_tensor(lb0, lb[:, 0], lb_t, ALU.mult))
            link(dve.tensor_scalar(one_minus_lb, lb0, -1.0, 1.0, ALU.mult, ALU.add))
            normed(0)
            modulation(0)
            modulation(1)
            gains_ready(0)
            norm(0, mod[:, 0, 0])

            dve.wait_ge(s_table, 16)

            def project(b):
                g, kind = b // 5, KINDS[b % 5]
                if kind == "gate":
                    dve.wait_ge(gate_sig, g + 1)
                    part = gate[:, GROUP * g:GROUP * (g + 1)].rearrange("p h t -> p (h t)")
                    dve.tensor_tensor(part, part, bank(2 * (b % 2), 2), ALU.mult).then_inc(unit_free[b % 2], 1)
                elif kind == "v":
                    dve.wait_ge(proj, b + 1)
                    dve.tensor_copy(v[:, :, g * BLOCK:(g + 1) * BLOCK], psum[:, 2 * (b % 2):2 * (b % 2) + 2, :])\
                       .then_inc(unit_free[b % 2], 1)

            def decay(g):
                for d in range(2):
                    dve.wait_ge(unit_free[(5 * g + d) % 2], (5 * g + d) // 2 + 1)
                    for h in range(GROUP * g, GROUP * (g + 1)):
                        mark(dve.tensor_scalar(bb[d][:, h], kk[d][:, h], one_minus_lb[:, h:h + 1], lb0[:, h:h + 1],
                                               ALU.mult, ALU.add))
                    done()
                    part = slice(GROUP * g, GROUP * (g + 1))
                    dve.tensor_scalar(kk[d][:, part], bb[d][:, part], -1.0, 1.0, ALU.mult, ALU.add)\
                       .then_inc(f_done, 1)
                for d in range(2):
                    dve.wait_ge(ln_done, 2 * g + d + 1)
                    out = bb[d][:, GROUP * g:GROUP * (g + 1)].rearrange("p h t -> p (h t)")
                    logs = dif[d].rearrange("p u t -> p (u t)")
                    if d:
                        out, logs = out[:, ::-1], logs[:, ::-1]
                    mark(dve.tensor_tensor_scan(out, scan_keep, logs, 0.0, ALU.mult, ALU.add))
                done()

            def decays(g, n):
                for d in range(2):
                    c = 8 * g + 2 * n + d
                    if n:
                        dve.wait_ge(exp_done, c - 1)
                    B = heads(bb[d], g)
                    if n < 3:
                        size = (128, 64, 32)[n]
                        at = size // 2 - (d == 0)
                        view = B.rearrange("p u (b t) -> p (u b) t", t=size)
                        shape = (P, UNITS * (T // size), size)
                        ins = dve.tensor_tensor(dif[d].rearrange("p u (b t) -> p (u b) t", t=size), view,
                                                view[:, :, at:at + 1].broadcast_to(shape), ALU.subtract)
                    else:
                        view = bb[d][:, GROUP * g:GROUP * (g + 1), 0:T]
                        at = T - 1 if d == 0 else 0
                        ins = dve.tensor_tensor(dif[d][:, 0:GROUP], view,
                                                view[:, :, at:at + 1].broadcast_to((P, GROUP, T)), ALU.subtract)
                    ins.then_inc(dif_done, 1)
                if n == 0:
                    dve.wait_ge(unit_free[(5 * g + 2) % 2], (5 * g + 2) // 2 + 1)
                for d in range(2):
                    dve.wait_ge(exp_done, 8 * g + 2 * n + d + 1)
                    if n < 2:
                        H = 64 >> n
                        vq, vk, vqq, vkk = (a.rearrange("p u (b t) -> p (u b) t", t=2 * H)
                                            for a in (Q[d], Kd[d], heads(q, g), heads(kk[d], g)))
                        early, behind = slice(0, H), slice(H, 2 * H)
                        qs, ks = (behind, early) if d == 0 else (early, behind)
                        dve.tensor_tensor(vq[:, :, qs], vq[:, :, qs], vqq[:, :, qs], ALU.mult)
                        ins = dve.tensor_tensor(vk[:, :, ks], vk[:, :, ks], vkk[:, :, ks], ALU.mult)
                    elif n == 2:
                        dve.tensor_tensor(Q[d], Q[d], heads(q, g), ALU.mult)
                        ins = dve.tensor_tensor(Kd[d], Kd[d], heads(kk[d], g), ALU.mult)
                    else:
                        part = slice(GROUP * g, GROUP * (g + 1))
                        dve.tensor_tensor(Q[d][:, 0:GROUP], Q[d][:, 0:GROUP], q[:, part, T:NT], ALU.mult)
                        ins = dve.tensor_tensor(Kd[d][:, 0:GROUP], Kd[d][:, 0:GROUP], kk[d][:, part, 0:T], ALU.mult)
                    ins.then_inc(qk_done, 1)

            def recur(g, item):
                if item == DECAY:
                    decay(g)
                elif item <= 3:
                    decays(g, item)
                if item == 3:
                    dve.wait_ge(qk_used, 8 * g + 6)
                    mark(dve.tensor_tensor(AT, psum[:, 4:6, :].rearrange("p b (u t) -> p (b u) t", t=T),
                                           mask_f.unsqueeze(1).broadcast_to((P, UNITS, T)), ALU.mult))
                    mark(dve.tensor_tensor(fb_sb, psum[:, 6, 0:UNITS * 32].rearrange("p (u t) -> p u t", t=32),
                                           mask_b.unsqueeze(1).broadcast_to((P, UNITS, 32)), ALU.mult))
                    done()
                    for i in range(4):
                        at = slice(32 * i, 32 * i + 32)
                        ins = dve.tensor_tensor(AT[at, :, at], AT[at, :, at], fb_sb[at], ALU.add)
                    ins.then_inc(at_done, 1)
                elif item == 4:
                    dve.wait_ge(pv_done, g + 1)
                    dve.tensor_copy(heads(oT, g), psum[:, 4:6, :].rearrange("p b (u t) -> p (b u) t", t=T))\
                       .then_inc(o_copied, 1)
                elif item == 5:
                    dve.wait_ge(o_rstd, g + 1)
                    part = oT[:, GROUP * g:GROUP * (g + 1)].rearrange("p h t -> p (h t)")
                    link(dve.scalar_tensor_tensor(out=part, in0=part, scalar=gn_w[:, 0:1],
                                                  in1=dif[0].rearrange("p u t -> p (u t)"), op0=ALU.mult, op1=ALU.mult))
                    dve.tensor_tensor(part, part, gate[:, GROUP * g:GROUP * (g + 1)].rearrange("p h t -> p (h t)"),
                                      ALU.mult).then_inc(o_done, 1)

            for b, middle, end, part, _ in ada_rounds():
                for g, item in middle:
                    recur(g, item)
                if part is not None:
                    modulation(part)
                for g, item in end:
                    recur(g, item)
                if b is not None:
                    project(b)
            gains_ready(1)

            def mixer_bank(m):
                def wait(k):
                    if k % 2 == 0:
                        dve.wait_ge(out_ps, 4 * m + k // 2 + 1)
                return wait

            residual(mod[:, 0, 2], mixer_bank(0))

            def top(values, pads, keep, out):
                for a in range(2):
                    best = best8[:, a]
                    link(dve.max(best, values[:, a, 0:values.shape[2] - pads]))
                    link(dve.memset(best[:, keep:8], 2 * LOW))
                    mark(dve.match_replace(out[:, a], best, values[:, a], 3 * LOW))
                done()

            scores, selv, t2, t3, mask = (route[:, n] for n in range(5))
            small16 = route[:, 5].rearrange("p a e -> p (a e)")
            m1, cnt, m2, c2 = (small16[:, 16 * n:16 * (n + 1)] for n in range(4))
            best8 = small16[:, 64:80].rearrange("p (a e) -> p a e", a=2)
            gs = route[:, 6].rearrange("p a e -> p (a e)")[:, 0:24].rearrange("p (a e) -> p a e", a=2)
            gs_o = route[:, 6].rearrange("p a e -> p (a e)")[:, 32:56].rearrange("p (a e) -> p a e", a=2)
            gmask = small16[:, 80:96].rearrange("p (a g) -> p a g", a=2)
            wsum = small16[:, 96:98]
            t1 = small16[:, 98:99]
            wide = route[:, 7:11].rearrange("p n a e -> p (n a e)")
            cand = wide[:, 0:2 * (E + 2)].rearrange("p (a e) -> p a e", a=2)
            cand_o = wide[:, 2 * (E + 2):4 * (E + 2)].rearrange("p (a e) -> p a e", a=2)

            def one_hots(M, r, expert, j):
                base = C_IOTA + r * SLOTS
                shape = (P, 2, 2, SLOTS)
                slots = (consts[:, base:base + SLOTS] if isinstance(base, int) else consts[:, bass.ds(base, SLOTS)])
                ranks = rank[:, :, bass.ds(expert, 2)] if not isinstance(expert, int) else rank[:, :, expert:expert + 2]
                dve.tensor_tensor(onehot[:, j].rearrange("p a (e s) -> p a e s", e=2),
                                  slots.unsqueeze(1).unsqueeze(1).broadcast_to(shape),
                                  ranks.unsqueeze(3).broadcast_to(shape), ALU.is_equal).then_inc(M.onehot, 1)

            def experts_front(m):
                M = moe[m]
                dve.sem_inc(M.y_rest, 2)
                normed(2 * m + 1)
                norm(2 * m + 1, mod[:, m, 3])
                link(dve.memset(gs, 2 * LOW))
                link(dve.memset(cand, 2 * LOW))
                dve.wait_ge(M.scores, 1)
                link(dve.tensor_tensor(selv, scores, router_b[:, m].unsqueeze(1).broadcast_to((P, 2, E)), ALU.add))

                def groups(a):
                    return a.rearrange("p a (g e) -> p (a g) e", g=GROUPS)

                link(dve.tensor_reduce(m1, groups(selv), AX.X, ALU.max))
                link(dve.tensor_tensor(groups(t2), groups(selv), m1.unsqueeze(2).broadcast_to((P, 16, 8)), ALU.is_equal))
                mark(dve.tensor_reduce(cnt, groups(t2), AX.X, ALU.add))
                link(dve.scalar_tensor_tensor(out=t3, in0=t2, scalar=LOW, in1=selv, op0=ALU.mult, op1=ALU.add))
                mark(dve.tensor_reduce(m2, groups(t3), AX.X, ALU.max))
                link(dve.tensor_scalar(c2, cnt, 1.5, LOW, ALU.is_lt, ALU.mult))
                link(dve.tensor_tensor(c2, c2, m1, ALU.add))
                link(dve.tensor_tensor(m2, m2, c2, ALU.max))
                link(dve.tensor_tensor(gs[:, :, 0:GROUPS], m1.rearrange("p (a g) -> p a g", a=2),
                                       m2.rearrange("p (a g) -> p a g", a=2), ALU.add))
                top(gs, 4, TOP_GROUPS, gs_o)
                link(dve.tensor_tensor(gmask, gs_o[:, :, 0:GROUPS], gs[:, :, 0:GROUPS], ALU.not_equal))
                link(dve.tensor_scalar(gmask, gmask, -1.0, -LOW, ALU.add, ALU.mult))
                for a in range(2):
                    mark(dve.tensor_tensor(cand[:, a, 0:E].rearrange("p (g e) -> p g e", g=GROUPS),
                                           selv[:, a].rearrange("p (g e) -> p g e", g=GROUPS),
                                           gmask[:, a].unsqueeze(2).broadcast_to((P, GROUPS, E // GROUPS)), ALU.add))
                done()
                top(cand, 2, TOP_K, cand_o)
                dve.tensor_tensor(mask, cand_o[:, :, 0:E], cand[:, :, 0:E], ALU.not_equal).then_inc(M.mask, 1)
                dve.wait_ge(M.mask, 1)
                link(dve.tensor_tensor(t2, scores, mask, ALU.mult))
                link(dve.tensor_reduce(wsum, t2, AX.X, ALU.add))
                link(dve.reciprocal(wsum, wsum))
                for a in range(2):
                    mark(dve.tensor_scalar(t2[:, a], t2[:, a], wsum[:, a:a + 1], ROUTED_SCALE, ALU.mult, ALU.mult))
                done()
                dve.wait_ge(M.rank_ps, 1)
                link(dve.scalar_tensor_tensor(out=t3, in0=psum[:, 5, 0:2 * E].rearrange("p (a e) -> p a e", a=2),
                                              scalar=1.0, in1=mask, op0=ALU.add, op1=ALU.mult))
                mark(dve.tensor_scalar(rank, t3, -1.0, None, ALU.add))
                link(dve.tensor_reduce(t1, psum[:, 5, 2 * E:3 * E], AX.X, ALU.max))
                link(dve.tensor_scalar(wsum[:, 0:1], t1, float(SLOTS), None, ALU.is_gt))
                link(dve.scalar_tensor_tensor(out=wsum[:, 1:2], in0=t1, scalar=2.0 * SLOTS, in1=wsum[:, 0:1],
                                              op0=ALU.is_gt, op1=ALU.add))
                dve.scalar_tensor_tensor(out=extra.bitcast(I32), in0=t1, scalar=3.0 * SLOTS, in1=wsum[:, 1:2],
                                         op0=ALU.is_gt, op1=ALU.add).then_inc(M.table, 1)
                for i in range(3):
                    link(dve.tensor_copy(comb[:, :, :, i], t2))
                    if i < 2:
                        link(dve.tensor_tensor(t2, t2, comb[:, :, :, i], ALU.subtract))
                for a in range(2):
                    if a:
                        one_hots(M, 0, 0, 0)
                    dve.wait_ge(M.sh_silu, a + 1)
                    dve.tensor_tensor(sh_hid[:, a], sh_silu[:, a], psum[:, 6 + a, F:2 * F], ALU.mult)\
                       .then_inc(M.hid if a else M.sh_hid, 1)

            def gathered(M, n, j):
                dve.wait_ge(M.xg_ps[1], n + 1)
                dve.tensor_copy(xg[:, j, 4:8], psum[:, 7, :].rearrange("p (k t) -> p k t", t=P)).then_inc(M.xg[1], 1)

            def pair_step(M, r, n, j, next_expert):
                if next_expert is not None:
                    one_hots(M, r, next_expert, 1 - j)
                dve.wait_ge(M.silu, n + 1)
                dve.wait_ge(M.hot_t, n + 1)
                dve.scalar_tensor_tensor(out=hid[:, j], in0=silu[:, j], scalar=slot_w[:, j:j + 1],
                                         in1=psum[:, 4, F:2 * F], op0=ALU.mult, op1=ALU.mult).then_inc(M.hid, 1)
                if next_expert is not None:
                    gathered(M, n + 1, 1 - j)
                for half in range(2):
                    dve.wait_ge(M.y_high, n * 2 + (half + 1))
                    ps = slice(half * (P // 2), (half + 1) * (P // 2))
                    dve.tensor_tensor(y_rest[:, :, ps].rearrange("s k p -> s p k"),
                                      psum[:, 6 + half, :].rearrange("s (p k) -> s p k", k=K),
                                      y[:, j, 0, :, ps].rearrange("s k p -> s p k"), ALU.subtract).then_inc(M.y_rest, 1)
                    dve.wait_ge(M.y_rest, n * 2 + (half + 3))
                    dve.wait_ge(M.y_mid, n * 2 + (half + 1))
                    ins = dve.tensor_tensor(y[:, j, 2, :, ps], y_rest[:, :, ps], y[:, j, 1, :, ps], ALU.subtract)
                ins.then_inc(M.y_low, 1)

            def experts_pass(M, r):
                if not isinstance(r, int):
                    one_hots(M, r, 0, 0)
                gathered(M, r * PAIRS, 0)
                pair_step(M, r, r * PAIRS, 0, 2)
                with dve.Fori(0, PAIRS // 2 - 1) as h:
                    for i in (1, 2):
                        pair_step(M, r, r * PAIRS + h * 2 + i, i % 2, h * 4 + 2 * (i + 1))
                pair_step(M, r, r * PAIRS + PAIRS - 1, 1, None)

            def experts(m):
                M = moe[m]
                dve.wait_ge(M.table, 1)
                experts_pass(M, 0)
                more = dve.value_load(extra[0:1, 0:1].bitcast(I32), min_val=0, max_val=3)
                with dve.If(more > 0):
                    with dve.Fori(0, more) as r:
                        experts_pass(M, r + 1)

                def added(k):
                    if k % 2 == 0:
                        dve.wait_ge(M.done, k // 2 + 1)

                residual(mod[:, m, 5], added)

            dve.wait_ge(st_out, 64)
            experts_front(0)
            experts(0)

            normed(2)
            norm(2, mod[:, 1, 0])
            for n in range(4):
                dve.wait_ge(bias_ps, n + 1)
                dve.tensor_tensor(bias[:, 4 * n:4 * n + 4], psum[:, 6 + n % 2, :].rearrange("p (h s) -> p h s", s=P),
                                  window.unsqueeze(1).broadcast_to((P, 4, P)), ALU.mult).then_inc(bias_done, 1)
            dve.wait_ge(bias_done, 4)
            link(dve.tensor_tensor(bias, bias, window_neg.unsqueeze(1).broadcast_to((P, A_HEADS, P)), ALU.add))
            for n in (2, 3):
                dve.wait_ge(proj, 10 + n + 1)
                dve.tensor_copy(kT[:, 4 * (n - 2):4 * (n - 2) + 4].rearrange("p k t -> p (k t)"), bank(2 * (n % 2), 2))\
                   .then_inc(unit_free[n % 2], 1)
            def probs_turned(g):
                dve.wait_ge(pt_ps, g + 1)
                for n in range(3):
                    dve.tensor_copy(PT[:, 4 * n:4 * n + 4].rearrange("p n t -> p (n t)"), bank(n)).then_inc(pt_sb, 1)

            def scores_read(g):
                j = g % 2
                dve.wait_ge(sc_ps, g + 1)
                for par in range(2):
                    ins = dve.tensor_reduce(neg_max[:, j, 4 + 2 * par:6 + 2 * par],
                                            psum[:, 6 + par, 0:2 * P].rearrange("p (i n) -> p i n", i=2), AX.X, ALU.max,
                                            negate=True)
                ins.then_inc(sc_pr, 1)
                for par in range(2):
                    lat = psum[:, 4 + par, :].rearrange("p (i n) -> p i n", i=2)
                    mark(dve.tensor_tensor(S_lat[:, j, 2 * par:2 * par + 2, 0:P], lat[:, :, 0:P],
                                           bias[:, 4 * g + par:4 * g + 4:2, :], ALU.add))
                    mark(dve.tensor_copy(S_lat[:, j, 2 * par:2 * par + 2, P:2 * P], lat[:, :, P:2 * P]))
                done()
                dve.tensor_reduce(neg_max[:, j, 0:4], S_lat[:, j], AX.X, ALU.max, negate=True).then_inc(sc_sb, 1)

            def probs(g):
                j = g % 2
                dve.wait_ge(p_exp, g + 1)
                link(dve.reciprocal(row_sum[:, j], row_sum[:, j]))
                dve.tensor_tensor(S_lat[:, j], S_lat[:, j],
                                  row_sum[:, j, 0:4].unsqueeze(2).broadcast_to((P, 4, 2 * P)), ALU.mult)
                dve.tensor_tensor(S_pr[:, j], S_pr[:, j],
                                  row_sum[:, j, 4:8].unsqueeze(2).broadcast_to((P, 4, P)), ALU.mult)\
                   .then_inc(p_norm, 1)

            for g in range(2):
                scores_read(g)
                probs(g)
            for g in range(4):
                probs_turned(g)
                if g in (1, 2):
                    probs(g + 1)
                if g < 2:
                    scores_read(g + 2)
            residual(mod[:, 1, 2], mixer_bank(1))

            dve.wait_ge(cache_out, 32)
            experts_front(1)
            experts(1)
            normed(4)
            norm(4, None)
            for n in (1, 3):
                dve.wait_ge(yt_ps, n + 1)
                dve.tensor_copy(y_tok[:, n // 2, :, 4:8].rearrange("s p k -> s k p"),
                                psum[:, n, :].rearrange("s (k p) -> s k p", p=P)).then_inc(yt_sb, 1)

        @block.tensor
        def _(pe):
            def mm(out, lhsT, rhs, start, stop, **kw):
                return pe.matmul(out, lhsT, rhs, start=start, stop=stop, skip_group_check=True, **kw)

            pe.wait_ge(s_const, 16)
            pe.wait_ge(s_x, 32)
            for n in range(4):
                for i in range(4):
                    k = 4 * (n // 2) + i
                    ins = pe.transpose(psum[:, n, i * T:(i + 1) * T], x_tok[:, n % 2, k::K], ident)
                ins.then_inc(x_ps, 1)
            pe.wait_ge(s_small, SMALL)
            for i in range(3):
                ins = pe.transpose(psum[:, 5, i * HEADS:(i + 1) * HEADS], lbrow[0:HEADS, i], ident[0:HEADS, 0:HEADS])
            ins.then_inc(lb_ps, 1)
            pe.wait_ge(ready, 5)

            def norm_sums(n):
                for i in range(4):
                    norm_sum(n, i)

            def norm_sum(n, i):
                pe.wait_ge(sq_done, 4 * n + i + 1)
                for k in (2 * i, 2 * i + 1):
                    ins = mm(psum[:, 4, 0:NT], ones, sq[:, k], k == 0, k == K - 1)
                if i == 3:
                    ins.then_inc(ssum, 1)

            norm_sums(0)
            pe.wait_ge(cond_done, 1)
            at_stage = [0]

            def staged():
                n = at_stage[0]
                at_stage[0] += 1
                pe.wait_ge(stage_in[rooms[n]], 16 * room_count[n])
                return stage[rooms[n]]

            def ada(n):
                w = staged()
                if n % 2:
                    pe.wait_ge(ada_row, n)
                elif n:
                    pe.wait_ge(mod_done, n // 2)
                for i in range(K // 4):
                    for c in range(4):
                        ins = mm(psum[32 * c:32 * c + 32, 7, :], cond_act[:, 4 * i + c, :], w[:, 4 * i + c, :],
                                 i == 0, i == K // 4 - 1)
                ins.then_inc(ada_ps, 1)

            def ada_columns(n):
                pe.wait_ge(ada_row, 2 * n + 2)
                for k in range(K):
                    ins = mm(psum[:, 7, 2 * k:2 * k + 2], mrow[:, k::K], sel, True, True)
                ins.then_inc(sel_ps, 1)

            for n in range(2):
                ada(2 * n)
                ada(2 * n + 1)
                ada_columns(n)
            pe.wait_ge(s_table, 16)

            BY_ARRIVAL = (0, 1, 4, 5, 2, 6, 3, 7)

            def h_chunk(n, k):
                pe.wait_ge(h_done[k // 4], 4 * n + k % 4 + 1)

            def project(b, by_rows, midway=lambda: None, norm=None):
                w = staged()
                u = 2 * (b % 2)
                if b >= 2:
                    pe.wait_ge(unit_free[b % 2], b // 2)
                if by_rows:
                    for a in range(2):
                        if a:
                            midway()
                        for k in range(K):
                            ins = mm(psum[:, u + a, :], hT[:, k, a * T:(a + 1) * T], w[:, k], k == 0, k == K - 1)
                else:
                    for n in range(4):
                        if n == 2:
                            midway()
                        for k in BY_ARRIVAL:
                            if norm is not None and n == 0:
                                h_chunk(norm, k)
                            ins = mm(psum[:, u + n // 2, (n % 2) * NT:(n % 2 + 1) * NT], w[:, k, n * P:(n + 1) * P],
                                     hT[:, k], k == BY_ARRIVAL[0], k == BY_ARRIVAL[-1])
                ins.then_inc(proj, 1)

            def scores(g, n):
                if n == 0 and g:
                    pe.wait_ge(o_rstd, g)
                if n == 2 and g:
                    pe.wait_ge(st_sb, 2 * g)
                for d in range(2):
                    pe.wait_ge(qk_done, 8 * g + 2 * n + d + 1)
                    for u in range(UNITS):
                        size = (128, 64, 32)[n]
                        for i in range(T // size):
                            early = slice(size * i, size * i + size // 2)
                            behind = slice(size * i + size // 2, size * (i + 1))
                            ss, ts = (early, behind) if d == 0 else (behind, early)
                            if n == 2:
                                ss = ts = slice(size * i, size * (i + 1))
                            if n == 2 and d:
                                out = psum[ss, 6, 32 * u:32 * u + 32]
                            else:
                                c = (u % 4) * T
                                out = psum[ss, 4 + u // 4, c + ts.start:c + ts.stop]
                            ins = mm(out, Kd[d][:, u, ss], Q[d][:, u, ts], True, True)
                    ins.then_inc(qk_used, 1)

            def values(g):
                pe.wait_ge(at_done, g + 1)
                pe.wait_ge(qk_done, 8 * g + 8)
                pe.wait_ge(unit_free[(5 * g + 3) % 2], (5 * g + 3) // 2 + 1)
                pe.wait_ge(s_s0, 32)
                for u in range(UNITS):
                    h, s = GROUP * g + u // 2, u % 2
                    out = psum[:, 4 + u // 4, (u % 4) * T:(u % 4 + 1) * T]
                    ins = mm(out, v[:, s, h * DV:(h + 1) * DV], AT[:, u], True, s == 0)
                    if s:
                        for d in range(2):
                            ins = mm(out, s0[:, d, h], Q[d][:, u // 2], False, d == 1)
                ins.then_inc(pv_done, 1)

            def turn_keys(g, d):
                if d:
                    pe.wait_ge(st_sb, 2 * g + 1)
                for i in range(GROUP):
                    ins = pe.transpose(psum[:, 6, i * T:(i + 1) * T], Kd[d][:, i], ident)
                ins.then_inc(kd_ps, 1)
                if d:
                    pe.wait_ge(kd_ps, 2 * g + 2)
                    pe.sem_inc(qk_used, 2)

            def state(g, d):
                pe.wait_ge(kd_sb, 2 * g + d + 1)
                for i in range(GROUP):
                    h = GROUP * g + i
                    ins = mm(psum[:, 6, i * DV:(i + 1) * DV], Kd[d][:, GROUP + i], v[:, 0, h * DV:(h + 1) * DV],
                             True, True)
                ins.then_inc(st_ps, 1)

            def recur(g, item):
                if item in (0, 1, 2):
                    scores(g, item)
                elif item == 3:
                    values(g)
                    turn_keys(g, 0)
                elif item == 4:
                    pe.wait_ge(o_sq, g + 1)
                    for i in range(2):
                        ins = mm(psum[:, 4 + i, :], ones, dif[0][:, 4 * i:4 * i + 4], True, True)
                    ins.then_inc(o_ssum, 1)
                    state(g, 0)
                elif item == 5:
                    turn_keys(g, 1)
                elif item == 6:
                    state(g, 1)

            for b, middle, end, part, adas in ada_rounds():
                def midway():
                    for g, item in middle:
                        recur(g, item)
                    if part is not None:
                        ada_columns(part)

                if b is not None:
                    project(b, KINDS[b % 5] == "v", midway, norm=0 if b == 0 else None)
                else:
                    midway()
                for n in adas[:1]:
                    ada(n)
                for g, item in end:
                    recur(g, item)
                for n in adas[1:]:
                    ada(n)

            def project_out(m, src, read):
                pe.wait_ge(late_in, 16 * (m + 1))
                for a, n in read:
                    pe.wait_ge(a, n)
                for part in range(2):
                    for k in range(K):
                        for h in range(part * K // 2, (part + 1) * K // 2):
                            ins = mm(psum[:, k // 2, (k % 2) * NT:(k % 2 + 1) * NT], late[:, h, k::K], src[:, h],
                                     h == 0 and k % 2 == 0, h == K - 1)
                        if part == 1 and k % 2:
                            ins.then_inc(out_ps, 1)
                            if k >= 5:
                                norm_sum(2 * m + 1, k // 2 - 2)
                    if part == 0:
                        ins.then_inc(late_half, 1)
                for i in range(2, 4):
                    norm_sum(2 * m + 1, i)

            project_out(0, oT, [(o_done, 2), (unit_free[0], 5), (unit_free[1], 5)])

            def experts_front(m):
                M = moe[m]
                for a in range(2):
                    for k in BY_ARRIVAL:
                        if a == 0:
                            h_chunk(2 * m + 1, k)
                        ins = mm(psum[:, 5, a * E:(a + 1) * E], hT[:, k, a * T:(a + 1) * T], router_w[:, m, k],
                                 k == BY_ARRIVAL[0], k == BY_ARRIVAL[-1])
                ins.then_inc(M.logits, 1)
                for n in range(4):
                    if n >= 2:
                        pe.wait_ge(M.htok, n - 1)
                    for i in range(4):
                        ins = pe.transpose(psum[:, 6 + n % 2, i * P:(i + 1) * P],
                                           hT[:, 4 * (n % 2) + i, (n // 2) * T:(n // 2 + 1) * T], ident)
                    ins.then_inc(M.htok_ps, 1)

                def shared(a):
                    pe.wait_ge(M.htok, 3 + a)
                    for k in range(K):
                        ins = mm(psum[:, 6 + a, :], hT[:, k, a * T:(a + 1) * T], ws_gu[:, k], k == 0, k == K - 1)
                    ins.then_inc(M.sh_ps, 1)

                pe.wait_ge(M.sh_in, 48)
                shared(0)
                pe.wait_ge(M.mask, 1)
                mask = route[:, 4]
                mm(psum[:, 5, 0:E], before, mask[:, 0], True, True)
                mm(psum[:, 5, E:2 * E], ones, mask[:, 0], True, False)
                mm(psum[:, 5, E:2 * E], before, mask[:, 1], False, True)
                mm(psum[:, 5, 2 * E:3 * E], ones, mask[:, 0], True, False)
                mm(psum[:, 5, 2 * E:3 * E], ones, mask[:, 1], False, True).then_inc(M.rank_ps, 1)
                shared(1)

            def turn_shared(M):
                for c in range(2):
                    for a in range(2):
                        ins = pe.transpose(psum[:, 4, c * NT + a * T:c * NT + (a + 1) * T],
                                           sh_hid[:, a, c * P:(c + 1) * P], ident)
                ins.then_inc(M.t_ps, 1)

            def shared_down(M):
                for k in range(K):
                    for c in range(2):
                        ins = mm(psum[:, k // 2, (k % 2) * NT:(k % 2 + 1) * NT], ws_dn[:, c, k::K], sh_hidT[:, c],
                                 k % 2 == 0 and c == 0, False)
                ins.then_inc(M.sh_used, 1)

            def gather(M, n, results, j, after_shared=False):
                pe.wait_ge(M.onehot, n + 1)
                for half in range(2):
                    if after_shared:
                        pe.wait_ge((M.sh_hid, M.hid)[half], 1)
                    pe.wait_ge(M.y_rest, results * 2 + (half + 1))
                    for i in range(4):
                        for a in range(2):
                            for part in range(3):
                                ins = mm(psum[:, 6 + half, i * P:(i + 1) * P], h_tok[:, part, a, 4 * half + i],
                                         onehot[:, j, a], a == 0 and part == 0, a == 1 and part == 2)
                    ins.then_inc(M.xg_ps[half], 1)

            def turn_hots(M, expert, j):
                for a in range(2):
                    mm(psum[:, 5, a * P:(a + 1) * P], onehot[:, j, a], ident_b, True, True)
                for a in range(2):
                    weights = comb[:, a, expert:expert + 2] if isinstance(expert, int) else comb[:, a, bass.ds(expert, 2)]
                    ins = mm(psum[:, 5, NT:NT + 6], onehot[:, j, a], weights.rearrange("p e i -> p (e i)"),
                             a == 0, a == 1)
                ins.then_inc(M.hot_ps, 1)

            def combine(M, j, last=False):
                for k in range(K):
                    for part in range(3):
                        ins = mm(psum[:, k // 2, (k % 2) * NT:(k % 2 + 1) * NT], y[:, j, part, k],
                                 onehot_t[:, j].rearrange("p a t -> p (a t)"), False, False)
                    if last and k % 2:
                        ins.then_inc(M.done, 1)

            def gate_up(M, n, j, load):
                pe.wait_ge(M.gu_in[j], load * 32)
                pe.wait_ge(M.xg[0], n + 1)
                pe.wait_ge(M.xg[1], n + 1)
                pe.wait_ge(M.hid, n + 1)
                for k in range(K):
                    for w in range(2):
                        for e in range(2):
                            at = slice(SLOTS * e, SLOTS * (e + 1))
                            ins = mm(psum[at, 4, w * F:(w + 1) * F], xg[:, j, k, at],
                                     ring[:, j, 2 * e + w, k * F:(k + 1) * F], k == 0 and w == 0, k == K - 1)
                ins.then_inc(M.gu, 1)

            def down(M, n, j, load, next_expert, first=False):
                if next_expert is not None:
                    gather(M, n + 1, n, 1 - j)
                pe.wait_ge(M.hid, n + 2)
                pe.wait_ge(M.hot_t, n + 1)
                for c in range(2):
                    ins = pe.transpose(psum[:, 5, c * P:(c + 1) * P], hid[:, j, c * P:(c + 1) * P], ident)
                ins.then_inc(M.t_ps, 1)
                if not first:
                    pe.wait_ge(M.y_low, n)
                    combine(M, 1 - j)
                pe.wait_ge(M.t_sb, n + 2)
                if next_expert is not None:
                    turn_hots(M, next_expert, 1 - j)
                pe.wait_ge(M.dn_in[j], load * 16)
                for half in range(2):
                    if next_expert is not None:
                        pe.wait_ge(M.xg[half], n + 2)
                    for c in range(2):
                        for e in range(2):
                            at = slice(SLOTS * e, SLOTS * (e + 1))
                            ins = mm(psum[at, 6 + half, :], hidT[:, j, c, at],
                                     ring[:, j, 4 + e, c * D + half * BLOCK:c * D + (half + 1) * BLOCK],
                                     c == 0, c == 1)
                    ins.then_inc(M.y_ps[half], 1)

            def experts_pass(M, r):
                n0, load0 = r * PAIRS, r * (PAIRS // 2) + 1
                gather(M, n0, n0, 0, after_shared=isinstance(r, int))
                if not isinstance(r, int):
                    pe.wait_ge(M.t_sb, n0 + 1)
                turn_hots(M, 0, 0)
                if isinstance(r, int):
                    turn_shared(M)
                    pe.wait_ge(M.t_sb, 1)
                gate_up(M, n0, 0, load0)
                if isinstance(r, int):
                    shared_down(M)
                down(M, n0, 0, load0, 2, first=isinstance(r, int))
                gate_up(M, n0 + 1, 1, load0)
                with pe.Fori(0, PAIRS // 2 - 1) as h:
                    for i in (1, 2):
                        n, load = n0 + h * 2 + i, load0 + h + i // 2
                        down(M, n, i % 2, load, h * 4 + 2 * (i + 1))
                        gate_up(M, n + 1, 1 - i % 2, load0 + h + 1)
                down(M, n0 + PAIRS - 1, 1, load0 + PAIRS // 2 - 1, None)

            def experts(m):
                M = moe[m]
                pe.wait_ge(M.h_low, 4)
                experts_pass(M, 0)
                pe.wait_ge(M.table, 1)
                more = pe.value_load(extra[0:1, 0:1].bitcast(I32), min_val=0, max_val=3)
                with pe.If(more > 0):
                    with pe.Fori(0, more) as r:
                        experts_pass(M, r + 1)
                pe.wait_ge(M.y_low, more * PAIRS + PAIRS)
                combine(M, 1, last=True)

            experts_front(0)
            experts(0)

            norm_sums(2)
            for b in range(10, 12):
                project(b, False, norm=2 if b == 10 else None)
            pe.wait_ge(cache_in, 32)
            for n in range(2):
                for i in range(4):
                    ins = pe.transpose(psum[:, 4 + n, i * P:(i + 1) * P], ck[:, (4 * n + i) * P:(4 * n + i + 1) * P], ident)
                ins.then_inc(tr_ps, 1)
            pe.wait_ge(bias_in, 64)
            for n in range(4):
                if n >= 2:
                    pe.wait_ge(bias_done, n - 1)
                mm(psum[:, 6 + n % 2, :], flip, bias[:, 4 * n:4 * n + 4].rearrange("p h s -> p (h s)"), True, True)\
                    .then_inc(bias_ps, 1)
            for b in range(12, 14):
                project(b, False)

            def new_keys():
                for n in range(2):
                    pe.wait_ge(tr_sb, n + 1)
                    pe.wait_ge(unit_free[n], 7)
                    for i in range(4):
                        ins = pe.transpose(psum[:, 4 + n, i * P:(i + 1) * P], kT[:, 4 * n + i, 0:T], ident)
                    ins.then_inc(tr_ps, 1)

            def attend(g):
                if g:
                    pe.wait_ge(sc_sb, g)
                    pe.wait_ge(pr_exp, g)
                else:
                    pe.wait_ge(tr_sb, 4)
                    pe.wait_ge(bias_done, 4)
                for i in range(2):
                    for par in range(2):
                        rows, c = slice(HD * par, HD * (par + 1)), 2 * g + i
                        at = psum[:, 4 + par, i * 2 * P:(i + 1) * 2 * P]
                        mm(at[:, 0:P], qT[rows, c, T:NT], kT[rows, c, T:NT], True, True)
                        mm(at[:, P:2 * P], qT[rows, c, T:NT], ckT[rows, c], True, True)
                for i in range(2):
                    for par in range(2):
                        rows, c = slice(HD * par, HD * (par + 1)), 2 * g + i
                        ins = mm(psum[:, 6 + par, i * P:(i + 1) * P], qT[rows, c, 0:T], kT[rows, c, 0:T], True, True)
                ins.then_inc(sc_ps, 1)

            project(14, True, new_keys)
            attend(0)
            project(15, True, lambda: attend(1))
            for u in range(2):
                pe.wait_ge(unit_free[u], 8)
            for g in range(4):
                if g == 2:
                    attend(3)
                pe.wait_ge(p_norm, g + 1)
                for n in range(4):
                    for i in range(2):
                        m = 2 * n + i
                        pe.transpose(psum[:, m // 4, (m % 4) * P:(m % 4 + 1) * P], S_lat[:, g % 2, n, i * P:(i + 1) * P], ident)
                for n in range(4):
                    ins = pe.transpose(psum[:, 2, n * P:(n + 1) * P], S_pr[:, g % 2, n], ident)
                ins.then_inc(pt_ps, 1)
                if g == 0:
                    attend(2)
                if g:
                    pe.wait_ge(oa_sb, g)
                for n in range(4):
                    par, i = n // 2, n % 2
                    cols = slice((4 * g + 2 * i + par) * HD, (4 * g + 2 * i + par + 1) * HD)
                    rows = slice(HD * par, HD * (par + 1))
                    pe.wait_ge(pt_sb, 3 * g + n // 2 + 1)
                    mm(psum[rows, 3, (2 * i + 1) * P:(2 * i + 2) * P], va[:, 1, cols], PT[:, 2 * n], True, False)
                    mm(psum[rows, 3, (2 * i + 1) * P:(2 * i + 2) * P], cv[:, cols], PT[:, 2 * n + 1], False, True)
                pe.wait_ge(pt_sb, 3 * g + 3)
                for n in range(4):
                    par, i = n // 2, n % 2
                    cols = slice((4 * g + 2 * i + par) * HD, (4 * g + 2 * i + par + 1) * HD)
                    rows = slice(HD * par, HD * (par + 1))
                    ins = mm(psum[rows, 3, 2 * i * P:(2 * i + 1) * P], va[:, 0, cols], PT[:, 8 + n], True, True)
                ins.then_inc(oa_ps, 1)
            project_out(1, oTa, [(oa_sb, 4)])
            experts_front(1)
            experts(1)
            norm_sums(4)
            for n in range(4):
                for i in range(4):
                    k = 4 * (n % 2) + i
                    h_chunk(4, k)
                    ins = pe.transpose(psum[:, n, i * P:(i + 1) * P], hT[:, k, (n // 2) * T:(n // 2 + 1) * T], ident)
                ins.then_inc(yt_ps, 1)


INPUTS = ["x_prompt", "x_sample", "state_hgrn_fwd", "state_hgrn_bwd", "cache_na_k", "cache_na_v", "c", "c_ctx",
          "norm1_w", "norm2_w", "ada_w", "ada_b", "hgrn_w_in", "hgrn_lb_logits", "hgrn_gn_w", "hgrn_w_out",
          "na_w_qkv", "na_rpb", "na_w_o", "moe_w_router", "moe_router_bias", "moe_w_gate", "moe_w_up", "moe_w_down",
          "shared_w_gate", "shared_w_up", "shared_w_down", "final_norm_w"]
OUTPUTS = [("out_prompt", (1, T, D)), ("out_sample", (1, T, D)),
           ("out_state_fwd", (1, 1, HEADS, DK, DV)), ("out_state_bwd", (1, 1, HEADS, DK, DV)),
           ("out_cache_k", (1, 1, T, A_HEADS, HD)), ("out_cache_v", (1, 1, T, A_HEADS, HD))]


def kernel(**inputs):
    import concourse.bacc as bacc
    from concourse.bass_utils import run_bass_kernel_spmd

    nc = bacc.Bacc("TRN2", target_bir_lowering=False, num_devices=1)
    arrays = {f"in_{n}": np.ascontiguousarray(inputs[n]) for n in INPUTS}
    arrays["in_table"] = shape_constants()
    io = {n[3:]: nc.dram_tensor(n, a.shape, mybir.dt.from_np(a.dtype), kind="ExternalInput").ap()
          for n, a in arrays.items()}
    for n, shape in OUTPUTS:
        io[n] = nc.dram_tensor(n, shape, F32, kind="ExternalOutput").ap()
    build(nc, io)
    r = run_bass_kernel_spmd(nc, [arrays], core_ids=[0])
    return tuple(r.results[0][n] for n, _ in OUTPUTS)
```
